# Optimizing a Trainium2 kernel written in Bass

```python
import jax, jax.numpy as jnp
from jax import lax
import numpy as np

D_MODEL = 1024
BATCH = 1
SEQ = 1024
DEPTH = 2

CHUNK = 64
N_Q_HEADS = 8
N_KV_HEADS = 2
GROUP = N_Q_HEADS // N_KV_HEADS
HEAD_DIM = 64
WINDOW = 128
WINDOW_CHUNKS = WINDOW // CHUNK
ROPE_THETA = 500000.0
ROT_DIM = HEAD_DIM // 4
N_HG_HEADS = 4
HG_KEY_DIM = 128
HG_VAL_DIM = 128
D_FF = 2816
CONV_WIDTH = 3
EPS = 1e-6
MASK_VALUE = -1e30
MAX_POS_OFFSET = 8192

ATT_Q = N_Q_HEADS * HEAD_DIM
ATT_KV = N_KV_HEADS * HEAD_DIM
HG_K = N_HG_HEADS * HG_KEY_DIM
HG_V = N_HG_HEADS * HG_VAL_DIM
SPLIT_1 = ATT_Q
SPLIT_2 = SPLIT_1 + ATT_KV
SPLIT_3 = SPLIT_2 + ATT_KV
SPLIT_4 = SPLIT_3 + HG_K
SPLIT_5 = SPLIT_4 + HG_K
SPLIT_6 = SPLIT_5 + HG_V
SPLIT_7 = SPLIT_6 + HG_V
D_IN = SPLIT_7 + 2 * D_MODEL

kernel_name = "hybrid_swa_sink_hgrn2_convglu"

def _rms_norm(x, g):
    xf = x.astype(jnp.float32)
    y = xf * lax.rsqrt(jnp.mean(xf * xf, axis=-1, keepdims=True) + EPS)
    return (y * g.astype(jnp.float32)).astype(x.dtype)

def _partial_rope(t, cos, sin):
    half = ROT_DIM // 2
    x1 = t[..., :half].astype(jnp.float32)
    x2 = t[..., half:ROT_DIM].astype(jnp.float32)
    rot = jnp.concatenate([x1 * cos - x2 * sin, x2 * cos + x1 * sin], axis=-1)
    return jnp.concatenate([rot.astype(t.dtype), t[..., ROT_DIM:]], axis=-1)

def _band_blocks(t):
    n = t.shape[1]
    pad = jnp.zeros(t.shape[:1] + (WINDOW_CHUNKS - 1,) + t.shape[2:], t.dtype)
    tp = jnp.concatenate([pad, t], axis=1)
    return jnp.concatenate([tp[:, j:j + n] for j in range(WINDOW_CHUNKS)], axis=2)

def _window_attention(q, k, v, sinks):
    b, s = q.shape[:2]
    n = s // CHUNK
    qc = q.reshape(b, n, CHUNK, N_KV_HEADS, GROUP, HEAD_DIM)
    kb = _band_blocks(k.reshape(b, n, CHUNK, N_KV_HEADS, HEAD_DIM))
    vb = _band_blocks(v.reshape(b, n, CHUNK, N_KV_HEADS, HEAD_DIM))
    scores = jnp.einsum('bncvgd,bnmvd->bnvgcm', qc.astype(jnp.float32),
                        kb.astype(jnp.float32)) * (HEAD_DIM ** -0.5)
    blk_valid = (jnp.arange(n)[:, None] + jnp.arange(WINDOW_CHUNKS)[None, :]) >= (WINDOW_CHUNKS - 1)
    valid = jnp.repeat(blk_valid, CHUNK, axis=1)
    scores = jnp.where(valid[None, :, None, None, None, :], scores, jnp.float32(MASK_VALUE))
    sink = jnp.broadcast_to(sinks.astype(jnp.float32).reshape(1, 1, N_KV_HEADS, GROUP, 1, 1),
                            scores.shape[:-1] + (1,))
    probs = jax.nn.softmax(jnp.concatenate([scores, sink], axis=-1), axis=-1)[..., :-1]
    out = jnp.einsum('bnvgcm,bnmvd->bncvgd', probs.astype(v.dtype), vb)
    return out.reshape(b, s, ATT_Q)

def _hgrn2(q, f_pre, i, lb):
    b, s, nh, dk = q.shape
    dv = i.shape[-1]
    n = s // CHUNK
    lb = lb.astype(jnp.float32)
    fp = f_pre.astype(jnp.float32)
    log_f = jnp.log(lb + (1.0 - lb) * jax.nn.sigmoid(fp))
    k = (1.0 - lb) * jax.nn.sigmoid(-fp)

    def to_chunks(t):
        return t.astype(jnp.float32).reshape(b, n, CHUNK, nh, t.shape[-1]).transpose(1, 0, 3, 2, 4)

    tri = jnp.tril(jnp.ones((CHUNK, CHUNK), dtype=bool))[:, :, None]

    def step(state, inp):
        qc, kc, vc, gc = inp
        cum = lax.cumsum(gc, axis=2)
        o_inter = jnp.einsum('bhtk,bhkv->bhtv', qc * jnp.exp(cum), state)
        diff = cum[:, :, :, None, :] - cum[:, :, None, :, :]
        decay = jnp.where(tri, jnp.exp(jnp.where(tri, diff, 0.0)), 0.0)
        scores = jnp.einsum('bhtk,bhsk,bhtsk->bhts', qc, kc, decay)
        o = o_inter + jnp.einsum('bhts,bhsv->bhtv', scores, vc)
        last = cum[:, :, -1:, :]
        state = jnp.exp(last[:, :, 0, :])[..., None] * state + jnp.einsum(
            'bhsk,bhsv->bhkv', kc * jnp.exp(last - cum), vc)
        return state, o

    s0 = jnp.zeros((b, nh, dk, dv), jnp.float32)
    _, o = lax.scan(step, s0, (to_chunks(q), to_chunks(k), to_chunks(i), to_chunks(log_f)))
    return o.transpose(1, 0, 3, 2, 4).reshape(b, s, nh, dv).astype(i.dtype)

def _causal_dwconv(u, w, bias):
    s = u.shape[1]
    up = jnp.pad(u, ((0, 0), (CONV_WIDTH - 1, 0), (0, 0)))
    out = up[:, 0:s] * w[0] + bias
    for j in range(1, CONV_WIDTH):
        out = out + up[:, j:j + s] * w[j]
    return out

def setup_inputs(seed: int = 0) -> dict:
    key = jax.random.key(seed)
    ks = jax.random.split(key, 20)
    f32 = jnp.float32
    nrm = lambda k, shape, scale: jax.random.normal(k, shape, f32) * scale
    x = jax.random.normal(ks[0], (BATCH, SEQ, D_MODEL), f32)
    offset = jax.random.randint(ks[1], (BATCH, 1), 0, MAX_POS_OFFSET, dtype=jnp.int32)
    positions = offset + jnp.arange(SEQ, dtype=jnp.int32)[None, :]
    return {
        "x": x,
        "positions": positions,
        "norm1_g": 1.0 + nrm(ks[2], (DEPTH, D_MODEL), 0.02),
        "w_in": nrm(ks[3], (DEPTH, D_MODEL, D_IN), D_MODEL ** -0.5),
        "q_norm_g": 1.0 + nrm(ks[4], (DEPTH, HEAD_DIM), 0.02),
        "k_norm_g": 1.0 + nrm(ks[5], (DEPTH, HEAD_DIM), 0.02),
        "sinks": nrm(ks[6], (DEPTH, N_Q_HEADS), 1.0),
        "lb_logits": nrm(ks[7], (DEPTH, HG_K), 0.5),
        "hg_norm_g": 1.0 + nrm(ks[8], (DEPTH, HG_VAL_DIM), 0.02),
        "w_branch_a": nrm(ks[9], (DEPTH, ATT_Q, D_MODEL), ATT_Q ** -0.5),
        "w_branch_b": nrm(ks[10], (DEPTH, HG_V, D_MODEL), HG_V ** -0.5),
        "w_out": nrm(ks[11], (DEPTH, D_MODEL, D_MODEL), D_MODEL ** -0.5),
        "norm2_g": 1.0 + nrm(ks[12], (DEPTH, D_MODEL), 0.02),
        "w_up": nrm(ks[13], (DEPTH, D_MODEL, 2 * D_FF), D_MODEL ** -0.5),
        "conv_w": nrm(ks[14], (DEPTH, CONV_WIDTH, D_FF), CONV_WIDTH ** -0.5),
        "conv_b": nrm(ks[15], (DEPTH, D_FF), 0.01),
        "w_down": nrm(ks[16], (DEPTH, D_FF, D_MODEL), D_FF ** -0.5),
    }

def reference(x, positions, norm1_g, w_in, q_norm_g, k_norm_g, sinks, lb_logits, hg_norm_g,
              w_branch_a, w_branch_b, w_out, norm2_g, w_up, conv_w, conv_b, w_down):
    f32 = jnp.float32
    b, s, _ = x.shape
    inv_freq = ROPE_THETA ** (-jnp.arange(0, ROT_DIM, 2, dtype=f32) / ROT_DIM)
    ang = positions.astype(f32)[..., None] * inv_freq
    cos = jnp.cos(ang)[:, :, None, :]
    sin = jnp.sin(ang)[:, :, None, :]
    lb_w = jax.nn.softmax(lb_logits.astype(f32), axis=0)
    lower_bounds = jnp.cumsum(lb_w, axis=0) - lb_w[0]

    for l in range(DEPTH):
        h = _rms_norm(x, norm1_g[l])
        proj = h @ w_in[l]
        aq, ak, av, hq, hf, hi, hgate, gates = jnp.split(
            proj, [SPLIT_1, SPLIT_2, SPLIT_3, SPLIT_4, SPLIT_5, SPLIT_6, SPLIT_7], axis=-1)
        aq = _partial_rope(_rms_norm(aq.reshape(b, s, N_Q_HEADS, HEAD_DIM), q_norm_g[l]), cos, sin)
        ak = _partial_rope(_rms_norm(ak.reshape(b, s, N_KV_HEADS, HEAD_DIM), k_norm_g[l]), cos, sin)
        av = av.reshape(b, s, N_KV_HEADS, HEAD_DIM)
        attn_out = _window_attention(aq, ak, av, sinks[l])
        hg = _hgrn2(jax.nn.silu(hq).reshape(b, s, N_HG_HEADS, HG_KEY_DIM),
                    hf.reshape(b, s, N_HG_HEADS, HG_KEY_DIM),
                    hi.reshape(b, s, N_HG_HEADS, HG_VAL_DIM),
                    lower_bounds[l].reshape(N_HG_HEADS, HG_KEY_DIM))
        hg = (_rms_norm(hg, hg_norm_g[l]) *
              jax.nn.silu(hgate.reshape(b, s, N_HG_HEADS, HG_VAL_DIM))).reshape(b, s, HG_V)
        g_a, g_b = jnp.split(gates, 2, axis=-1)
        merged = (jax.nn.sigmoid(g_a) * (attn_out @ w_branch_a[l]) +
                  jax.nn.sigmoid(g_b) * (hg @ w_branch_b[l]))
        x = x + merged @ w_out[l]
        h2 = _rms_norm(x, norm2_g[l])
        gate, val = jnp.split(h2 @ w_up[l], 2, axis=-1)
        gate = _causal_dwconv(gate, conv_w[l], conv_b[l])
        x = x + (jax.nn.silu(gate) * val) @ w_down[l]
    return x


_drawn_inputs = setup_inputs


def setup_inputs(seed=0):
    import zlib

    import numpy as np

    out = dict(_drawn_inputs(seed))
    spreads = {}
    factors = {'norm1_g': 3.647,
     'q_norm_g': 8.0,
     'k_norm_g': 8.0,
     'sinks': 8.0,
     'lb_logits': 3.405,
     'hg_norm_g': 6.074,
     'norm2_g': 2.807,
     'conv_b': 7.912}
    for name, (base, spread) in spreads.items():
        noise = np.random.default_rng([zlib.crc32(name.encode()), seed]).standard_normal(out[name].shape)
        drawn = base * np.exp(spread * noise) if base else spread * noise
        out[name] = __import__('jax').numpy.asarray(drawn.astype(out[name].dtype))
    for name, factor in factors.items():
        out[name] = (out[name] * factor).astype(out[name].dtype)
    return out
```

```python
import concourse.bass as bass
import concourse.mybir as mybir
import numpy as np

F32 = mybir.dt.float32
F32R = mybir.dt.float32r
I32 = mybir.dt.int32
U8 = mybir.dt.uint8
ALU = mybir.AluOpType
ACT = mybir.ActivationFunctionType
AX = mybir.AxisListType
ds = bass.ds

P = 128
SEQ, D, DEPTH = 1024, 1024, 2
CHUNK, HD, NQ, NKV = 64, 64, 8, 2
ROT = HD // 4
NH = 4
DFF = 2816
EPS = 1e-6
THETA = 500000.0
NEG = -1e30
HALF = SEQ // 2
NB = SEQ // P
KT = D // P
FT = DFF // P
PAIRS = NQ // 2
COL_K, COL_V = 512, 640
COL_HQ, COL_HF, COL_HI, COL_HG, COL_GA, COL_GB = 768, 1280, 1792, 2304, 2816, 3840

PG1, PG2, PHG, PLB, PQG, PKG, PCW, PCB = 0, 8, 16, 17, 21, 22, 23, 89
NROW = 111
POML, PSINK, NPAR = 111, 115, 123

C_ID, C_ONES, C_BLK, C_ROT, C_MASK, C_FREQ, C_LEV = 0, 128, 256, 384, 512, 896, 897
NCONST = C_LEV + 7 * P
LEVELS = (0, 32, 16, 8, 4, 2, 1)

W_QK, W_HEAD, W_MERGE, W_OUT, W_FFN, W_LAYER = 0, 6, 22, 46, 54, 120
O_HEAD, O_MERGE, O_OUT, O_FFN, O_LAYER = 6, 22, 54, 62, 194
B_PRO, B_NORM1, B_QK, B_HEAD, B_NORM2, B_LAYER = 18, 0, 2, 24, 128, 130
HG_USES = 12
HEAD_USES = 2 * HG_USES + 2
PRO_LOADS = 16 * (3 + DEPTH * 11 + 2)
HIDDEN_GROUPS = FT // 2
TINY = 2.0 ** -63


def constants():
    c = np.zeros((P, NCONST), np.float32)
    c[:, C_ID:C_ID + P] = np.eye(P)
    c[:, C_ONES:C_ONES + P] = 1.0
    for h in range(2):
        s = slice(h * HD, (h + 1) * HD)
        c[s, C_BLK + h * HD:C_BLK + (h + 1) * HD] = 1.0
        for i in range(ROT // 2):
            c[h * HD + ROT // 2 + i, C_ROT + h * HD + i] = -1.0
            c[h * HD + i, C_ROT + h * HD + ROT // 2 + i] = 1.0
    for first in range(2):
        m = np.zeros((P, 192), np.float32)
        m[:CHUNK, 2 * CHUNK:] = NEG
        m[CHUNK:, :CHUNK] = NEG
        if first:
            m[:, :CHUNK] = NEG
        c[:, C_MASK + 192 * first:C_MASK + 192 * (first + 1)] = m
    s, t = np.arange(P)[:, None], np.arange(P)[None, :]
    for n, w in enumerate(LEVELS):
        if w == 0:
            m = s == t
        else:
            m = (s // (2 * w) == t // (2 * w)) & (s % (2 * w) < w) & (t % (2 * w) >= w)
        c[:, C_LEV + P * n:C_LEV + P * (n + 1)] = m
    freq = np.float32(THETA) ** (-np.arange(0, ROT, 2, dtype=np.float32) / np.float32(ROT))
    for h in range(2):
        c[h * HD:h * HD + ROT, C_FREQ] = np.concatenate([freq, freq])
    return c



class Steps:

    def __init__(self, eng, sem, rnd, size):
        self.eng, self.sem, self.base, self.size, self.n = eng, sem, rnd * size, size, 0

    def __call__(self, ins):
        self.n += 1
        ins.then_inc(self.sem, 1)
        self.eng.wait_ge(self.sem, self.base + self.n)

    def end(self):
        assert self.n == self.size, (self.sem, self.n, self.size)


def apart(eng, sem):
    eng.wait_ge(sem, 1)


def taken_before(l, o, par):
    return 1 + l * O_LAYER + o - par


def taken(l, o, par, half):
    return taken_before(l, o, par) + half + 1


def used(l, w, n):
    return 8 * (l * W_LAYER + w) + n


def use(l, b):
    return B_PRO + l * B_LAYER + b


def head_use(t):
    return B_HEAD + 2 + HEAD_USES * t


def token_major_use(t):
    return B_HEAD + HEAD_USES * t


def halves(t, c):
    return t.rearrange("p (b two c) -> p b two c", two=2, c=c)


def build(nc, A, out):
    R1 = 16512
    R2 = R1 + 32768
    R3 = R2 + 65536
    R4 = R3 + 65536

    def at(name, off, shape, dt=F32):
        return nc.alloc_sbuf_tensor_at(name, [P] + list(shape), dt, offset=off)

    XT = at("x_t", R1, [KT, SEQ])
    MG = at("merged", R1, [KT, SEQ])
    KF = at("k_feat", R1, [P + SEQ])
    VT = at("v_tok", R1 + 4608, [NB + 1, P])
    CUM = at("cum", R1 + 9216, [SEQ])
    QS = at("hg_q", R1 + 13312, [SEQ])
    KK = at("hg_k", R1 + 17408, [SEQ])
    IT = at("hg_i_tok", R1 + 21504, [NB, P])
    TMP = at("evac", R1 + 25600, [SEQ])
    STATE = at("state", R1 + 29696, [5, P])
    EL = at("exp_last", R1 + 32256, [SEQ // CHUNK])
    HH = at("h_hi", R2, [KT, SEQ], F32R)
    HL = at("h_lo", R2 + 32768, [KT, SEQ], F32R)
    XIN = at("x_in", R2, [NB, D])
    AH = at("a_hi", R3, [4, SEQ], F32R)
    AL = at("a_lo", R3 + 16384, [4, SEQ], F32R)
    GH = at("g_hi", R3 + 32768, [4, SEQ], F32R)
    GL = at("g_lo", R3 + 49152, [4, SEQ], F32R)
    QF = at("q_feat", R3, [4, SEQ])
    OF = at("o_feat", R3 + 32768, [4, SEQ])
    GATE = at("gate", R3 + 49152, [4, SEQ])
    QR = [at(f"qk_raw{i}", R3 + x, [SEQ]) for i, x in enumerate((32768, 45056))]
    SQ = [at(f"qk_sq{i}", R3 + x, [SEQ]) for i, x in enumerate((36864, 61440))]
    T2 = at("qk_rotated", R3 + 40960, [SEQ])
    ROPE = at("rope", R3 + 53248, [2, SEQ])
    NSQ = at("norm_sq", R3 + 32768, [4, HALF])
    NACC = at("norm_sum", R3 + 40960, [SEQ])
    NRS = at("norm_rs", R3 + 45056, [SEQ])
    NHF = at("norm_h", R3 + 49152, [2, HALF])
    ANG = [at(f"ang{i}", R3 + 4096 * i, [SEQ]) for i in range(5)]
    POSI = at("pos_i", R3 + 20480, [SEQ], I32)
    PROW = at("par_rows", R3 + 24576, [2, P])
    LEVF = at("level_f", R3 + 28672, [896])
    OUTB = at("out_rows", R3, [2, D])
    UH = at("u_hi", R3, [2, 2, SEQ], F32R)
    UL = at("u_lo", R3 + 16384, [2, 2, SEQ], F32R)
    CB = at("conv_in", R3 + 32768, [2, SEQ + 2])
    CO = at("conv_out", R3 + 41088, [2, SEQ])
    UF = at("u_f", R3 + 49280, [2, SEQ])
    r = R4

    def more(name, shape, size, dt=F32):
        nonlocal r
        r += size
        return at(name, r - size, shape, dt)

    RAW = more("w_raw", [2, SEQ], 8192)
    WH = more("w_hi", [2, SEQ], 8192, F32R)
    WL = more("w_lo", [2, SEQ], 8192, F32R)
    CONST = more("consts", [C_LEV], 3616)
    LEVM = more("level_masks", [7, P], 896, U8)
    PARA = more("par_all", [DEPTH, NPAR], 992)
    PAR = more("par", [NPAR], 512)
    SA = at("sig", r, [2, SEQ])
    E = more("decay", [3, HALF], 6144)
    ST = more("s_t", [4, P], 2048)
    QE = more("q_decayed", [HALF], 2048)
    KE = more("k_decayed", [HALF], 2048)
    QB = more("q_block", [P], 512)
    PR = more("probs", [2, 2 * P], 2048)
    PT = more("probs_t", [4, P], 2048)
    STAT = more("stats", [16], 64)
    SMALL = more("small", [32], 128)
    assert r <= 229344, r

    IDENT, ONES = CONST[:, C_ID:C_ID + P], CONST[:, C_ONES:C_ONES + P]
    FREQ = CONST[:, C_FREQ:C_FREQ + 1]
    BLK, ROTM = CONST[:, C_BLK:C_BLK + P], CONST[:, C_ROT:C_ROT + P]

    G = [nc.alloc_psum_tensor(f"gemm{i}", [P, 512], F32) for i in range(4)]
    SC = nc.alloc_psum_tensor("scores", [P, 512], F32)
    PX = nc.alloc_psum_tensor("probs_x", [P, 512], F32)
    SM = [nc.alloc_psum_tensor(f"small_ps{i}", [P, 512], F32) for i in range(2)]

    XS = nc.dram_tensor("x_spill", [P, KT, SEQ], F32, kind="Internal")
    RS = nc.dram_tensor("rope_spill", [P, 2, SEQ], F32, kind="Internal")

    sem = nc.alloc_semaphore
    s_pro = sem("prologue_loaded")
    s_raw = [sem(f"weights_loaded{i}") for i in range(2)]
    s_rawfree = sem("raw_slot_free")
    s_whi = sem("weights_hi")
    s_split = sem("weights_split")
    s_gemm = sem("gemm_progress")
    s_taken = [sem(f"gemm_taken{i}") for i in range(2)]
    s_sw = sem("small_written")
    s_sr = sem("small_read")
    s_par = sem("params_ready")
    s_rope = sem("rope_saved")
    s_rl = sem("rope_loaded")
    s_sp = sem("x_spilled")
    s_xb = sem("x_back")
    s_sq = sem("norm_squares")
    s_acc = sem("norm_sum")
    s_sd = sem("norm_sd")
    s_h = sem("norm_h")
    s_hhi = sem("norm_h_hi")
    s_hlo = sem("norm_h_lo")
    s_qkq = sem("qk_squares")
    s_qks = sem("qk_sd")
    s_qkn = sem("qk_normed")
    s_qkd = sem("qk_done")
    s_ang = sem("angles")
    s_sin = sem("sines")
    s_lbx = sem("lb_exp")
    s_qb = sem("q_block_ready")
    s_as = sem("att_scores")
    s_am = sem("att_shift")
    s_ae = sem("att_exp")
    s_ap = sem("att_probs")
    s_at = sem("att_probs_t")
    s_ac = sem("att_probs_t_copied")
    s_ao = sem("att_out")
    s_ad = sem("att_done")
    s_rows = sem("hg_upper_rows")
    s_clamp = sem("hg_f_clamped")
    s_ln = sem("hg_ln")
    s_cum = sem("hg_cum")
    s_el = sem("hg_exp_last")
    s_sub = sem("hg_exponent")
    s_exp = sem("hg_exp")
    s_fac = sem("hg_factor")
    s_qe = sem("hg_q_decayed")
    s_ket = sem("hg_k_tok")
    s_state = sem("hg_state")
    s_stu = sem("hg_state_used")
    s_osq = sem("hg_o_sq")
    s_osd = sem("hg_o_sd")
    s_hgd = sem("hg_done")
    s_mg = sem("merged_ready")
    s_mh = sem("merged_hi")
    s_ml = sem("merged_lo")
    s_co = sem("conv_ready")
    s_si = sem("silu_ready")
    s_uhi = sem("u_hi_ready")
    s_ulo = sem("u_lo_ready")
    s_x = sem("x_ready")
    s_out = [sem(f"stored{i}") for i in range(2)]
    d_init, d_norm, d_qk, d_att, d_split, d_hgn, d_prep, d_ffn = (
        sem(f"dve_{n}") for n in ("init", "norm", "qk", "att", "a_split", "hg_norm", "prep", "ffn"))
    d_sink, d_par, d_z = (sem(f"dve_{n}") for n in ("sink", "par", "zero"))

    block = nc.Block()
    block.__enter__()

    @block.sync
    def _(sp):
        sp.dma_start(CONST[:, :], A["consts"][:, 0:C_LEV]).then_inc(s_pro, 16)
        sp.dma_start(LEVF[:, :], A["consts"][:, C_LEV:C_LEV + 896]).then_inc(s_pro, 16)
        sp.dma_start(POSI[:, :], A["positions"].to_broadcast([P, SEQ])).then_inc(s_pro, 16)
        for l in range(DEPTH):
            for name, row, k in (("norm1_g", PG1, KT), ("norm2_g", PG2, KT), ("hg_norm_g", PHG, 1),
                                 ("lb_logits", PLB, NH), ("conv_b", PCB, FT)):
                sp.dma_start(PROW[row:row + k, l, :],
                             A[name][l].rearrange("(k c) -> k c", c=P)).then_inc(s_pro, 16)
            for name, row in (("q_norm_g", PQG), ("k_norm_g", PKG)):
                for h in range(2):
                    sp.dma_start(PROW[row:row + 1, l, h * HD:(h + 1) * HD],
                                 A[name][l:l + 1, :]).then_inc(s_pro, 16)
            sp.dma_start(PROW[PCW:PCW + 3 * FT, l, :],
                         A["conv_w"][l].rearrange("j (k c) -> (j k) c", c=P)).then_inc(s_pro, 16)
            sp.dma_start(PARA[:, l, PSINK:PSINK + NQ],
                         A["sinks"][l:l + 1, :].to_broadcast([P, NQ])).then_inc(s_pro, 16)
        x_rows = A["x"][0].rearrange("(b p) d -> p b d", p=P)
        for b in (slice(0, 4), slice(4, 8)):
            sp.dma_start(XIN[:, b, :], x_rows[:, b, :]).then_inc(s_pro, 16)

        def load(l, w, slot, parts, waited=False):
            assert len(parts) == 3
            if not waited:
                apart(sp, s_mg)
                sp.wait_ge(s_rawfree, l * W_LAYER + w + 1)
            for dst, src in parts:
                sp.dma_start(dst, src).then_inc(s_raw[slot], 16)

        def columns(l, w, slot, name, col):
            dst = RAW[:, slot, :].rearrange("p (k c) -> p k c", k=KT)
            src = A[name][l].rearrange("(k p) n -> p k n", p=P)
            load(l, w, slot, [(dst[:, a:b, :], src[:, a:b, ds(col, P)]) for a, b in ((0, 3), (3, 6), (6, 8))])

        with sp.Fori(0, DEPTH) as l:
            columns(l, 0, 0, "w_in", COL_V)
            columns(l, 1, 1, "w_in", COL_K)
            sp.wait_ge(s_x, (l + 1) * KT)
            for k in (slice(0, 4), slice(4, 8)):
                sp.dma_start(XS[:, k, :], XT[:, k, :]).then_inc(s_sp, 16)
            sp.wait_ge(s_rope, 16)
            sp.wait_ge(s_rawfree, l * W_LAYER + 3)
            sp.dma_start(ROPE[:, :, :], RS[:, :, :]).then_inc(s_rl, 16)
            for t in range(PAIRS):
                w = 2 + t
                dst = RAW[:, w % 2, :].rearrange("p (k c) -> p k c", k=KT)
                src = A["w_in"][l].rearrange("(k p) n -> p k n", p=P)
                c0, c1 = t * HD, (t + PAIRS) * HD
                load(l, w, w % 2, [(dst[:, :, 0:HD], src[:, :, c0:c0 + HD]),
                            (dst[:, 0:4, HD:P], src[:, 0:4, c1:c1 + HD]),
                            (dst[:, 4:8, HD:P], src[:, 4:8, c1:c1 + HD])], waited=(t == 0))
            with sp.Fori(0, NH) as t:
                for i, col in enumerate((COL_HG, COL_HI, COL_HQ, COL_HF)):
                    columns(l, W_HEAD + 4 * t + i, i % 2, "w_in", t * P + col)
            with sp.Fori(0, KT // 2) as jj:
                for h in range(2):
                    w = 6 * jj + (W_MERGE + 3 * h)
                    j = 2 * jj + h
                    columns(l, w, (3 * h) % 2, "w_in", j * P + COL_GA)
                    columns(l, w + 1, (3 * h + 1) % 2, "w_in", j * P + COL_GB)
                    dst = RAW[:, (3 * h + 2) % 2, :].rearrange("p (k c) -> p k c", k=KT)
                    wa = A["w_branch_a"][l].rearrange("(g t p) n -> g p t n", g=2, t=PAIRS)
                    wb = A["w_branch_b"][l].rearrange("(k p) n -> p k n", p=P)
                    load(l, w + 2, (3 * h + 2) % 2, [(dst[0:HD, 0:4, :], wa[0][:, :, ds(j * P, P)]),
                                    (dst[HD:P, 0:4, :], wa[1][:, :, ds(j * P, P)]),
                                    (dst[:, 4:8, :], wb[:, :, ds(j * P, P)])])
            sp.wait_ge(s_ml, (l + 1) * 2 * KT)
            for k in (slice(0, 4), slice(4, 8)):
                sp.dma_start(XT[:, k, :], XS[:, k, :]).then_inc(s_xb, 16)
            with sp.Fori(0, KT // 2) as jj:
                for h in range(2):
                    columns(l, 2 * jj + (W_OUT + h), h, "w_out", (2 * jj + h) * P)

            def up(g, w):
                for i in range(2):
                    columns(l, w + 2 * i, 0, "w_up", (2 * g + i) * P)
                    columns(l, w + 2 * i + 1, 1, "w_up", (2 * g + i) * P + DFF)

            def down(g, w):
                for h in range(2):
                    dst = RAW[:, h, :].rearrange("p (k n) -> p k n", k=2)
                    src = A["w_down"][l].rearrange("(k p) n -> p k n", p=P)
                    c = h * HALF
                    load(l, w + h, h, [(dst[:, 0:1, :], src[:, ds(2 * g, 1), c:c + HALF]),
                                    (dst[:, 1:2, 0:256], src[:, ds(2 * g + 1, 1), c:c + 256]),
                                    (dst[:, 1:2, 256:HALF], src[:, ds(2 * g + 1, 1), c + 256:c + HALF])])

            up(0, W_FFN)
            with sp.Fori(0, HIDDEN_GROUPS // 2) as p:
                w = 12 * p + (W_FFN + 4)
                up(2 * p + 1, w)
                down(2 * p, w + 4)
                up(2 * p + 2, w + 6)
                down(2 * p + 1, w + 10)
            down(HIDDEN_GROUPS - 1, W_LAYER - 2)
        out_rows = out[0].rearrange("(b p) d -> b p d", p=P)
        for b in range(NB):
            sp.wait_ge(s_sr, use(DEPTH, 2 * b + 1) + 1)
            sp.dma_start(out_rows[b], OUTB[:, b % 2, :]).then_inc(s_out[b % 2], 16)
        for i in range(2):
            sp.wait_ge(s_out[i], 16 * NB // 2)
        sp.wait_ge(s_sp, 32 * DEPTH)

    @block.gpsimd
    def _(pool):
        pool.memset(SMALL[:, 0:1], 0.0).then_inc(s_rawfree, 1)
        pool.memset(SMALL[:, 1:2], 0.0).then_inc(s_rawfree, 1)

        def split(w, slot):
            pool.wait_ge(s_raw[slot], 24 * (w - slot) + 48)
            pool.tensor_tensor(WH[:, slot, :], RAW[:, slot, :], ONES[:, 0:1].to_broadcast([P, SEQ]),
                               ALU.mult).then_inc(s_whi, 1)
            pool.wait_ge(s_whi, w + 1)
            pool.tensor_tensor(WL[:, slot, :], RAW[:, slot, :], WH[:, slot, :].bitcast(F32),
                               ALU.subtract).then_inc(s_split, 1)
            pool.wait_ge(s_split, w + 1)
            pool.tensor_tensor(SMALL[:, 2:3], SMALL[:, 0:1], SMALL[:, 1:2], ALU.add).then_inc(s_rawfree, 1)

        pool.wait_ge(s_pro, PRO_LOADS)
        split(0, 0)
        split(1, 1)
        with pool.Fori(1, DEPTH * W_LAYER // 2) as u:
            for s in range(2):
                pool.wait_ge(s_gemm, 16 * u + 8 * (s - 1))
                split(2 * u + s, s)

    @block.tensor
    def _(pe):
        pe.wait_ge(s_pro, PRO_LOADS)
        for b in range(B_PRO):
            if b >= 2:
                pe.wait_ge(s_sr, b - 1)
            bank = SM[b % 2]
            if b < 2:
                mm = pe.transpose(bank[:, 0:NROW], PROW[0:NROW, b, :], IDENT[0:NROW, 0:NROW])
            else:
                j, half = (b - 2) % KT, (b - 2) // KT
                for i in range(4):
                    mm = pe.transpose(bank[:, i * P:(i + 1) * P],
                                      XIN[:, 4 * half + i, j * P:(j + 1) * P], IDENT)
            mm.then_inc(s_sw, 1)

        def small(l, b, par):
            pe.wait_ge(s_sr, use(l, b) - 1)
            return SM[par]

        def passes(slot, xh, xl, half, weights, dst, marks, part=None):
            steps = [(a, x, k) for k in range(len(weights))
                     for a, x in ((WH, xh), (WH, xl), (WL, xh))]
            total = len(steps)
            lo, hi = (0, total) if part is None else (part * total // 2, (part + 1) * total // 2)
            for n in range(lo, hi):
                a, x, k = steps[n]
                mm = pe.matmul(dst, a[:, slot, weights[k]], x(k, half), start=(n == 0),
                               stop=(n == total - 1))
                if (n + 1) * marks % total == 0:
                    mm.then_inc(s_gemm, 1)

        def moving(t):
            return lambda k, half: t[:, k, half * HALF:(half + 1) * HALF]

        whole = [slice(k * P, (k + 1) * P) for k in range(KT)]

        def tile(l, w, slot, o, par, half, part=None):
            if part in (None, 0) and half == 0:
                pe.wait_ge(s_split, l * W_LAYER + w + 1)
                pe.wait_ge(s_taken[par], taken_before(l, o, par))
            passes(slot, moving(HH), moving(HL), half, whole, G[2 * par + half][:, :], 4, part)

        def norm_sum(l, n, b):
            for half in range(2):
                pe.wait_ge(s_acc, (2 * l + n) * 14 + 7 * (half + 1))
                bank = small(l, b + half, half)
                pe.matmul(bank[:, :], ONES, NACC[:, half * HALF:(half + 1) * HALF],
                          start=True, stop=True).then_inc(s_sw, 1)

        def qk_sum(l, i):
            for half in range(2):
                bank = small(l, B_QK + 2 + 4 * i + half, half)
                pe.wait_ge(s_qkq, l * 10 + 2 * i + half + 1)
                pe.matmul(bank[:, :], BLK, SQ[i % 2][:, half * HALF:(half + 1) * HALF],
                          start=True, stop=True).then_inc(s_sw, 1)

        def qk_rotate(l, i):
            pe.wait_ge(s_qkn, l * 5 + i + 1)
            for half in range(2):
                bank = small(l, B_QK + 4 + 4 * i + half, half)
                pe.matmul(bank[:, :], ROTM, QR[i % 2][:, half * HALF:(half + 1) * HALF],
                          start=True, stop=True).then_inc(s_sw, 1)

        def to_token_major(l, b, src):
            for half in range(2):
                bank = small(l, b + half, half)
                for i in range(4):
                    c = (4 * half + i) * P
                    mm = pe.transpose(bank[:, i * P:(i + 1) * P], src[:, c:c + P], IDENT)
                mm.then_inc(s_sw, 1)

        def att_scores(l, t, m):
            pe.wait_ge(s_qb, (4 * l + t) * 8 + m + 1)
            for h in range(2):
                rows = slice(h * HD, (h + 1) * HD)
                if h == 1:
                    pe.wait_ge(s_as, 2 * ((4 * l + t) * 8 + m) + 1)
                pe.matmul(SC[:, h * 192:(h + 1) * 192], QB[rows, :],
                          KF[rows, m * P + CHUNK:(m + 2) * P], start=True, stop=True).then_inc(s_as, 1)

        def att_transpose(l, t, m):
            pe.wait_ge(s_ap, (4 * l + t) * 8 + m + 1)
            for n in range(4):
                mm = pe.transpose(PX[:, n * P:(n + 1) * P], PR[:, n // 2, (n % 2) * P:(n % 2 + 1) * P],
                                  IDENT)
            mm.then_inc(s_at, 1)

        def att_values(l, t, m):
            pe.wait_ge(s_ac, (4 * l + t) * 8 + m + 1)
            for h in range(2):
                rows = slice(h * HD, (h + 1) * HD)
                for kb in range(2):
                    mm = pe.matmul(PX[rows, 0:P], VT[:, m + kb, rows], PT[:, 2 * h + kb, :],
                                   start=(kb == 0), stop=(kb == 1))
            mm.then_inc(s_ao, 1)

        def hg_step(l, t, step):
            half, s = step // 8, step % 8
            b = head_use(t) + HG_USES * half
            rnd = 4 * l + t
            tok = half * HALF

            def product(n, lhs, rhs):
                bank = small(l, b + n, n % 2)
                for i in range(4):
                    c = slice(i * P, (i + 1) * P)
                    mm = pe.matmul(bank[:, c], lhs[:, c], rhs[:, c], start=True, stop=True)
                mm.then_inc(s_sw, 1)

            if s == 0:
                pe.wait_ge(s_cum, rnd + 1)
                product(0, KK[:, tok:tok + HALF], QS[:, tok:tok + HALF])
            if s < 6:
                pe.wait_ge(s_fac, rnd * 12 + 6 * half + s + 1)
                product(s + 1, E[:, s % 3, :], E[:, s % 3, :])
            if s == 5:
                pe.wait_ge(s_ket, rnd * 2 + half + 1)
                bank = small(l, b + 7, 1)
                for i in range(4):
                    mm = pe.transpose(bank[:, i * P:(i + 1) * P], KE[:, i * P:(i + 1) * P], IDENT)
                mm.then_inc(s_sw, 1)
            if s == 6:
                pe.wait_ge(s_sr, use(l, token_major_use(t) + 1) + 1)
                pe.wait_ge(s_sr, use(l, b + 7) + 1)
                for q in range(2):
                    bank = small(l, b + 8 + q, q)
                    for n, i in enumerate((0, 2, 1, 3)):
                        c = 4 * q + i
                        if n == 2:
                            pe.wait_ge(s_rows, rnd * 4 + 2 * half + q + 1)
                        rows = slice((c % 2) * CHUNK, (c % 2 + 1) * CHUNK)
                        mm = pe.matmul(bank[:, i * P:(i + 1) * P], KE[rows, (c // 2) * P:(c // 2 + 1) * P],
                                       IT[rows, 4 * half + c // 2, :], start=True, stop=True)
                        if n == 1:
                            mm.then_inc(s_rows, 1)
                    mm.then_inc(s_sw, 1)
            if s == 7:
                pe.wait_ge(s_sr, use(l, b + 6) + 1)
                pe.wait_ge(s_qe, rnd * 2 + half + 1)
                bank = small(l, b + 10, 0)
                for c in range(8):
                    cols = slice(c * CHUNK, (c + 1) * CHUNK)
                    pe.matmul(bank[:, cols], IT[:, 4 * half + c // 2, :],
                              ST[:, c // 2, (c % 2) * CHUNK:(c % 2 + 1) * CHUNK], start=True, stop=False)
                    n = 8 * half + c
                    pe.wait_ge(s_state, rnd * 16 + n + 1)
                    mm = pe.matmul(bank[:, cols], STATE[:, n % 5, :], QE[:, cols], start=False, stop=True)
                    if c < 7:
                        mm.then_inc(s_stu, 1)
                mm.then_inc(s_sw, 1)

        def hg_norm_sum(l, t, half):
            pe.wait_ge(s_osq, (4 * l + t) * 2 + half + 1)
            bank = small(l, head_use(t) + HG_USES * half + 11, 1)
            pe.matmul(bank[:, :], ONES, QE[:, :], start=True, stop=True).then_inc(s_sw, 1)

        def head_round(l, t, fresh, behind):
            for u in range(16):
                i, half, part = u // 4, u // 2 % 2, u % 2
                if fresh:
                    tile(l, 4 * t + (W_HEAD + i), i % 2, 4 * t + (O_HEAD + i), i % 2, half, part)
                    if u % 2 == 0:
                        att_scores(l, t, u // 2)
                    else:
                        att_transpose(l, t, u // 2)
                if behind:
                    if u == 8:
                        hg_norm_sum(l, t - 1, 0)
                    hg_step(l, t - 1, u)
                if fresh and u % 2 == 1:
                    att_values(l, t, u // 2)
            if behind:
                hg_norm_sum(l, t - 1, 1)
            if fresh:
                o = 4 * t + (O_HEAD + 1)
                pe.wait_ge(s_taken[1], taken(l, o, 1, 1))
                to_token_major(l, token_major_use(t), TMP)

        with pe.Fori(0, DEPTH) as l:
            norm_sum(l, 0, B_NORM1)
            for w in range(6):
                for half in range(2):
                    if w == 0:
                        pe.wait_ge(s_hlo, (2 * l) * 16 + 8 * (half + 1))
                    tile(l, w, w % 2, w, w % 2, half)
                    if w == 1 and half == 0:
                        pe.wait_ge(s_taken[0], taken(l, 0, 0, 1))
                        to_token_major(l, B_QK, TMP)
                    if w >= 2:
                        (qk_sum if half == 0 else qk_rotate)(l, w - 2)
            qk_sum(l, 4)
            qk_rotate(l, 4)
            head_round(l, 0, True, False)
            with pe.Fori(1, NH) as t:
                head_round(l, t, True, True)
            head_round(l, NH, False, True)
            with pe.Fori(0, KT // 2) as jj:
                for h in range(2):
                    if h == 0:
                        pe.wait_ge(s_ad, 32 * l + 32)
                        pe.wait_ge(s_hgd, 4 * l + 4)
                    w, o = 6 * jj + (W_MERGE + 3 * h), 8 * jj + (O_MERGE + 4 * h)
                    for i in range(2):
                        for half in range(2):
                            tile(l, w + i, (3 * h + i) % 2, o + i, i, half)
                    slot = (3 * h + 2) % 2
                    pe.wait_ge(s_split, l * W_LAYER + w + 3)
                    for i, (xh, xl) in enumerate(((AH, AL), (GH, GL))):
                        pe.wait_ge(s_taken[i], taken_before(l, o + 2 + i, i))
                        for half in range(2):
                            passes(slot, moving(xh), moving(xl), half, whole[4 * i:4 * i + 4],
                                   G[2 * i + half][:, :], 2)
            with pe.Fori(0, KT // 2) as jj:
                for h in range(2):
                    for half in range(2):
                        if half == 0 and h == 0:
                            pe.wait_ge(s_ml, l * 2 * KT + 8)
                        if half == 1 and h == 0:
                            pe.wait_ge(s_ml, l * 2 * KT + 16)
                        tile(l, 2 * jj + (W_OUT + h), h, 2 * jj + (O_OUT + h), h, half)
            norm_sum(l, 1, B_NORM2)

            def up(w, o, wait_h=False):
                for i in range(4):
                    for half in range(2):
                        if wait_h and i == 0:
                            pe.wait_ge(s_hlo, (2 * l + 1) * 16 + 8 * (half + 1))
                        tile(l, w + i, i % 2, o + i, i % 2, half)

            def down(g, w, o, buf):
                pe.wait_ge(s_ulo, (l * HIDDEN_GROUPS + g + 1) * 2)
                for j in range(KT):
                    slot, par = j // 4, j % 2
                    if j % 4 == 0:
                        pe.wait_ge(s_split, l * W_LAYER + w + slot + 1)
                    pe.wait_ge(s_taken[par], taken_before(l, o + j, par))
                    cols = [slice(k * HALF + (j % 4) * P, k * HALF + (j % 4 + 1) * P) for k in range(2)]
                    for half in range(2):
                        passes(slot, moving(UH[:, buf]), moving(UL[:, buf]), half, cols,
                               G[2 * par + half][:, :], 1)

            up(W_FFN, O_FFN, True)
            with pe.Fori(0, HIDDEN_GROUPS // 2) as p:
                w, o = 12 * p + (W_FFN + 4), 24 * p + (O_FFN + 4)
                up(w, o)
                down(2 * p, w + 4, o + 4, 0)
                up(w + 6, o + 12)
                down(2 * p + 1, w + 10, o + 16, 1)
            down(HIDDEN_GROUPS - 1, W_LAYER - 2, O_LAYER - 8, 0)
        for b in range(2 * NB):
            if b == 0:
                pe.wait_ge(s_x, (DEPTH + 1) * KT)
            bank = small(DEPTH, b, b % 2)
            for i in range(4):
                mm = pe.transpose(bank[:, i * P:(i + 1) * P],
                                  XT[:, 4 * (b % 2) + i, (b // 2) * P:(b // 2 + 1) * P], IDENT)
            mm.then_inc(s_sw, 1)

    @block.scalar
    def _(act):
        f = nc.scalar.activation
        act.wait_ge(s_ang, 2)
        for i in range(2):
            f(ROPE[:, i, :], ANG[3 + i][:, :], ACT.Sin).then_inc(s_sin, 1)
        act.wait_ge(s_sin, 2)
        act.dma_start(RS[:, :, :], ROPE[:, :, :]).then_inc(s_rope, 16)
        act.wait_ge(s_lbx, 1)
        f(SMALL[:, 8:16], SMALL[:, 8:16], ACT.Exp).then_inc(s_lbx, 1)

        def cols(half):
            return slice(half * HALF, (half + 1) * HALF)

        def evac(l, w, o, par, half, dst, func=ACT.Copy, n=None, **kw):
            act.wait_ge(s_gemm, used(l, w, 4 * (half + 1) if n is None else n))
            f(dst, G[2 * par + half][:, :], func, **kw).then_inc(s_taken[par], 1)

        def norm(l, n):
            r0 = 2 * l + n
            for half in range(2):
                for j in range(KT):
                    i = half * KT + j
                    if half == 0:
                        if n == 0:
                            act.wait_ge(s_x, l * KT + j + 1)
                        else:
                            act.wait_ge(s_taken[j % 2], taken(l, O_OUT + j, j % 2, 1))
                    if j >= 4 or half == 1:
                        k = i - 4
                        act.wait_ge(s_acc, r0 * 14 + 7 * (k // KT) + max(k % KT, 1))
                    f(NSQ[:, i % 4, :], XT[:, j, cols(half)], ACT.Square).then_inc(s_sq, 1)
            for half in range(2):
                act.wait_ge(s_sr, use(l, (B_NORM1, B_NORM2)[n] + half) + 1)
                f(NRS[:, cols(half)], NRS[:, cols(half)], ACT.Sqrt).then_inc(s_sd, 1)
            for i in range(2 * KT):
                act.wait_ge(s_h, r0 * 16 + i + 1)
                f(HH[:, i % KT, cols(i // KT)], NHF[:, i % 2, :], ACT.Copy).then_inc(s_hhi, 1)

        def q_block(l, t, m):
            f(QB[:, :], QF[:, ds(t * 1, 1), m * P:(m + 1) * P] if not isinstance(t, int)
              else QF[:, t:t + 1, m * P:(m + 1) * P], ACT.Copy).then_inc(s_qb, 1)

        def att_exp(l, t, m):
            act.wait_ge(s_am, (4 * l + t) * 8 + m + 1)
            for h in range(2):
                f(PR[:, h, CHUNK:], PR[:, h, CHUNK:], ACT.Exp, bias=STAT[:, 4 + h:5 + h],
                  scale=HD ** -0.5, accum_out=STAT[:, 8 + h:9 + h])
            f(STAT[:, 10:12], STAT[:, 6:8], ACT.Exp).then_inc(s_ae, 1)

        def hg_exp(l, t, half, n):
            rnd = (4 * l + t) * 2 + half
            sub = (0, 1, 2, 3, 4, 5, 5, 6)[n]
            act.wait_ge(s_sub, rnd * 7 + sub + 1)
            if n == 6:
                f(QE[:, :], CUM[:, cols(half)], ACT.Exp).then_inc(s_exp, 1)
            else:
                x = KE[:, :] if n == 5 else E[:, (n if n < 5 else 5) % 3, :]
                f(x, x, ACT.Exp).then_inc(s_exp, 1)

        def hg_step(l, t, step):
            half, s = step // 8, step % 8
            for n in {0: (2,), 1: (3,), 2: (4, 5, 6), 3: (7,)}.get(s, ()):
                hg_exp(l, t, half, n)
            if half == 0 and s in (6, 7):
                hg_exp(l, t, 1, s - 6)
            if s == 7:
                act.wait_ge(s_sr, use(l, head_use(t) + HG_USES * half + 10) + 1)
                f(QE[:, :], (OF[:, ds(t, 1), cols(half)]), ACT.Square).then_inc(s_osq, 1)

        def hg_norm(l, t, half):
            act.wait_ge(s_sr, use(l, head_use(t) + HG_USES * half + 11) + 1)
            f(KE[:, :], KE[:, :], ACT.Sqrt).then_inc(s_osd, 1)

        def head_round(l, t, fresh, behind):
            if fresh:
                q_block(l, t, 0)
            for u in range(16):
                if fresh and u in (5, 9):
                    i = u // 4 - 1
                    w, o = 4 * t + (W_HEAD + i), 4 * t + (O_HEAD + i)
                    for half in range(2):
                        if i == 0:
                            evac(l, w, o, 0, half, GATE[:, ds(t, 1), cols(half)], ACT.Silu)
                        else:
                            evac(l, w, o, 1, half, TMP[:, cols(half)])
                if behind:
                    if u == 8:
                        hg_norm(l, t - 1, 0)
                if fresh and u % 2 == 0:
                    att_exp(l, t, u // 2)
                    if u < 14:
                        q_block(l, t, u // 2 + 1)
                if behind:
                    hg_step(l, t - 1, u)
            if behind:
                hg_norm(l, t - 1, 1)
                act.wait_ge(s_hgd, 4 * l + t)
            if fresh:
                w, o = 4 * t + (W_HEAD + 2), 4 * t + (O_HEAD + 2)
                for half in range(2):
                    evac(l, w, o, 0, half, QS[:, cols(half)], ACT.Silu)
                for half in range(2):
                    act.wait_ge(s_gemm, used(l, w + 1, 4 * (half + 1)))
                    f(KK[:, cols(half)], G[2 + half][:, :], ACT.Sigmoid, scale=-1.0)
                    f(CUM[:, cols(half)], G[2 + half][:, :], ACT.Sigmoid).then_inc(s_taken[1], 1)
                for h in range(1):
                    act.wait_ge(s_clamp, 4 * l + t + 1)
                    f(CUM[:, :], CUM[:, :], ACT.Ln, bias=LBCUR[:, 0:1], scale=LBCUR[:, 1:2]).then_inc(s_ln, 1)
                act.wait_ge(s_cum, 4 * l + t + 1)
                f(EL[:, :], CUM[:, CHUNK - 1::CHUNK], ACT.Exp).then_inc(s_el, 1)
                for n in range(2):
                    hg_exp(l, t, 0, n)

        LBCUR = STAT[:, 14:16]

        with act.Fori(0, DEPTH) as l:
            norm(l, 0)
            act.wait_ge(s_sp, 32 * l + 32)
            for half in range(2):
                evac(l, 0, 0, 0, half, TMP[:, cols(half)])
            for i in range(5):
                w = i + 1
                if i >= 2:
                    act.wait_ge(s_qkd, 5 * l + i - 1)
                for half in range(2):
                    act.wait_ge(s_gemm, used(l, w, 4 * (half + 1)))
                    f(SQ[i % 2][:, cols(half)], G[2 * (w % 2) + half][:, :], ACT.Square).then_inc(s_qkq, 1)
                    f(QR[i % 2][:, cols(half)], G[2 * (w % 2) + half][:, :], ACT.Copy).then_inc(s_taken[w % 2], 1)
                for half in range(2):
                    act.wait_ge(s_sr, use(l, B_QK + 2 + 4 * i + half) + 1)
                    f(SQ[i % 2][:, cols(half)], SQ[i % 2][:, cols(half)], ACT.Sqrt).then_inc(s_qks, 1)
            act.wait_ge(s_qkd, 5 * l + 5)
            head_round(l, 0, True, False)
            with act.Fori(1, NH) as t:
                head_round(l, t, True, True)
            head_round(l, NH, False, True)
            with act.Fori(0, KT // 2) as jj:
                for h in range(2):
                    w, o = 6 * jj + (W_MERGE + 3 * h), 8 * jj + (O_MERGE + 4 * h)
                    act.wait_ge(s_mg, 8 * l + 2 * jj + (h + 1))
                    for i in range(2):
                        for half in range(2):
                            evac(l, w + i, o + i, i, half, SA[:, i, cols(half)], ACT.Sigmoid)
            act.wait_ge(s_mg, 8 * l + 9)
            for i in range(2 * KT):
                f(HH[:, i % KT, cols(i // KT)], MG[:, i % KT, cols(i // KT)], ACT.Copy).then_inc(s_mh, 1)
            norm(l, 1)

            def up(g, w, o, buf):
                n = (l * HIDDEN_GROUPS + g) * 2
                for i in range(2):
                    for half in range(2):
                        evac(l, w + 2 * i, o + 2 * i, 0, half, CB[:, i, 2 + half * HALF:2 + (half + 1) * HALF])
                    act.wait_ge(s_co, n + i + 1)
                    f(CO[:, i, :], CO[:, i, :], ACT.Silu).then_inc(s_si, 1)
                    act.wait_ge(s_taken[1], taken(l, o + 2 * i + 1, 1, 1))
                    f(UH[:, buf, i, :], UF[:, i, :], ACT.Copy).then_inc(s_uhi, 1)

            up(0, W_FFN, O_FFN, 0)
            with act.Fori(0, HIDDEN_GROUPS // 2) as p:
                w, o = 12 * p + (W_FFN + 4), 24 * p + (O_FFN + 4)
                up(2 * p + 1, w, o, 1)
                up(2 * p + 2, w + 6, o + 12, 0)

    @block.vector
    def _(dve):
        tt, ts_, stt, copy = dve.tensor_tensor, dve.tensor_scalar, dve.scalar_tensor_tensor, dve.tensor_copy

        def cols(half):
            return slice(half * HALF, (half + 1) * HALF)

        def over(ap, shape):
            return ap.to_broadcast(shape)

        for par in range(2):
            dve.memset(SMALL[:, 28 + par:29 + par], 0.0).then_inc(s_taken[par], 1)
        dve.memset(SMALL[:, 30:31], 0.0).then_inc(s_mg, 1)
        init = Steps(dve, d_init, 0, SIZES["init"])
        init(dve.memset(PR[:, :, :], 0.0))
        dve.wait_ge(s_pro, PRO_LOADS)
        init(copy(LEVM[:, :, :], LEVF[:, :].rearrange("p (n c) -> p n c", n=7)))
        for b in range(2):
            dve.wait_ge(s_sw, b + 1)
            copy(PARA[:, b, 0:NROW], SM[b][:, 0:NROW]).then_inc(s_sr, 1)
        assert DEPTH == 2
        lbs = [PARA[:, l, PLB:PLB + NH] for l in range(DEPTH)]
        dve.wait_ge(s_sr, 2)
        init(tt(SMALL[:, 4:8], lbs[0], lbs[1], ALU.max))
        for l in range(DEPTH):
            init(tt(SMALL[:, 8 + 4 * l:12 + 4 * l], lbs[l], SMALL[:, 4:8], ALU.subtract))
        init(tt(SMALL[:, 4:8], SMALL[:, 4:8], SMALL[:, 4:8], ALU.subtract))
        dve.memset(SMALL[:, 31:32], 0.0).then_inc(s_lbx, 1)
        two_pi, parts = 2 * np.pi, []
        for _ in range(4):
            m, e = np.frexp(two_pi)
            parts.append(float(np.ldexp(np.floor(m * 2048) / 2048, e)))
            two_pi -= parts[-1]
        magic = 1.5 * 2 ** 23
        pos, ang, turns = ANG[0], ANG[1], ANG[2]
        init(copy(pos[:, :], POSI[:, :]))
        init(ts_(ang[:, :], pos[:, :], FREQ, None, ALU.mult))
        for i, quarter in enumerate((0.25, 0.0)):
            red = ANG[3 + i]
            init(ts_(turns[:, :], ang[:, :], float(1 / (2 * np.pi)), quarter, ALU.mult, ALU.add))
            init(ts_(turns[:, :], turns[:, :], magic, None, ALU.add))
            init(ts_(turns[:, :], turns[:, :], -magic, None, ALU.add))
            src = ang
            for c in parts:
                init(stt(red[:, :], turns[:, :], -c, src[:, :], ALU.mult, ALU.add))
                src = red
            init(ts_(red[:, :], red[:, :], quarter * 2 * np.pi, 3.1415925, ALU.add, ALU.min))
            ts_(red[:, :], red[:, :], -3.1415925, None, ALU.max).then_inc(s_ang, 1)
        dve.wait_ge(s_lbx, 2)
        e0, e1 = SMALL[:, 8:12], SMALL[:, 12:16]
        init(tt(SMALL[:, 16:20], e0, e1, ALU.add))
        init(dve.reciprocal(SMALL[:, 20:24], SMALL[:, 16:20]))
        init(tt(e0, e0, SMALL[:, 20:24], ALU.mult))
        init(tt(e1, e1, SMALL[:, 20:24], ALU.mult))
        init(tt(lbs[0], e0, e0, ALU.subtract))
        init(tt(SMALL[:, 16:20], e0, e1, ALU.add))
        init(tt(lbs[1], SMALL[:, 16:20], e0, ALU.subtract))
        for l in range(DEPTH):
            init(ts_(PARA[:, l, POML:POML + NH], lbs[l], -1.0, 1.0, ALU.mult, ALU.add))
        for b in range(2, B_PRO):
            j, half = (b - 2) % KT, (b - 2) // KT
            dve.wait_ge(s_sw, b + 1)
            copy(XT[:, j, cols(half)], SM[b % 2][:, :]).then_inc(s_sr, 1)
            if half == 1:
                dve.wait_ge(s_sr, b + 1)
                dve.memset(SMALL[:, 31:32], 0.0).then_inc(s_x, 1)
        init.end()

        def written(l, b):
            dve.wait_ge(s_sw, use(l, b) + 1)

        def norm(l, n, b, gain):
            r0 = 2 * l + n
            for half in range(2):
                for j in range(1, KT):
                    i = half * KT + j
                    dve.wait_ge(s_sq, r0 * 16 + i + 1)
                    acc = NACC[:, cols(half)]
                    if j == 1:
                        tt(acc, NSQ[:, (i - 1) % 4, :], NSQ[:, i % 4, :], ALU.add).then_inc(s_acc, 1)
                    else:
                        dve.wait_ge(s_acc, r0 * 14 + 7 * half + j - 1)
                        tt(acc, acc, NSQ[:, i % 4, :], ALU.add).then_inc(s_acc, 1)
            for half in range(2):
                written(l, b + half)
                rs = NRS[:, cols(half)]
                ts_(rs, SM[half][:, :], 1.0 / D, EPS, ALU.mult, ALU.add).then_inc(s_sr, 1)
            st = Steps(dve, d_norm, r0, SIZES["norm"])
            for half in range(2):
                rs = NRS[:, cols(half)]
                dve.wait_ge(s_sd, r0 * 2 + half + 1)
                st(dve.reciprocal(rs, rs))
                for j in range(KT + 1):
                    i = half * KT + j
                    if j < KT:
                        if i >= 2:
                            dve.wait_ge(s_hlo, r0 * 16 + i - 1)
                        stt(NHF[:, i % 2, :], XT[:, j, cols(half)], PAR[:, gain + j:gain + j + 1], rs,
                            ALU.mult, ALU.mult).then_inc(s_h, 1)
                    if j > 0:
                        dve.wait_ge(s_hhi, r0 * 16 + i)
                        tt(HL[:, j - 1, cols(half)], NHF[:, (i - 1) % 2, :],
                           HH[:, j - 1, cols(half)].bitcast(F32), ALU.subtract).then_inc(s_hlo, 1)
            st.end()

        def qk(l, i):
            st = Steps(dve, d_qk, 5 * l + i, SIZES["qk"])
            gain = PAR[:, PKG:PKG + 1] if i == 0 else PAR[:, PQG:PQG + 1]
            raw, var = QR[i % 2], SQ[i % 2]
            b = B_QK + 2 + 4 * i
            for half in range(2):
                written(l, b + half)
                ts_(var[:, cols(half)], SM[half][:, :], 1.0 / HD, EPS, ALU.mult, ALU.add).then_inc(s_sr, 1)
            dve.wait_ge(s_qks, 10 * l + 2 * i + 2)
            st(dve.reciprocal(var[:, :], var[:, :]))
            dve.wait_ge(s_taken[(i + 1) % 2], taken(l, i + 1, (i + 1) % 2, 1))
            stt(raw[:, :], raw[:, :], gain, var[:, :], ALU.mult, ALU.mult).then_inc(s_qkn, 1)
            for half in range(2):
                written(l, b + 2 + half)
                tt(T2[:, cols(half)], SM[half][:, :], ROPE[:, 1, cols(half)], ALU.mult).then_inc(s_sr, 1)
            dve.wait_ge(s_sr, use(l, b + 4))
            st(tt(raw[:, :], raw[:, :], ROPE[:, 0, :], ALU.mult))
            dst = KF[:, P:] if i == 0 else QF[:, i - 1, :]
            tt(dst, raw[:, :], T2[:, :], ALU.add).then_inc(s_qkd, 1)

        def att_shift(l, t, m):
            a = (4 * l + t) * 8 + m
            st = Steps(dve, d_att, a, SIZES["att"])
            dve.wait_ge(s_as, 2 * a + 2)
            mask = CONST[:, C_MASK + 192 * (m == 0):C_MASK + 192 * (m == 0) + 192]
            scores = PR[:, :, CHUNK:]
            st(tt(scores, SC[:, 0:384].rearrange("p (h k) -> p h k", h=2),
                  mask.rearrange("p (o k) -> p o k", o=1).to_broadcast([P, 2, 192]), ALU.add))
            st(dve.tensor_reduce(STAT[:, 0:2], scores, AX.X, ALU.max))
            sink = SINKT[:, 0:2]
            st(stt(STAT[:, 2:4], STAT[:, 0:2], HD ** -0.5, sink, ALU.mult, ALU.max))
            st(tt(STAT[:, 6:8], sink, STAT[:, 2:4], ALU.subtract))
            ts_(STAT[:, 4:6], STAT[:, 2:4], -1.0, None, ALU.mult).then_inc(s_am, 1)
            return st

        def att_probs(l, t, m, st):
            a = (4 * l + t) * 8 + m
            dve.wait_ge(s_ae, a + 1)
            st(tt(STAT[:, 8:10], STAT[:, 8:10], STAT[:, 10:12], ALU.add))
            st(dve.reciprocal(STAT[:, 12:14], STAT[:, 8:10]))
            tt(PR[:, :, CHUNK:], PR[:, :, CHUNK:],
               STAT[:, 12:14].rearrange("p (h o) -> p h o", o=1).to_broadcast([P, 2, 192]),
               ALU.mult).then_inc(s_ap, 1)
            st.end()
            dve.wait_ge(s_at, a + 1)
            copy(PT[:, :, :], PX[:, :].rearrange("p (n c) -> p n c", n=4)).then_inc(s_ac, 1)

        def att_split(l, t, m):
            a = (4 * l + t) * 8 + m
            dve.wait_ge(s_ao, a + 1)
            blk = slice(m * P, (m + 1) * P)
            st = Steps(dve, d_split, a, 1)
            st(ts_(AH[:, ds(t, 1), blk], PX[:, 0:P].rearrange("p (o c) -> p o c", o=1), 1.0, None, ALU.mult))
            tt(AL[:, ds(t, 1), blk], PX[:, 0:P].rearrange("p (o c) -> p o c", o=1),
               AH[:, ds(t, 1), blk].bitcast(F32), ALU.subtract).then_inc(s_ad, 1)

        def exponent(l, t, half, n):
            c = LEVELS[n + 1]
            cum, e = halves(CUM[:, cols(half)], c), halves(E[:, n % 3, :], c)
            meet = cum[:, :, 0, c - 1:c].to_broadcast([P, HALF // (2 * c), c])
            tt(e[:, :, 0, :], meet, cum[:, :, 0, :], ALU.subtract)
            tt(e[:, :, 1, :], cum[:, :, 1, :], meet, ALU.subtract).then_inc(s_sub, 1)

        def factor(l, t, half, n):
            rnd = (4 * l + t) * 2 + half
            c = LEVELS[n + 1]
            dve.wait_ge(s_exp, rnd * 8 + (n if n < 5 else 7) + 1)
            e = halves(E[:, n % 3, :], c)
            for two, x in enumerate((KK, QS)):
                ins = tt(e[:, :, two, :], e[:, :, two, :], halves(x[:, cols(half)], c)[:, :, two, :], ALU.mult)
            ins.then_inc(s_fac, 1)

        def states(l, t, half, lo, hi):
            rnd = 4 * l + t
            for m in range(lo, hi + 1):
                n = 8 * half + m
                bank, col = SM[(m - 1) // 4], ((m - 1) % 4) * P
                if m >= 5:
                    dve.wait_ge(s_stu, rnd * 14 + 7 * half + m - 4)
                last = m % 4 == 0
                if n < 16:
                    dve.wait_ge(s_state, rnd * 16 + n)
                    ins = stt(STATE[:, n % 5, :], STATE[:, (n - 1) % 5, :], EL[:, n - 1:n],
                              bank[:, col:col + P], ALU.mult, ALU.add)
                    ins.then_inc(s_state, 1)
                if last:
                    if n < 16:
                        dve.wait_ge(s_state, rnd * 16 + n + 1)
                    else:
                        dve.wait_ge(s_state, rnd * 16 + n)
                    dve.memset(SMALL[:, 31:32], 0.0).then_inc(s_sr, 1)

        def hg_step(l, t, step):
            half, s = step // 8, step % 8
            rnd = 4 * l + t
            b = head_use(t) + HG_USES * half
            bank3 = lambda i: SM[i][:, :].rearrange("p (n c) -> p n c", n=4)
            mask = lambda n: LEVM[:, n:n + 1, :].to_broadcast([P, 4, P])
            if s < 5:
                factor(l, t, half, s + 1)
            if s < 4:
                exponent(l, t, half, s + 2) if s != 3 else None
            if s == 2:
                c3 = lambda x: x.rearrange("p (n c) -> p n c", c=CHUNK)
                cum = c3(CUM[:, cols(half)])
                tt(c3(KE[:, :]), cum[:, :, CHUNK - 1:CHUNK].to_broadcast([P, 8, CHUNK]), cum,
                   ALU.subtract).then_inc(s_sub, 1)
            if s == 3:
                exponent(l, t, half, 5)
                dve.wait_ge(s_exp, (rnd * 2 + half) * 8 + 7)
                tt(KE[:, :], KE[:, :], KK[:, cols(half)], ALU.mult).then_inc(s_ket, 1)
                tt(QE[:, :], QE[:, :], QS[:, cols(half)], ALU.mult).then_inc(s_qe, 1)
            if s == 6 and half == 0:
                exponent(l, t, 1, 0)
            if s == 7 and half == 0:
                exponent(l, t, 1, 1)
                factor(l, t, 1, 0)
            if s == 0:
                written(l, b)
                tt(ST[:, :, :], bank3(0), mask(0), ALU.mult).then_inc(s_sr, 1)
            if s < 6:
                written(l, b + s + 1)
                dve.wait_ge(s_sr, use(l, b + s) + 1)
                dve.memset(SMALL[:, 31:32], 0.0)
                dve.copy_predicated(ST[:, :, :], mask(s + 1), bank3((s + 1) % 2)).then_inc(s_sr, 1)
            if s == 5:
                written(l, b + 7)
                copy(KE[:, :], SM[1][:, :]).then_inc(s_sr, 1)
            if s == 6:
                written(l, b + 8)
                if half == 0:
                    dve.wait_ge(s_el, rnd + 1)
                states(l, t, half, 1, 4)
            if s == 7:
                written(l, b + 9)
                states(l, t, half, 5, 8)
                written(l, b + 10)
                ts_(OF[:, ds(t, 1), cols(half)], SM[0][:, :].rearrange("p (o c) -> p o c", o=1),
                    1.0, None, ALU.mult).then_inc(s_sr, 1)

        def hg_norm(l, t, half):
            rnd = (4 * l + t) * 2 + half
            b = head_use(t) + HG_USES * half
            st = Steps(dve, d_hgn, rnd, SIZES["hgn"])
            written(l, b + 11)
            ts_(KE[:, :], SM[1][:, :], 1.0 / P, EPS, ALU.mult, ALU.add).then_inc(s_sr, 1)
            dve.wait_ge(s_osd, rnd + 1)
            r3 = lambda x: x.rearrange("p (o c) -> p o c", o=1)
            ke = r3(KE[:, :])
            st(dve.reciprocal(KE[:, :], KE[:, :]))
            st(stt(ke, ke, PAR[:, PHG:PHG + 1], OF[:, ds(t, 1), cols(half)], ALU.mult, ALU.mult))
            st(tt(ke, ke, GATE[:, ds(t, 1), cols(half)], ALU.mult))
            st(ts_(GH[:, ds(t, 1), cols(half)], ke, 1.0, None, ALU.mult))
            ins = tt(GL[:, ds(t, 1), cols(half)], ke, GH[:, ds(t, 1), cols(half)].bitcast(F32), ALU.subtract)
            if half == 1:
                ins.then_inc(s_hgd, 1)
            st.end()

        def prepare(l, t):
            rnd = 4 * l + t
            o = 4 * t + (O_HEAD + 3)
            st = Steps(dve, d_prep, rnd, SIZES["prep"])
            apart(dve, s_pro)
            st(ts_(STAT[:, 14:15], PAR[:, ds(t + PLB, 1)], 1.0, None, ALU.mult))
            st(ts_(STAT[:, 15:16], PAR[:, ds(t + POML, 1)], 1.0, None, ALU.mult))
            st(dve.memset(STATE[:, 0, :], 0.0))
            dve.memset(SMALL[:, 31:32], 0.0).then_inc(s_state, 1)
            dve.wait_ge(s_taken[1], taken(l, o, 1, 1))
            ts_(CUM[:, :], CUM[:, :], TINY, None, ALU.max).then_inc(s_clamp, 1)
            st(ts_(KK[:, :], KK[:, :], STAT[:, 15:16], None, ALU.mult))
            b = token_major_use(t)
            for half in range(2):
                written(l, b + half)
                copy(IT[:, 4 * half:4 * half + 4, :],
                     SM[half][:, :].rearrange("p (n c) -> p n c", n=4)).then_inc(s_sr, 1)
            dve.wait_ge(s_ln, rnd + 1)
            for n in range(SEQ // CHUNK):
                c = CUM[:, n * CHUNK:(n + 1) * CHUNK]
                ins = dve.tensor_tensor_scan(c, ONES[:, 0:CHUNK], c, 0.0, ALU.mult, ALU.add)
            st(ins)
            dve.memset(SMALL[:, 31:32], 0.0).then_inc(s_cum, 1)
            exponent(l, t, 0, 0)
            exponent(l, t, 0, 1)
            factor(l, t, 0, 0)
            st.end()

        SINKT = SMALL[:, 24:26]

        def head_round(l, t, fresh, behind):
            if fresh:
                st = Steps(dve, d_sink, 4 * l + t, 1)
                st(ts_(SINKT, PAR[:, ds(t + PSINK, 2, step=PAIRS)], 1.0, None, ALU.mult))
            for u in range(16):
                if behind and u == 8:
                    hg_norm(l, t - 1, 0)
                if fresh:
                    if u % 2 == 0:
                        att = att_shift(l, t, u // 2)
                    else:
                        att_probs(l, t, u // 2, att)
                if behind:
                    hg_step(l, t - 1, u)
                if fresh and u % 2 == 1:
                    att_split(l, t, u // 2)
            if behind:
                hg_norm(l, t - 1, 1)
            if fresh:
                prepare(l, t)

        with dve.Fori(0, DEPTH) as l:
            st = Steps(dve, d_par, l, 1)
            st(ts_(PAR[:, :], PARA[:, ds(l, 1), :].rearrange("p o n -> p (o n)"), 1.0, None, ALU.mult))
            norm(l, 0, B_NORM1, PG1)
            dve.wait_ge(s_sp, 32 * l + 32)
            dve.memset(KF[:, 0:P], 0.0)
            dve.memset(VT[:, 0, :], 0.0)
            for half in range(2):
                written(l, B_QK + half)
                ins = copy(VT[:, 1 + 4 * half:5 + 4 * half, :],
                           SM[half][:, :].rearrange("p (n c) -> p n c", n=4))
                ins.then_inc(s_sr, 1)
            dve.wait_ge(s_rl, 16 * l + 16)
            for i in range(5):
                qk(l, i)
            dve.wait_ge(s_qkd, 5 * l + 5)
            head_round(l, 0, True, False)
            with dve.Fori(1, NH) as t:
                head_round(l, t, True, True)
            head_round(l, NH, False, True)
            with dve.Fori(0, KT // 2) as jj:
                for h in range(2):
                    w, o = 6 * jj + (W_MERGE + 3 * h), 8 * jj + (O_MERGE + 4 * h)
                    for i in range(2):
                        dve.wait_ge(s_taken[i], taken(l, o + i, i, 1))
                        for half in range(2):
                            dve.wait_ge(s_gemm, used(l, w + 2, 4 * i + 2 * (half + 1)))
                            tt(SA[:, i, cols(half)], SA[:, i, cols(half)], G[2 * i + half][:, :],
                               ALU.mult).then_inc(s_taken[i], 1)
                    dve.wait_ge(s_taken[0], taken(l, o + 2, 0, 1))
                    dve.wait_ge(s_taken[1], taken(l, o + 3, 1, 1))
                    tt(MG[:, ds(2 * jj + h, 1), :], SA[:, 0:1, :], SA[:, 1:2, :], ALU.add).then_inc(s_mg, 1)
            for i in range(2 * KT):
                dve.wait_ge(s_mh, l * 16 + i + 1)
                c = cols(i // KT)
                tt(HL[:, i % KT, c], MG[:, i % KT, c], HH[:, i % KT, c].bitcast(F32),
                   ALU.subtract).then_inc(s_ml, 1)
            with dve.Fori(0, KT // 2) as jj:
                for h in range(2):
                    w, o = 2 * jj + (W_OUT + h), 2 * jj + (O_OUT + h)
                    dve.wait_ge(s_xb, 32 * l + 32)
                    for half in range(2):
                        dve.wait_ge(s_gemm, used(l, w, 4 * (half + 1)))
                        x = XT[:, ds(2 * jj + h, 1), cols(half)]
                        tt(x, x, G[2 * h + half][:, :].rearrange("p (o c) -> p o c", o=1),
                           ALU.add).then_inc(s_taken[h], 1)
            norm(l, 1, B_NORM2, PG2)
            st = Steps(dve, d_z, l, 1)
            st(dve.memset(CB[:, :, 0:2], 0.0))

            def up(g, w, o, buf):
                n = (l * HIDDEN_GROUPS + g) * 2
                st = Steps(dve, d_ffn, l * HIDDEN_GROUPS + g, 4)
                for i in range(2):
                    tap = lambda j: PAR[:, ds(2 * g + (PCW + j * FT + i), 1)]
                    dve.wait_ge(s_taken[0], taken(l, o + 2 * i, 0, 1))
                    co, cb = CO[:, i, :], CB[:, i, :]
                    st(ts_(co, cb[:, 0:SEQ], tap(0), tap(3), ALU.mult, ALU.add))
                    st(stt(co, cb[:, 1:SEQ + 1], tap(1), co, ALU.mult, ALU.add))
                    stt(co, cb[:, 2:SEQ + 2], tap(2), co, ALU.mult, ALU.add).then_inc(s_co, 1)
                    dve.wait_ge(s_si, n + i + 1)
                    for half in range(2):
                        dve.wait_ge(s_gemm, used(l, w + 2 * i + 1, 4 * (half + 1)))
                        tt(UF[:, i, cols(half)], co[:, cols(half)], G[2 + half][:, :],
                           ALU.mult).then_inc(s_taken[1], 1)
                    dve.wait_ge(s_uhi, n + i + 1)
                    tt(UL[:, buf, i, :], UF[:, i, :], UH[:, buf, i, :].bitcast(F32),
                       ALU.subtract).then_inc(s_ulo, 1)
                st.end()

            def down(w, o, done=False):
                for j in range(KT):
                    par = j % 2
                    for half in range(2):
                        dve.wait_ge(s_gemm, used(l, w + j // 4, 2 * (j % 4) + half + 1))
                        x = XT[:, j, cols(half)]
                        tt(x, x, G[2 * par + half][:, :], ALU.add).then_inc(s_taken[par], 1)
                    if done:
                        dve.wait_ge(s_taken[par], taken(l, o + j, par, 1))
                        dve.memset(SMALL[:, 31:32], 0.0).then_inc(s_x, 1)

            up(0, W_FFN, O_FFN, 0)
            with dve.Fori(0, HIDDEN_GROUPS // 2) as p:
                w, o = 12 * p + (W_FFN + 4), 24 * p + (O_FFN + 4)
                up(2 * p + 1, w, o, 1)
                down(w + 4, o + 4)
                up(2 * p + 2, w + 6, o + 12, 0)
                down(w + 10, o + 16)
            down(W_LAYER - 2, O_LAYER - 8, True)
        for b in range(2 * NB):
            written(DEPTH, b)
            if b % 2 == 0 and b >= 4:
                dve.wait_ge(s_out[b // 2 % 2], 16 * (b // 4))
            copy(OUTB[:, (b // 2) % 2, cols(b % 2)], SM[b % 2][:, :]).then_inc(s_sr, 1)

    block.__exit__(None, None, None)


SIZES = {"init": 33, "norm": 2, "qk": 2, "att": 6, "hgn": 4, "prep": 5}

_INS = ["x", "positions", "norm1_g", "w_in", "q_norm_g", "k_norm_g", "sinks", "lb_logits", "hg_norm_g",
        "w_branch_a", "w_branch_b", "w_out", "norm2_g", "w_up", "conv_w", "conv_b", "w_down"]


def kernel(**inputs):
    import concourse.bacc as _bacc
    from concourse.bass_utils import run_bass_kernel_spmd as _run

    nc = _bacc.Bacc("TRN2", target_bir_lowering=False, num_devices=1)
    arrays, args = {}, {}
    for name in _INS + ["consts"]:
        a = constants() if name == "consts" else np.ascontiguousarray(inputs[name])
        arrays[f"in_{name}"] = a
        args[name] = nc.dram_tensor(f"in_{name}", a.shape, mybir.dt.from_np(a.dtype), kind="ExternalInput").ap()
    out = nc.dram_tensor("out_x", (1, SEQ, D), F32, kind="ExternalOutput").ap()
    build(nc, args, out)
    r = _run(nc, [arrays], core_ids=[0])
    return r.results[0]["out_x"]
```

```python
import concourse.bass as bass
import concourse.mybir as mybir
import numpy as np

F32 = mybir.dt.float32
F32R = mybir.dt.float32r
I32 = mybir.dt.int32
U8 = mybir.dt.uint8
ALU = mybir.AluOpType
ACT = mybir.ActivationFunctionType
AX = mybir.AxisListType
ds = bass.ds

P = 128
SEQ, D, DEPTH = 1024, 1024, 2
CHUNK, HD, NQ, NKV = 64, 64, 8, 2
ROT = HD // 4
NH = 4
DFF = 2816
EPS = 1e-6
THETA = 500000.0
NEG = -1e30
HALF = SEQ // 2
NB = SEQ // P
KT = D // P
FT = DFF // P
PAIRS = NQ // 2
COL_K, COL_V = 512, 640
COL_HQ, COL_HF, COL_HI, COL_HG, COL_GA, COL_GB = 768, 1280, 1792, 2304, 2816, 3840

PG1, PG2, PHG, PLB, PQG, PKG, PCW, PCB = 0, 8, 16, 17, 21, 22, 23, 89
NROW = 111
POML, PSINK, NPAR = 111, 115, 123

C_ID, C_ONES, C_BLK, C_ROT, C_MASK, C_FREQ, C_LEV = 0, 128, 256, 384, 512, 896, 897
NCONST = C_LEV + 7 * P
LEVELS = (0, 32, 16, 8, 4, 2, 1)

W_QK, W_HEAD, W_MERGE, W_OUT, W_FFN, W_LAYER = 0, 6, 22, 46, 54, 120
O_HEAD, O_MERGE, O_OUT, O_FFN, O_LAYER = 6, 22, 54, 62, 194
B_PRO, B_NORM1, B_QK, B_HEAD, B_NORM2, B_LAYER = 18, 0, 2, 24, 128, 130
HG_USES = 12
HEAD_USES = 2 * HG_USES + 2
CONST_LOADS, PARAM_LOADS = 16 * 3, 16 * 11 * DEPTH
PAIRED = ((2, 8), (-4, 8))
HIDDEN_GROUPS = FT // 2
MERGED = [(j, half) for half in range(2) for j in range(KT - 1)] + [(KT - 1, half) for half in range(2)]
TINY = 2.0 ** -63


def constants():
    c = np.zeros((P, NCONST), np.float32)
    c[:, C_ID:C_ID + P] = np.eye(P)
    c[:, C_ONES:C_ONES + P] = 1.0
    for h in range(2):
        s = slice(h * HD, (h + 1) * HD)
        c[s, C_BLK + h * HD:C_BLK + (h + 1) * HD] = 1.0
        for i in range(ROT // 2):
            c[h * HD + ROT // 2 + i, C_ROT + h * HD + i] = -1.0
            c[h * HD + i, C_ROT + h * HD + ROT // 2 + i] = 1.0
    for first in range(2):
        m = np.zeros((P, 192), np.float32)
        m[:CHUNK, 2 * CHUNK:] = NEG
        m[CHUNK:, :CHUNK] = NEG
        if first:
            m[:, :CHUNK] = NEG
        c[:, C_MASK + 192 * first:C_MASK + 192 * (first + 1)] = m
    s, t = np.arange(P)[:, None], np.arange(P)[None, :]
    for n, w in enumerate(LEVELS):
        if w == 0:
            m = s == t
        else:
            m = (s // (2 * w) == t // (2 * w)) & (s % (2 * w) < w) & (t % (2 * w) >= w)
        c[:, C_LEV + P * n:C_LEV + P * (n + 1)] = m
    freq = np.float32(THETA) ** (-np.arange(0, ROT, 2, dtype=np.float32) / np.float32(ROT))
    for h in range(2):
        c[h * HD:h * HD + ROT, C_FREQ] = np.concatenate([freq, freq])
    return c



class Steps:

    def __init__(self, eng, sem, rnd, size):
        self.eng, self.sem, self.base, self.size, self.n = eng, sem, rnd * size, size, 0

    def __call__(self, ins):
        self.n += 1
        ins.then_inc(self.sem, 1)
        self.eng.wait_ge(self.sem, self.base + self.n)

    def end(self):
        assert self.n == self.size, (self.sem, self.n, self.size)


def apart(eng, sem):
    eng.wait_ge(sem, 1)


def taken_before(l, o, par):
    return 1 + l * O_LAYER + o - par


def taken(l, o, par, half):
    return taken_before(l, o, par) + half + 1


def used(l, w, n):
    return 8 * (l * W_LAYER + w) + n


def use(l, b):
    return B_PRO + l * B_LAYER + b


def qk_sum_use(i):
    return B_QK + 2 + 2 * max(2 * i - 1, 0)


def qk_rotate_use(i):
    return B_QK + 2 + 2 * min(2 * i + 2, 9)


def head_use(t):
    return B_HEAD + 2 + HEAD_USES * t


def token_major_use(t):
    return B_HEAD + HEAD_USES * t


def halves(t, c):
    return t.rearrange("p (b two c) -> p b two c", two=2, c=c)


def build(nc, A, out):
    R1 = 16512
    R2 = R1 + 32768
    R3 = R2 + 65536
    R4 = R3 + 65536

    def at(name, off, shape, dt=F32):
        return nc.alloc_sbuf_tensor_at(name, [P] + list(shape), dt, offset=off)

    XT = at("x_t", R1, [KT, SEQ])
    MG = at("merged", R1, [KT, SEQ])
    KF = at("k_feat", R1, [P + SEQ])
    VT = at("v_tok", R1 + 4608, [NB + 1, P])
    CUM = at("cum", R1 + 9216, [SEQ])
    QS = at("hg_q", R1 + 13312, [SEQ])
    KK = at("hg_k", R1 + 17408, [SEQ])
    IT = at("hg_i_tok", R1 + 21504, [NB, P])
    TMP = at("evac", R1 + 25600, [SEQ])
    STATE = at("state", R1 + 29696, [5, P])
    EL = at("exp_last", R1 + 32256, [SEQ // CHUNK])
    HH = at("h_hi", R2, [KT, SEQ], F32R)
    HL = at("h_lo", R2 + 32768, [KT, SEQ], F32R)
    XIN = at("x_in", R2, [NB, D])
    AH = at("a_hi", R3, [4, SEQ], F32R)
    AL = at("a_lo", R3 + 16384, [4, SEQ], F32R)
    GH = at("g_hi", R3 + 32768, [4, SEQ], F32R)
    GL = at("g_lo", R3 + 49152, [4, SEQ], F32R)
    QF = at("q_feat", R3, [4, SEQ])
    OF = at("o_feat", R3 + 32768, [4, SEQ])
    GATE = at("gate", R3 + 49152, [4, SEQ])
    QR = [at(f"qk_raw{i}", R3 + x, [SEQ]) for i, x in enumerate((32768, 45056))]
    SQ = [at(f"qk_sq{i}", R3 + x, [SEQ]) for i, x in enumerate((36864, 61440))]
    T2 = at("qk_rotated", R3 + 40960, [SEQ])
    QKR = at("qk_rs", R3 + 28672, [SEQ])
    ROPE = at("rope", R3 + 53248, [2, SEQ])
    NSQ = at("norm_sq", R3 + 32768, [4, HALF])
    NACC = at("norm_sum", R3 + 40960, [SEQ])
    NRS = at("norm_rs", R3 + 45056, [SEQ])
    NHF = at("norm_h", R3 + 49152, [2, HALF])
    ANG = [at(f"ang{i}", R3 + 4096 * i, [SEQ]) for i in range(5)]
    POSI = at("pos_i", R3 + 20480, [SEQ], I32)
    PROW = at("par_rows", R3 + 24576, [2, P])
    LEVF = at("level_f", R3 + 28672, [896])
    OUTB = at("out_rows", R3, [2, D])
    UH = at("u_hi", R3, [2, 2, SEQ], F32R)
    UL = at("u_lo", R3 + 16384, [2, 2, SEQ], F32R)
    CB = at("conv_in", R3 + 32768, [2, SEQ + 2])
    CO = at("conv_out", R3 + 41088, [2, SEQ])
    UF = at("u_f", R3 + 49280, [2, SEQ])
    r = R4

    def more(name, shape, size, dt=F32):
        nonlocal r
        r += size
        return at(name, r - size, shape, dt)

    RAW = more("w_raw", [2, SEQ], 8192)
    WH = more("w_hi", [2, SEQ], 8192, F32R)
    WL = more("w_lo", [2, SEQ], 8192, F32R)
    CONST = more("consts", [C_LEV], 3616)
    LEVM = more("level_masks", [7, P], 896, U8)
    PARA = more("par_all", [DEPTH, NPAR], 992)
    PAR = more("par", [NPAR], 512)
    SA = at("sig", r, [2, SEQ])
    E = more("decay", [3, HALF], 6144)
    ST = more("s_t", [4, P], 2048)
    QE = more("q_decayed", [HALF], 2048)
    KE = more("k_decayed", [HALF], 2048)
    QB = more("q_block", [P], 512)
    PR = more("probs", [2, 2 * P], 2048)
    PT = more("probs_t", [4, P], 2048)
    GA = [at(f"gates_{i}", x, [1, SEQ]) for i, x in enumerate((R1, R1 + 4096, R1 + 25600, r - 4096))]
    STAT = more("stats", [16], 64)
    SMALL = more("small", [32], 128)
    assert r <= 229344, r

    IDENT, ONES = CONST[:, C_ID:C_ID + P], CONST[:, C_ONES:C_ONES + P]
    FREQ = CONST[:, C_FREQ:C_FREQ + 1]
    BLK, ROTM = CONST[:, C_BLK:C_BLK + P], CONST[:, C_ROT:C_ROT + P]

    G = [nc.alloc_psum_tensor(f"gemm{i}", [P, 512], F32) for i in range(4)]
    SC = nc.alloc_psum_tensor("scores", [P, 512], F32)
    PX = nc.alloc_psum_tensor("probs_x", [P, 512], F32)
    SM = [nc.alloc_psum_tensor(f"small_ps{i}", [P, 512], F32) for i in range(2)]

    XS = nc.dram_tensor("x_spill", [P, KT, SEQ], F32, kind="Internal")
    RS = nc.dram_tensor("rope_spill", [P, 2, SEQ], F32, kind="Internal")

    sem = nc.alloc_semaphore
    s_const = sem("constants_loaded")
    s_params = sem("params_loaded")
    s_xin = [sem(f"x_loaded{i}") for i in range(2)]
    s_raw = [sem(f"weights_loaded{i}") for i in range(2)]
    s_rawfree = sem("raw_slot_free")
    s_whi = sem("weights_hi")
    s_split = sem("weights_split")
    s_gemm = sem("gemm_progress")
    s_taken = [sem(f"gemm_taken{i}") for i in range(2)]
    s_sw = sem("small_written")
    s_sr = sem("small_read")
    s_par = sem("params_ready")
    s_rope = sem("rope_saved")
    s_rl = sem("rope_loaded")
    s_sp = sem("x_spilled")
    s_xb = sem("x_back")
    s_sq = sem("norm_squares")
    s_acc = sem("norm_sum")
    s_sd = sem("norm_sd")
    s_h = sem("norm_h")
    s_hhi = sem("norm_h_hi")
    s_hlo = sem("norm_h_lo")
    s_qkq = sem("qk_squares")
    s_qks = sem("qk_sd")
    s_qkn = sem("qk_normed")
    s_qkd = sem("qk_done")
    s_ang = sem("angles")
    s_sin = sem("sines")
    s_lbx = sem("lb_exp")
    s_qb = sem("q_block_ready")
    s_as = sem("att_scores")
    s_am = sem("att_shift")
    s_ae = sem("att_exp")
    s_ap = sem("att_probs")
    s_at = sem("att_probs_t")
    s_ac = sem("att_probs_t_copied")
    s_ao = sem("att_out")
    s_ad = sem("att_done")
    s_rows = sem("hg_upper_rows")
    s_clamp = sem("hg_f_clamped")
    s_ln = sem("hg_ln")
    s_cum = sem("hg_cum")
    s_el = sem("hg_exp_last")
    s_sub = sem("hg_exponent")
    s_exp = sem("hg_exp")
    s_fac = sem("hg_factor")
    s_qe = sem("hg_q_decayed")
    s_ket = sem("hg_k_tok")
    s_state = sem("hg_state")
    s_stu = sem("hg_state_used")
    s_osq = sem("hg_o_sq")
    s_osd = sem("hg_o_sd")
    s_hgd = sem("hg_done")
    s_mg = sem("merged_ready")
    s_mh = sem("merged_hi")
    s_ml = sem("merged_lo")
    s_co = sem("conv_ready")
    s_si = sem("silu_ready")
    s_uhi = sem("u_hi_ready")
    s_ulo = sem("u_lo_ready")
    s_x = sem("x_ready")
    s_out = [sem(f"stored{i}") for i in range(2)]
    d_init, d_norm, d_qk, d_att, d_split, d_hgn, d_prep, d_ffn = (
        sem(f"dve_{n}") for n in ("init", "norm", "qk", "att", "a_split", "hg_norm", "prep", "ffn"))
    d_rope = sem("dve_rope")
    d_sink, d_par, d_z = (sem(f"dve_{n}") for n in ("sink", "par", "zero"))

    block = nc.Block()
    block.__enter__()

    @block.sync
    def _(sp):
        sp.dma_start(CONST[:, :], A["consts"][:, 0:C_LEV]).then_inc(s_const, 16)
        sp.dma_start(LEVF[:, :], A["consts"][:, C_LEV:C_LEV + 896]).then_inc(s_const, 16)
        sp.dma_start(POSI[:, :], A["positions"].to_broadcast([P, SEQ])).then_inc(s_const, 16)
        for l in range(DEPTH):
            for name, row, k in (("norm1_g", PG1, KT), ("norm2_g", PG2, KT), ("hg_norm_g", PHG, 1),
                                 ("lb_logits", PLB, NH), ("conv_b", PCB, FT)):
                sp.dma_start(PROW[row:row + k, l, :],
                             A[name][l].rearrange("(k c) -> k c", c=P)).then_inc(s_params, 16)
            for name, row in (("q_norm_g", PQG), ("k_norm_g", PKG)):
                for h in range(2):
                    sp.dma_start(PROW[row:row + 1, l, h * HD:(h + 1) * HD],
                                 A[name][l:l + 1, :]).then_inc(s_params, 16)
            sp.dma_start(PROW[PCW:PCW + 3 * FT, l, :],
                         A["conv_w"][l].rearrange("j (k c) -> (j k) c", c=P)).then_inc(s_params, 16)
            sp.dma_start(PARA[:, l, PSINK:PSINK + NQ],
                         A["sinks"][l:l + 1, :].to_broadcast([P, NQ])).then_inc(s_params, 16)
        x_rows = A["x"][0].rearrange("(b p) d -> p b d", p=P)
        for b in range(2):
            sp.dma_start(XIN[:, 4 * b:4 * b + 4, :], x_rows[:, 4 * b:4 * b + 4, :]).then_inc(s_xin[b], 16)

        def load(l, w, slot, parts, waited=False):
            assert len(parts) == 3
            if not waited:
                apart(sp, s_mg)
                sp.wait_ge(s_rawfree, l * W_LAYER + w + 1)
            for dst, src in parts:
                sp.dma_start(dst, src).then_inc(s_raw[slot], 16)

        def columns(l, w, slot, name, col):
            dst = RAW[:, slot, :].rearrange("p (k c) -> p k c", k=KT)
            src = A[name][l].rearrange("(k p) n -> p k n", p=P)
            load(l, w, slot, [(dst[:, a:b, :], src[:, a:b, ds(col, P)]) for a, b in ((0, 3), (3, 6), (6, 8))])

        with sp.Fori(0, DEPTH) as l:
            columns(l, 0, 0, "w_in", COL_V)
            columns(l, 1, 1, "w_in", COL_K)
            sp.wait_ge(s_x, (l + 1) * KT)
            for k in (slice(0, 4), slice(4, 8)):
                sp.dma_start(XS[:, k, :], XT[:, k, :]).then_inc(s_sp, 16)
            sp.wait_ge(s_rope, 16)
            sp.wait_ge(s_rawfree, l * W_LAYER + 3)
            sp.dma_start(ROPE[:, :, :], RS[:, :, :]).then_inc(s_rl, 16)
            for t in range(PAIRS):
                w = 2 + t
                dst = RAW[:, w % 2, :].rearrange("p (k c) -> p k c", k=KT)
                src = A["w_in"][l].rearrange("(k p) n -> p k n", p=P)
                c0, c1 = t * HD, (t + PAIRS) * HD
                load(l, w, w % 2, [(dst[:, :, 0:HD], src[:, :, c0:c0 + HD]),
                            (dst[:, 0:4, HD:P], src[:, 0:4, c1:c1 + HD]),
                            (dst[:, 4:8, HD:P], src[:, 4:8, c1:c1 + HD])], waited=(t == 0))
            with sp.Fori(0, NH) as t:
                for i, col in enumerate((COL_HG, COL_HI, COL_HQ, COL_HF)):
                    columns(l, W_HEAD + 4 * t + i, i % 2, "w_in", t * P + col)

            def branches(w, slot, j):
                dst = RAW[:, slot, :].rearrange("p (k c) -> p k c", k=KT)
                wa = A["w_branch_a"][l].rearrange("(g t p) n -> g p t n", g=2, t=PAIRS)
                wb = A["w_branch_b"][l].rearrange("(k p) n -> p k n", p=P)
                load(l, w, slot, [(dst[0:HD, 0:4, :], wa[0][:, :, ds(j * P, P)]),
                                  (dst[HD:P, 0:4, :], wa[1][:, :, ds(j * P, P)]),
                                  (dst[:, 4:8, :], wb[:, :, ds(j * P, P)])])

            for j in range(2):
                columns(l, W_MERGE + 2 * j, 0, "w_in", j * P + COL_GA)
                columns(l, W_MERGE + 2 * j + 1, 1, "w_in", j * P + COL_GB)
            for j in range(2):
                branches(W_MERGE + 4 + j, j, j)
            with sp.Fori(1, KT // 2) as jj:
                for h in range(2):
                    w = 6 * jj + (W_MERGE + 3 * h)
                    j = 2 * jj + h
                    columns(l, w, (3 * h) % 2, "w_in", j * P + COL_GA)
                    columns(l, w + 1, (3 * h + 1) % 2, "w_in", j * P + COL_GB)
                    branches(w + 2, (3 * h + 2) % 2, j)
            for h in range(2):
                columns(l, W_OUT + h, h, "w_out", h * P)
            sp.wait_ge(s_ml, (l + 1) * 2 * KT)
            for k in (slice(0, 4), slice(4, 8)):
                sp.dma_start(XT[:, k, :], XS[:, k, :]).then_inc(s_xb, 16)
            with sp.Fori(1, KT // 2) as jj:
                for h in range(2):
                    columns(l, 2 * jj + (W_OUT + h), h, "w_out", (2 * jj + h) * P)

            def up(g, w):
                for i in range(2):
                    columns(l, w + 2 * i, 0, "w_up", (2 * g + i) * P)
                    columns(l, w + 2 * i + 1, 1, "w_up", (2 * g + i) * P + DFF)

            def down(g, w):
                for h in range(2):
                    dst = RAW[:, h, :].rearrange("p (k n) -> p k n", k=2)
                    src = A["w_down"][l].rearrange("(k p) n -> p k n", p=P)
                    c = h * HALF
                    load(l, w + h, h, [(dst[:, 0:1, :], src[:, ds(2 * g, 1), c:c + HALF]),
                                    (dst[:, 1:2, 0:256], src[:, ds(2 * g + 1, 1), c:c + 256]),
                                    (dst[:, 1:2, 256:HALF], src[:, ds(2 * g + 1, 1), c + 256:c + HALF])])

            up(0, W_FFN)
            with sp.Fori(0, HIDDEN_GROUPS // 2) as p:
                w = 12 * p + (W_FFN + 4)
                up(2 * p + 1, w)
                down(2 * p, w + 4)
                up(2 * p + 2, w + 6)
                down(2 * p + 1, w + 10)
            down(HIDDEN_GROUPS - 1, W_LAYER - 2)
        out_rows = out[0].rearrange("(b p) d -> b p d", p=P)
        for b in range(NB):
            sp.wait_ge(s_sr, use(DEPTH, 2 * b + 1) + 1)
            sp.dma_start(out_rows[b], OUTB[:, b % 2, :]).then_inc(s_out[b % 2], 16)
        for i in range(2):
            sp.wait_ge(s_out[i], 16 * NB // 2)
        sp.wait_ge(s_sp, 32 * DEPTH)

    @block.gpsimd
    def _(pool):
        pool.memset(SMALL[:, 0:1], 0.0).then_inc(s_rawfree, 1)
        pool.memset(SMALL[:, 1:2], 0.0).then_inc(s_rawfree, 1)

        def split(w, slot):
            pool.wait_ge(s_raw[slot], 24 * (w - slot) + 48)
            pool.tensor_tensor(WH[:, slot, :], RAW[:, slot, :], ONES[:, 0:1].to_broadcast([P, SEQ]),
                               ALU.mult).then_inc(s_whi, 1)
            pool.wait_ge(s_whi, w + 1)
            pool.tensor_tensor(WL[:, slot, :], RAW[:, slot, :], WH[:, slot, :].bitcast(F32),
                               ALU.subtract).then_inc(s_split, 1)
            pool.wait_ge(s_split, w + 1)
            pool.tensor_tensor(SMALL[:, 2:3], SMALL[:, 0:1], SMALL[:, 1:2], ALU.add).then_inc(s_rawfree, 1)

        pool.wait_ge(s_const, CONST_LOADS)
        split(0, 0)
        split(1, 1)
        with pool.Fori(1, DEPTH * W_LAYER // 2) as u:
            for s in range(2):
                pool.wait_ge(s_gemm, 16 * u + 8 * (s - 1))
                split(2 * u + s, s)

    @block.tensor
    def _(pe):
        pe.wait_ge(s_const, CONST_LOADS)
        pe.wait_ge(s_params, PARAM_LOADS)
        for b in range(B_PRO):
            if b >= 2:
                pe.wait_ge(s_sr, b - 1)
            bank = SM[b % 2]
            if b < 2:
                mm = pe.transpose(bank[:, 0:NROW], PROW[0:NROW, b, :], IDENT[0:NROW, 0:NROW])
            else:
                j, half = (b - 2) % KT, (b - 2) // KT
                if j == 0:
                    pe.wait_ge(s_xin[half], 16)
                for i in range(4):
                    mm = pe.transpose(bank[:, i * P:(i + 1) * P],
                                      XIN[:, 4 * half + i, j * P:(j + 1) * P], IDENT)
            mm.then_inc(s_sw, 1)

        def small(l, b, par):
            pe.wait_ge(s_sr, use(l, b) - 1)
            return SM[par]

        def passes(slot, xh, xl, half, weights, dst, marks, part=None, h_count=None):
            steps = [(a, x, k) for k in range(len(weights))
                     for a, x in ((WH, xh), (WH, xl), (WL, xh))]
            total = len(steps)
            lo, hi = (0, total) if part is None else (part * total // 2, (part + 1) * total // 2)
            for n in range(lo, hi):
                a, x, k = steps[n]
                if h_count is not None and n % 3 == 0:
                    pe.wait_ge(s_hlo, h_count + (k + 1))
                mm = pe.matmul(dst, a[:, slot, weights[k]], x(k, half), start=(n == 0),
                               stop=(n == total - 1))
                if (n + 1) * marks % total == 0:
                    mm.then_inc(s_gemm, 1)

        def moving(t):
            return lambda k, half: t[:, k, half * HALF:(half + 1) * HALF]

        whole = [slice(k * P, (k + 1) * P) for k in range(KT)]

        def tile(l, w, slot, o, par, half, part=None, marks=4, h_count=None):
            if part in (None, 0) and half == 0:
                pe.wait_ge(s_split, l * W_LAYER + w + 1)
                pe.wait_ge(s_taken[par], taken_before(l, o, par))
            passes(slot, moving(HH), moving(HL), half, whole, G[2 * par + half][:, :],
                   marks, part, h_count)

        def first_tiles(l, norm, w, o):
            for half in range(2):
                h_count = (2 * l + norm) * 16 + 8 * half
                for i in range(2):
                    marks = (2, 2) if half == 0 else (4, 8)
                    tile(l, w + i, i, o + i, i, half, marks=marks[i], h_count=h_count if i == 0 else None)

        def norm_sum(l, n, b):
            for half in range(2):
                pe.wait_ge(s_acc, (2 * l + n) * 14 + 7 * (half + 1))
                bank = small(l, b + half, half)
                pe.matmul(bank[:, :], ONES, NACC[:, half * HALF:(half + 1) * HALF],
                          start=True, stop=True).then_inc(s_sw, 1)

        def qk_sum(l, i):
            for half in range(2):
                bank = small(l, qk_sum_use(i) + half, half)
                pe.wait_ge(s_qkq, l * 10 + 2 * i + half + 1)
                pe.matmul(bank[:, :], BLK, SQ[i % 2][:, half * HALF:(half + 1) * HALF],
                          start=True, stop=True).then_inc(s_sw, 1)

        def qk_rotate(l, i):
            pe.wait_ge(s_qkn, l * 5 + i + 1)
            for half in range(2):
                bank = small(l, qk_rotate_use(i) + half, half)
                pe.matmul(bank[:, :], ROTM, QR[i % 2][:, half * HALF:(half + 1) * HALF],
                          start=True, stop=True).then_inc(s_sw, 1)

        def to_token_major(l, b, src):
            for half in range(2):
                bank = small(l, b + half, half)
                for i in range(4):
                    c = (4 * half + i) * P
                    mm = pe.transpose(bank[:, i * P:(i + 1) * P], src[:, c:c + P], IDENT)
                mm.then_inc(s_sw, 1)

        def att_scores(l, t, m):
            pe.wait_ge(s_qb, (4 * l + t) * 8 + m + 1)
            for h in range(2):
                rows = slice(h * HD, (h + 1) * HD)
                if h == 1:
                    pe.wait_ge(s_as, 2 * ((4 * l + t) * 8 + m) + 1)
                pe.matmul(SC[:, h * 192:(h + 1) * 192], QB[rows, :],
                          KF[rows, m * P + CHUNK:(m + 2) * P], start=True, stop=True).then_inc(s_as, 1)

        def att_transpose(l, t, m):
            pe.wait_ge(s_ap, (4 * l + t) * 8 + m + 1)
            for n in range(4):
                mm = pe.transpose(PX[:, n * P:(n + 1) * P], PR[:, n // 2, (n % 2) * P:(n % 2 + 1) * P],
                                  IDENT)
            mm.then_inc(s_at, 1)

        def att_values(l, t, m):
            pe.wait_ge(s_ac, (4 * l + t) * 8 + m + 1)
            for h in range(2):
                rows = slice(h * HD, (h + 1) * HD)
                for kb in range(2):
                    mm = pe.matmul(PX[rows, 0:P], VT[:, m + kb, rows], PT[:, 2 * h + kb, :],
                                   start=(kb == 0), stop=(kb == 1))
            mm.then_inc(s_ao, 1)

        def hg_step(l, t, step):
            half, s = step // 8, step % 8
            b = head_use(t) + HG_USES * half
            rnd = 4 * l + t
            tok = half * HALF

            def product(n, lhs, rhs):
                bank = small(l, b + n, n % 2)
                for i in range(4):
                    c = slice(i * P, (i + 1) * P)
                    mm = pe.matmul(bank[:, c], lhs[:, c], rhs[:, c], start=True, stop=True)
                mm.then_inc(s_sw, 1)

            if s == 0:
                pe.wait_ge(s_cum, rnd + 1)
                product(0, KK[:, tok:tok + HALF], QS[:, tok:tok + HALF])
            if s < 6:
                pe.wait_ge(s_fac, rnd * 12 + 6 * half + s + 1)
                product(s + 1, E[:, s % 3, :], E[:, s % 3, :])
            if s == 5:
                pe.wait_ge(s_ket, rnd * 2 + half + 1)
                bank = small(l, b + 7, 1)
                for i in range(4):
                    mm = pe.transpose(bank[:, i * P:(i + 1) * P], KE[:, i * P:(i + 1) * P], IDENT)
                mm.then_inc(s_sw, 1)
            if s == 6:
                pe.wait_ge(s_sr, use(l, token_major_use(t) + 1) + 1)
                pe.wait_ge(s_sr, use(l, b + 7) + 1)
                for q in range(2):
                    bank = small(l, b + 8 + q, q)
                    for n, i in enumerate((0, 2, 1, 3)):
                        c = 4 * q + i
                        if n == 2:
                            pe.wait_ge(s_rows, rnd * 4 + 2 * half + q + 1)
                        rows = slice((c % 2) * CHUNK, (c % 2 + 1) * CHUNK)
                        mm = pe.matmul(bank[:, i * P:(i + 1) * P], KE[rows, (c // 2) * P:(c // 2 + 1) * P],
                                       IT[rows, 4 * half + c // 2, :], start=True, stop=True)
                        if n == 1:
                            mm.then_inc(s_rows, 1)
                    mm.then_inc(s_sw, 1)
            if s == 7:
                pe.wait_ge(s_sr, use(l, b + 6) + 1)
                pe.wait_ge(s_qe, rnd * 2 + half + 1)
                bank = small(l, b + 10, 0)
                for c in range(8):
                    cols = slice(c * CHUNK, (c + 1) * CHUNK)
                    pe.matmul(bank[:, cols], IT[:, 4 * half + c // 2, :],
                              ST[:, c // 2, (c % 2) * CHUNK:(c % 2 + 1) * CHUNK], start=True, stop=False)
                    n = 8 * half + c
                    pe.wait_ge(s_state, rnd * 16 + n + 1)
                    mm = pe.matmul(bank[:, cols], STATE[:, n % 5, :], QE[:, cols], start=False, stop=True)
                    if c < 7:
                        mm.then_inc(s_stu, 1)
                mm.then_inc(s_sw, 1)

        def hg_norm_sum(l, t, half):
            pe.wait_ge(s_osq, (4 * l + t) * 2 + half + 1)
            bank = small(l, head_use(t) + HG_USES * half + 11, 1)
            pe.matmul(bank[:, :], ONES, QE[:, :], start=True, stop=True).then_inc(s_sw, 1)

        def head_round(l, t, fresh, behind):
            for u in range(16):
                if fresh and u % 2 == 0:
                    att_scores(l, t, u // 2)
                i, half, part = u // 4, u // 2 % 2, u % 2
                tile(l, 4 * t + (W_HEAD + i), i % 2, 4 * t + (O_HEAD + i), i % 2, half, part)
                if fresh:
                    if not behind and u == 1:
                        qk_sum(l, 4)
                        qk_rotate(l, 3)
                    if not behind and u == 5:
                        qk_rotate(l, 4)
                    if u % 2 == 1:
                        att_transpose(l, t, u // 2)
                if behind:
                    if u == 8:
                        hg_norm_sum(l, t - 1, 0)
                    hg_step(l, t - 1, u)
                if fresh and u % 2 == 1:
                    att_values(l, t, u // 2)
            if behind:
                hg_norm_sum(l, t - 1, 1)
            if fresh:
                o = 4 * t + (O_HEAD + 1)
                pe.wait_ge(s_taken[1], taken(l, o, 1, 1))
                to_token_major(l, token_major_use(t), TMP)

        with pe.Fori(0, DEPTH) as l:
            norm_sum(l, 0, B_NORM1)
            first_tiles(l, 0, 0, 0)
            for w in range(2, 6):
                for half in range(2):
                    tile(l, w, w % 2, w, w % 2, half)
                    if w == 2 and half == 0:
                        pe.wait_ge(s_taken[0], taken(l, 0, 0, 1))
                        to_token_major(l, B_QK, TMP)
                    if w >= 2 and half == 0:
                        qk_sum(l, w - 2)
                    if w >= 3 and half == 0:
                        qk_rotate(l, w - 3)
            head_round(l, 0, True, False)
            with pe.Fori(1, NH) as t:
                head_round(l, t, True, True)
            head_round(l, NH, False, True)

            def branches(w, slot, o):
                pe.wait_ge(s_split, l * W_LAYER + w + 1)
                for i, (xh, xl) in enumerate(((AH, AL), (GH, GL))):
                    pe.wait_ge(s_taken[i], taken_before(l, o + i, i))
                    for half in range(2):
                        passes(slot, moving(xh), moving(xl), half, whole[4 * i:4 * i + 4],
                               G[2 * i + half][:, :], 2)

            pe.wait_ge(s_ad, 32 * l + 32)
            pe.wait_ge(s_hgd, 4 * l + 4)
            for j in range(2):
                branches(W_MERGE + 4 + j, j, O_MERGE + 4 + 2 * j)
            with pe.Fori(1, KT // 2) as jj:
                for h in range(2):
                    w, o = 6 * jj + (W_MERGE + 3 * h), 8 * jj + (O_MERGE + 4 * h)
                    for i in range(2):
                        for half in range(2):
                            tile(l, w + i, (3 * h + i) % 2, o + i, i, half)
                    branches(w + 2, (3 * h + 2) % 2, o + 2)
            with pe.Fori(0, KT // 2) as jj:
                for h in range(2):
                    for half in range(2):
                        if half == 0 and h == 0:
                            pe.wait_ge(s_ml, l * 2 * KT + 15)
                        if half == 1 and h == 0:
                            pe.wait_ge(s_ml, l * 2 * KT + 16)
                        tile(l, 2 * jj + (W_OUT + h), h, 2 * jj + (O_OUT + h), h, half)
            norm_sum(l, 1, B_NORM2)

            def up(w, o, first=False):
                if first:
                    first_tiles(l, 1, w, o)
                for i in range(2 if first else 0, 4):
                    for half in range(2):
                        tile(l, w + i, i % 2, o + i, i % 2, half)

            def down(g, w, o, buf):
                pe.wait_ge(s_ulo, (l * HIDDEN_GROUPS + g + 1) * 2)
                for j in range(KT):
                    slot, par = j // 4, j % 2
                    if j % 4 == 0:
                        pe.wait_ge(s_split, l * W_LAYER + w + slot + 1)
                    pe.wait_ge(s_taken[par], taken_before(l, o + j, par))
                    cols = [slice(k * HALF + (j % 4) * P, k * HALF + (j % 4 + 1) * P) for k in range(2)]
                    for half in range(2):
                        passes(slot, moving(UH[:, buf]), moving(UL[:, buf]), half, cols,
                               G[2 * par + half][:, :], 1)

            up(W_FFN, O_FFN, True)
            with pe.Fori(0, HIDDEN_GROUPS // 2) as p:
                w, o = 12 * p + (W_FFN + 4), 24 * p + (O_FFN + 4)
                up(w, o)
                down(2 * p, w + 4, o + 4, 0)
                up(w + 6, o + 12)
                down(2 * p + 1, w + 10, o + 16, 1)
            down(HIDDEN_GROUPS - 1, W_LAYER - 2, O_LAYER - 8, 0)
        for b in range(2 * NB):
            if b == 0:
                pe.wait_ge(s_x, (DEPTH + 1) * KT)
            bank = small(DEPTH, b, b % 2)
            for i in range(4):
                mm = pe.transpose(bank[:, i * P:(i + 1) * P],
                                  XT[:, 4 * (b % 2) + i, (b // 2) * P:(b // 2 + 1) * P], IDENT)
            mm.then_inc(s_sw, 1)

    @block.scalar
    def _(act):
        f = nc.scalar.activation
        act.wait_ge(s_ang, 2)
        for i in range(2):
            f(ROPE[:, i, :], ANG[3 + i][:, :], ACT.Sin).then_inc(s_sin, 1)
        act.wait_ge(s_sin, 2)
        act.dma_start(RS[:, :, :], ROPE[:, :, :]).then_inc(s_rope, 16)
        act.wait_ge(s_lbx, 1)
        f(SMALL[:, 8:16], SMALL[:, 8:16], ACT.Exp).then_inc(s_lbx, 1)

        def cols(half):
            return slice(half * HALF, (half + 1) * HALF)

        def evac(l, w, o, par, half, dst, func=ACT.Copy, n=None, **kw):
            act.wait_ge(s_gemm, used(l, w, 4 * (half + 1) if n is None else n))
            f(dst, G[2 * par + half][:, :], func, **kw).then_inc(s_taken[par], 1)

        def rsqrt(x, done, n, dst=None):
            dst = x if dst is None else dst
            f(dst, x, ACT.Ln).then_inc(done, 1)
            act.wait_ge(done, 2 * n + 1)
            f(dst, dst, ACT.Exp, scale=-0.5).then_inc(done, 1)

        def norm(l, n):
            r0 = 2 * l + n
            for half in range(2):
                for j in range(KT):
                    i = half * KT + j
                    if half == 0:
                        if n == 0:
                            act.wait_ge(s_x, l * KT + j + 1)
                        else:
                            act.wait_ge(s_taken[j % 2], taken(l, O_OUT + j, j % 2, 1))
                    if j >= 4 or half == 1:
                        k = i - 4
                        act.wait_ge(s_acc, r0 * 14 + 7 * (k // KT) + max(k % KT, 1))
                    f(NSQ[:, i % 4, :], XT[:, j, cols(half)], ACT.Square).then_inc(s_sq, 1)
            for half in range(2):
                act.wait_ge(s_sr, use(l, (B_NORM1, B_NORM2)[n] + half) + 1)
                rsqrt(NRS[:, cols(half)], s_sd, r0 * 2 + half)
            for i in range(2 * KT):
                act.wait_ge(s_h, r0 * 16 + i + 1)
                f(HH[:, i % KT, cols(i // KT)], NHF[:, i % 2, :], ACT.Copy).then_inc(s_hhi, 1)

        def qk_rsqrt(l, i):
            for half in range(2):
                act.wait_ge(s_sr, use(l, qk_sum_use(i) + half) + 1)
                rsqrt(SQ[i % 2][:, cols(half)], s_qks, l * 10 + 2 * i + half, QKR[:, cols(half)])

        def q_block(l, t, m):
            f(QB[:, :], QF[:, ds(t, 1), m * P:(m + 1) * P], ACT.Copy).then_inc(s_qb, 1)

        def att_exp(l, t, m):
            act.wait_ge(s_am, (4 * l + t) * 8 + m + 1)
            for h in range(2):
                f(PR[:, h, CHUNK:], PR[:, h, CHUNK:], ACT.Exp, bias=STAT[:, 4 + h:5 + h],
                  scale=HD ** -0.5, accum_out=STAT[:, 8 + h:9 + h])
            f(STAT[:, 10:12], STAT[:, 6:8], ACT.Exp).then_inc(s_ae, 1)

        def hg_exp(l, t, half, n):
            rnd = (4 * l + t) * 2 + half
            sub = (0, 1, 2, 3, 4, 5, 5, 6)[n]
            act.wait_ge(s_sub, rnd * 7 + sub + 1)
            if n == 6:
                f(QE[:, :], CUM[:, cols(half)], ACT.Exp).then_inc(s_exp, 1)
            else:
                x = KE[:, :] if n == 5 else E[:, (n if n < 5 else 5) % 3, :]
                f(x, x, ACT.Exp).then_inc(s_exp, 1)

        def hg_step(l, t, step):
            half, s = step // 8, step % 8
            for n in {0: (2,), 1: (3,), 2: (4, 5, 6), 3: (7,)}.get(s, ()):
                hg_exp(l, t, half, n)
            if half == 0 and s in (6, 7):
                hg_exp(l, t, 1, s - 6)
            if s == 7:
                act.wait_ge(s_sr, use(l, head_use(t) + HG_USES * half + 10) + 1)
                f(QE[:, :], (OF[:, ds(t, 1), cols(half)]), ACT.Square).then_inc(s_osq, 1)

        def hg_norm(l, t, half, part=None):
            n = (4 * l + t) * 2 + half
            if part in (None, 0):
                act.wait_ge(s_sr, use(l, head_use(t) + HG_USES * half + 11) + 1)
                f(KE[:, :], KE[:, :], ACT.Ln).then_inc(s_osd, 1)
            if part in (None, 1):
                act.wait_ge(s_osd, 2 * n + 1)
                f(KE[:, :], KE[:, :], ACT.Exp, scale=-0.5).then_inc(s_osd, 1)

        def head_round(l, t, fresh, behind, pair_follows=True):
            if fresh and not behind:
                q_block(l, t, 0)
            for u in range(16):
                if not fresh and u in (5, 9, 13):
                    i = u // 4 - 1
                    for half in range(2):
                        evac(l, W_MERGE + i, O_MERGE + i, i % 2, half, GA[i][:, 0, cols(half)], ACT.Sigmoid)
                if fresh and u in (5, 9):
                    i = u // 4 - 1
                    w, o = 4 * t + (W_HEAD + i), 4 * t + (O_HEAD + i)
                    for half in range(2):
                        if i == 0:
                            evac(l, w, o, 0, half, GATE[:, ds(t, 1), cols(half)], ACT.Silu)
                        else:
                            evac(l, w, o, 1, half, TMP[:, cols(half)])
                if fresh and u % 2 == 0:
                    att_exp(l, t, u // 2)
                    if u < 14:
                        q_block(l, t, u // 2 + 1)
                    elif pair_follows:
                        q_block(l, t + 1, 0)
                    if not behind and u == 2:
                        qk_rsqrt(l, 4)
                if behind:
                    if u == 8:
                        hg_norm(l, t - 1, 0)
                    hg_step(l, t - 1, u)
            if behind and not fresh:
                for half in range(2):
                    evac(l, W_MERGE + 3, O_MERGE + 3, 1, half, GA[3][:, 0, cols(half)], ACT.Sigmoid)
                hg_norm(l, t - 1, 1)
            if fresh:
                w, o = 4 * t + (W_HEAD + 2), 4 * t + (O_HEAD + 2)
                for half in range(2):
                    evac(l, w, o, 0, half, QS[:, cols(half)], ACT.Silu)
                for half in range(2):
                    act.wait_ge(s_gemm, used(l, w + 1, 4 * (half + 1)))
                    f(KK[:, cols(half)], G[2 + half][:, :], ACT.Sigmoid, scale=-1.0)
                    f(CUM[:, cols(half)], G[2 + half][:, :], ACT.Sigmoid).then_inc(s_taken[1], 1)
                if behind:
                    hg_norm(l, t - 1, 1, 0)
                act.wait_ge(s_clamp, 4 * l + t + 1)
                f(CUM[:, :], CUM[:, :], ACT.Ln, bias=LBCUR[:, 0:1], scale=LBCUR[:, 1:2]).then_inc(s_ln, 1)
                if behind:
                    hg_norm(l, t - 1, 1, 1)
                act.wait_ge(s_cum, 4 * l + t + 1)
                f(EL[:, :], CUM[:, CHUNK - 1::CHUNK], ACT.Exp).then_inc(s_el, 1)
                for n in range(2):
                    hg_exp(l, t, 0, n)

        LBCUR = STAT[:, 14:16]

        with act.Fori(0, DEPTH) as l:
            norm(l, 0)
            act.wait_ge(s_sp, 32 * l + 32)
            for half in range(2):
                evac(l, 0, 0, 0, half, TMP[:, cols(half)], n=PAIRED[0][half])
            for i in range(5):
                w = i + 1
                if i >= 2:
                    act.wait_ge(s_qkd, 5 * l + i - 1)
                for half in range(2):
                    act.wait_ge(s_gemm, used(l, w, PAIRED[1][half] if i == 0 else 4 * (half + 1)))
                    f(SQ[i % 2][:, cols(half)], G[2 * (w % 2) + half][:, :], ACT.Square).then_inc(s_qkq, 1)
                    f(QR[i % 2][:, cols(half)], G[2 * (w % 2) + half][:, :], ACT.Copy).then_inc(s_taken[w % 2], 1)
                if i < 4:
                    qk_rsqrt(l, i)
            act.wait_ge(s_qkd, 5 * l + 2)
            head_round(l, 0, True, False)
            with act.Fori(1, NH - 1) as t:
                head_round(l, t, True, True)
            head_round(l, NH - 1, True, True, False)
            head_round(l, NH, False, True)
            with act.Fori(1, KT // 2) as jj:
                for h in range(2):
                    w, o = 6 * jj + (W_MERGE + 3 * h), 8 * jj + (O_MERGE + 4 * h)
                    act.wait_ge(s_mg, 8 * l + 2 * jj + (h + 1))
                    for i in range(2):
                        for half in range(2):
                            evac(l, w + i, o + i, i, half, SA[:, i, cols(half)], ACT.Sigmoid)
            for j, half in MERGED:
                if half == 0:
                    act.wait_ge(s_mg, 8 * l + j + 2)
                f(HH[:, j, cols(half)], MG[:, j, cols(half)], ACT.Copy).then_inc(s_mh, 1)
            norm(l, 1)

            def up(g, w, o, buf, first=False):
                n = (l * HIDDEN_GROUPS + g) * 2
                for i in range(2):
                    for half in range(2):
                        n_gemm = PAIRED[0][half] if first and i == 0 else 4 * (half + 1)
                        evac(l, w + 2 * i, o + 2 * i, 0, half, CB[:, i, 2 + half * HALF:2 + (half + 1) * HALF],
                             n=n_gemm)
                    act.wait_ge(s_co, n + i + 1)
                    f(CO[:, i, :], CO[:, i, :], ACT.Silu).then_inc(s_si, 1)
                    act.wait_ge(s_taken[1], taken(l, o + 2 * i + 1, 1, 1))
                    f(UH[:, buf, i, :], UF[:, i, :], ACT.Copy).then_inc(s_uhi, 1)

            up(0, W_FFN, O_FFN, 0, True)
            with act.Fori(0, HIDDEN_GROUPS // 2) as p:
                w, o = 12 * p + (W_FFN + 4), 24 * p + (O_FFN + 4)
                up(2 * p + 1, w, o, 1)
                up(2 * p + 2, w + 6, o + 12, 0)

    @block.vector
    def _(dve):
        tt, ts_, stt, copy = dve.tensor_tensor, dve.tensor_scalar, dve.scalar_tensor_tensor, dve.tensor_copy

        def cols(half):
            return slice(half * HALF, (half + 1) * HALF)

        def over(ap, shape):
            return ap.to_broadcast(shape)

        for par in range(2):
            dve.memset(SMALL[:, 28 + par:29 + par], 0.0).then_inc(s_taken[par], 1)
        dve.memset(SMALL[:, 30:31], 0.0).then_inc(s_mg, 1)
        init = Steps(dve, d_init, 0, SIZES["init"])
        init(dve.memset(PR[:, :, :], 0.0))
        dve.wait_ge(s_const, CONST_LOADS)
        init(copy(LEVM[:, :, :], LEVF[:, :].rearrange("p (n c) -> p n c", n=7)))
        two_pi, parts = 2 * np.pi, []
        for _ in range(4):
            m, e = np.frexp(two_pi)
            parts.append(float(np.ldexp(np.floor(m * 2048) / 2048, e)))
            two_pi -= parts[-1]
        magic = 1.5 * 2 ** 23
        pos, ang, turns = ANG[0], ANG[1], ANG[2]
        init(copy(pos[:, :], POSI[:, :]))
        init(ts_(ang[:, :], pos[:, :], FREQ, None, ALU.mult))
        for i, quarter in enumerate((0.25, 0.0)):
            red = ANG[3 + i]
            init(ts_(turns[:, :], ang[:, :], float(1 / (2 * np.pi)), quarter, ALU.mult, ALU.add))
            init(ts_(turns[:, :], turns[:, :], magic, None, ALU.add))
            init(ts_(turns[:, :], turns[:, :], -magic, None, ALU.add))
            src = ang
            for c in parts:
                init(stt(red[:, :], turns[:, :], -c, src[:, :], ALU.mult, ALU.add))
                src = red
            init(ts_(red[:, :], red[:, :], quarter * 2 * np.pi, 3.1415925, ALU.add, ALU.min))
            ts_(red[:, :], red[:, :], -3.1415925, None, ALU.max).then_inc(s_ang, 1)
        for b in range(2):
            dve.wait_ge(s_sw, b + 1)
            copy(PARA[:, b, 0:NROW], SM[b][:, 0:NROW]).then_inc(s_sr, 1)
        assert DEPTH == 2
        lbs = [PARA[:, l, PLB:PLB + NH] for l in range(DEPTH)]
        dve.wait_ge(s_sr, 2)
        init(tt(SMALL[:, 4:8], lbs[0], lbs[1], ALU.max))
        for l in range(DEPTH):
            init(tt(SMALL[:, 8 + 4 * l:12 + 4 * l], lbs[l], SMALL[:, 4:8], ALU.subtract))
        init(tt(SMALL[:, 4:8], SMALL[:, 4:8], SMALL[:, 4:8], ALU.subtract))
        dve.memset(SMALL[:, 31:32], 0.0).then_inc(s_lbx, 1)
        dve.wait_ge(s_lbx, 2)
        e0, e1 = SMALL[:, 8:12], SMALL[:, 12:16]
        init(tt(SMALL[:, 16:20], e0, e1, ALU.add))
        init(dve.reciprocal(SMALL[:, 20:24], SMALL[:, 16:20]))
        init(tt(e0, e0, SMALL[:, 20:24], ALU.mult))
        init(tt(e1, e1, SMALL[:, 20:24], ALU.mult))
        init(tt(lbs[0], e0, e0, ALU.subtract))
        init(tt(SMALL[:, 16:20], e0, e1, ALU.add))
        init(tt(lbs[1], SMALL[:, 16:20], e0, ALU.subtract))
        for l in range(DEPTH):
            init(ts_(PARA[:, l, POML:POML + NH], lbs[l], -1.0, 1.0, ALU.mult, ALU.add))
        for b in range(2, B_PRO):
            j, half = (b - 2) % KT, (b - 2) // KT
            dve.wait_ge(s_sw, b + 1)
            copy(XT[:, j, cols(half)], SM[b % 2][:, :]).then_inc(s_sr, 1)
            if half == 1:
                dve.wait_ge(s_sr, b + 1)
                dve.memset(SMALL[:, 31:32], 0.0).then_inc(s_x, 1)
        init.end()

        def written(l, b):
            dve.wait_ge(s_sw, use(l, b) + 1)

        def norm(l, n, b, gain):
            r0 = 2 * l + n
            for half in range(2):
                for j in range(1, KT):
                    i = half * KT + j
                    dve.wait_ge(s_sq, r0 * 16 + i + 1)
                    acc = NACC[:, cols(half)]
                    if j == 1:
                        tt(acc, NSQ[:, (i - 1) % 4, :], NSQ[:, i % 4, :], ALU.add).then_inc(s_acc, 1)
                    else:
                        dve.wait_ge(s_acc, r0 * 14 + 7 * half + j - 1)
                        tt(acc, acc, NSQ[:, i % 4, :], ALU.add).then_inc(s_acc, 1)
            for half in range(2):
                written(l, b + half)
                rs = NRS[:, cols(half)]
                ts_(rs, SM[half][:, :], 1.0 / D, EPS, ALU.mult, ALU.add).then_inc(s_sr, 1)
            for half in range(2):
                rs = NRS[:, cols(half)]
                dve.wait_ge(s_sd, 2 * (r0 * 2 + half + 1))
                for j in range(KT + 1):
                    i = half * KT + j
                    if j < KT:
                        if i >= 2:
                            dve.wait_ge(s_hlo, r0 * 16 + i - 1)
                        stt(NHF[:, i % 2, :], XT[:, j, cols(half)], PAR[:, gain + j:gain + j + 1], rs,
                            ALU.mult, ALU.mult).then_inc(s_h, 1)
                    if j > 0:
                        dve.wait_ge(s_hhi, r0 * 16 + i)
                        tt(HL[:, j - 1, cols(half)], NHF[:, (i - 1) % 2, :],
                           HH[:, j - 1, cols(half)].bitcast(F32), ALU.subtract).then_inc(s_hlo, 1)

        def qk_variance(l, i):
            var = SQ[i % 2]
            for half in range(2):
                written(l, qk_sum_use(i) + half)
                ts_(var[:, cols(half)], SM[half][:, :], 1.0 / HD, EPS, ALU.mult, ALU.add).then_inc(s_sr, 1)

        def qk_norm(l, i):
            st = Steps(dve, d_qk, 5 * l + i, 3)
            gain = PAR[:, PKG:PKG + 1] if i == 0 else PAR[:, PQG:PQG + 1]
            raw, var = QR[i % 2], SQ[i % 2]
            dve.wait_ge(s_qks, 2 * (10 * l + 2 * i + 2))
            rs = QKR[:, :]
            st(stt(var[:, :], var[:, :], -0.5, rs, ALU.mult, ALU.mult))
            st(tt(var[:, :], var[:, :], rs, ALU.mult))
            st(stt(var[:, :], var[:, :], 1.5, rs, ALU.add, ALU.mult))
            dve.wait_ge(s_taken[(i + 1) % 2], taken(l, i + 1, (i + 1) % 2, 1))
            stt(raw[:, :], raw[:, :], gain, var[:, :], ALU.mult, ALU.mult).then_inc(s_qkn, 1)

        def qk_rope(l, i):
            st = Steps(dve, d_rope, 5 * l + i, 1)
            raw = QR[i % 2]
            b = qk_rotate_use(i)
            for half in range(2):
                written(l, b + half)
                tt(T2[:, cols(half)], SM[half][:, :], ROPE[:, 1, cols(half)], ALU.mult).then_inc(s_sr, 1)
            dve.wait_ge(s_sr, use(l, b + 2))
            st(tt(raw[:, :], raw[:, :], ROPE[:, 0, :], ALU.mult))
            dst = KF[:, P:] if i == 0 else QF[:, i - 1, :]
            tt(dst, raw[:, :], T2[:, :], ALU.add).then_inc(s_qkd, 1)

        def att_shift(l, t, m):
            a = (4 * l + t) * 8 + m
            st = Steps(dve, d_att, a, SIZES["att"])
            dve.wait_ge(s_as, 2 * a + 2)
            mask = CONST[:, C_MASK + 192 * (m == 0):C_MASK + 192 * (m == 0) + 192]
            scores = PR[:, :, CHUNK:]
            st(tt(scores, SC[:, 0:384].rearrange("p (h k) -> p h k", h=2),
                  mask.rearrange("p (o k) -> p o k", o=1).to_broadcast([P, 2, 192]), ALU.add))
            st(dve.tensor_reduce(STAT[:, 0:2], scores, AX.X, ALU.max))
            sink = SINKT[:, 0:2]
            st(stt(STAT[:, 2:4], STAT[:, 0:2], HD ** -0.5, sink, ALU.mult, ALU.max))
            st(tt(STAT[:, 6:8], sink, STAT[:, 2:4], ALU.subtract))
            ts_(STAT[:, 4:6], STAT[:, 2:4], -1.0, None, ALU.mult).then_inc(s_am, 1)
            return st

        def att_probs(l, t, m, st):
            a = (4 * l + t) * 8 + m
            dve.wait_ge(s_ae, a + 1)
            st(tt(STAT[:, 8:10], STAT[:, 8:10], STAT[:, 10:12], ALU.add))
            st(dve.reciprocal(STAT[:, 12:14], STAT[:, 8:10]))
            tt(PR[:, :, CHUNK:], PR[:, :, CHUNK:],
               STAT[:, 12:14].rearrange("p (h o) -> p h o", o=1).to_broadcast([P, 2, 192]),
               ALU.mult).then_inc(s_ap, 1)
            st.end()
            dve.wait_ge(s_at, a + 1)
            copy(PT[:, :, :], PX[:, :].rearrange("p (n c) -> p n c", n=4)).then_inc(s_ac, 1)

        def att_split(l, t, m):
            a = (4 * l + t) * 8 + m
            dve.wait_ge(s_ao, a + 1)
            blk = slice(m * P, (m + 1) * P)
            st = Steps(dve, d_split, a, 1)
            st(ts_(AH[:, ds(t, 1), blk], PX[:, 0:P].rearrange("p (o c) -> p o c", o=1), 1.0, None, ALU.mult))
            tt(AL[:, ds(t, 1), blk], PX[:, 0:P].rearrange("p (o c) -> p o c", o=1),
               AH[:, ds(t, 1), blk].bitcast(F32), ALU.subtract).then_inc(s_ad, 1)

        def exponent(l, t, half, n):
            c = LEVELS[n + 1]
            cum, e = halves(CUM[:, cols(half)], c), halves(E[:, n % 3, :], c)
            meet = cum[:, :, 0, c - 1:c].to_broadcast([P, HALF // (2 * c), c])
            tt(e[:, :, 0, :], meet, cum[:, :, 0, :], ALU.subtract)
            tt(e[:, :, 1, :], cum[:, :, 1, :], meet, ALU.subtract).then_inc(s_sub, 1)

        def factor(l, t, half, n):
            rnd = (4 * l + t) * 2 + half
            c = LEVELS[n + 1]
            dve.wait_ge(s_exp, rnd * 8 + (n if n < 5 else 7) + 1)
            e = halves(E[:, n % 3, :], c)
            for two, x in enumerate((KK, QS)):
                ins = tt(e[:, :, two, :], e[:, :, two, :], halves(x[:, cols(half)], c)[:, :, two, :], ALU.mult)
            ins.then_inc(s_fac, 1)

        def states(l, t, half, lo, hi):
            rnd = 4 * l + t
            for m in range(lo, hi + 1):
                n = 8 * half + m
                bank, col = SM[(m - 1) // 4], ((m - 1) % 4) * P
                if m >= 5:
                    dve.wait_ge(s_stu, rnd * 14 + 7 * half + m - 4)
                last = m % 4 == 0
                if n < 16:
                    dve.wait_ge(s_state, rnd * 16 + n)
                    ins = stt(STATE[:, n % 5, :], STATE[:, (n - 1) % 5, :], EL[:, n - 1:n],
                              bank[:, col:col + P], ALU.mult, ALU.add)
                    ins.then_inc(s_state, 1)
                if last:
                    if n < 16:
                        dve.wait_ge(s_state, rnd * 16 + n + 1)
                    else:
                        dve.wait_ge(s_state, rnd * 16 + n)
                    dve.memset(SMALL[:, 31:32], 0.0).then_inc(s_sr, 1)

        def hg_step(l, t, step):
            half, s = step // 8, step % 8
            rnd = 4 * l + t
            b = head_use(t) + HG_USES * half
            bank3 = lambda i: SM[i][:, :].rearrange("p (n c) -> p n c", n=4)
            mask = lambda n: LEVM[:, n:n + 1, :].to_broadcast([P, 4, P])
            if s < 5:
                factor(l, t, half, s + 1)
            if s < 4:
                exponent(l, t, half, s + 2) if s != 3 else None
            if s == 2:
                c3 = lambda x: x.rearrange("p (n c) -> p n c", c=CHUNK)
                cum = c3(CUM[:, cols(half)])
                tt(c3(KE[:, :]), cum[:, :, CHUNK - 1:CHUNK].to_broadcast([P, 8, CHUNK]), cum,
                   ALU.subtract).then_inc(s_sub, 1)
            if s == 3:
                exponent(l, t, half, 5)
                dve.wait_ge(s_exp, (rnd * 2 + half) * 8 + 7)
                tt(KE[:, :], KE[:, :], KK[:, cols(half)], ALU.mult).then_inc(s_ket, 1)
                tt(QE[:, :], QE[:, :], QS[:, cols(half)], ALU.mult).then_inc(s_qe, 1)
            if s == 6 and half == 0:
                exponent(l, t, 1, 0)
            if s == 7 and half == 0:
                exponent(l, t, 1, 1)
                factor(l, t, 1, 0)
            if s == 0:
                written(l, b)
                tt(ST[:, :, :], bank3(0), mask(0), ALU.mult).then_inc(s_sr, 1)
            if s < 6:
                written(l, b + s + 1)
                dve.wait_ge(s_sr, use(l, b + s) + 1)
                dve.memset(SMALL[:, 31:32], 0.0)
                dve.copy_predicated(ST[:, :, :], mask(s + 1), bank3((s + 1) % 2)).then_inc(s_sr, 1)
            if s == 5:
                written(l, b + 7)
                copy(KE[:, :], SM[1][:, :]).then_inc(s_sr, 1)
            if s == 6:
                written(l, b + 8)
                if half == 0:
                    dve.wait_ge(s_el, rnd + 1)
                states(l, t, half, 1, 4)
            if s == 7:
                written(l, b + 9)
                states(l, t, half, 5, 8)
                written(l, b + 10)
                ts_(OF[:, ds(t, 1), cols(half)], SM[0][:, :].rearrange("p (o c) -> p o c", o=1),
                    1.0, None, ALU.mult).then_inc(s_sr, 1)

        def hg_variance(l, t, half):
            written(l, head_use(t) + HG_USES * half + 11)
            ts_(KE[:, :], SM[1][:, :], 1.0 / P, EPS, ALU.mult, ALU.add).then_inc(s_sr, 1)

        def hg_norm(l, t, half):
            rnd = (4 * l + t) * 2 + half
            st = Steps(dve, d_hgn, rnd, SIZES["hgn"])
            dve.wait_ge(s_osd, 2 * rnd + 2)
            r3 = lambda x: x.rearrange("p (o c) -> p o c", o=1)
            ke = r3(KE[:, :])
            st(stt(ke, ke, PAR[:, PHG:PHG + 1], OF[:, ds(t, 1), cols(half)], ALU.mult, ALU.mult))
            st(tt(ke, ke, GATE[:, ds(t, 1), cols(half)], ALU.mult))
            st(ts_(GH[:, ds(t, 1), cols(half)], ke, 1.0, None, ALU.mult))
            ins = tt(GL[:, ds(t, 1), cols(half)], ke, GH[:, ds(t, 1), cols(half)].bitcast(F32), ALU.subtract)
            if half == 1:
                ins.then_inc(s_hgd, 1)
            st.end()

        def prepare(l, t, behind):
            rnd = 4 * l + t
            o = 4 * t + (O_HEAD + 3)
            st = Steps(dve, d_prep, rnd, SIZES["prep"])
            st(ts_(STAT[:, 14:15], PAR[:, ds(t + PLB, 1)], 1.0, None, ALU.mult))
            st(ts_(STAT[:, 15:16], PAR[:, ds(t + POML, 1)], 1.0, None, ALU.mult))
            st(dve.memset(STATE[:, 0, :], 0.0))
            dve.memset(SMALL[:, 31:32], 0.0).then_inc(s_state, 1)
            dve.wait_ge(s_taken[1], taken(l, o, 1, 1))
            ts_(CUM[:, :], CUM[:, :], TINY, None, ALU.max).then_inc(s_clamp, 1)
            st(ts_(KK[:, :], KK[:, :], STAT[:, 15:16], None, ALU.mult))
            b = token_major_use(t)
            for half in range(2):
                written(l, b + half)
                copy(IT[:, 4 * half:4 * half + 4, :],
                     SM[half][:, :].rearrange("p (n c) -> p n c", n=4)).then_inc(s_sr, 1)
            dve.wait_ge(s_ln, rnd + 1)
            for n in range(SEQ // CHUNK):
                c = CUM[:, n * CHUNK:(n + 1) * CHUNK]
                ins = dve.tensor_tensor_scan(c, ONES[:, 0:CHUNK], c, 0.0, ALU.mult, ALU.add)
            st(ins)
            dve.memset(SMALL[:, 31:32], 0.0).then_inc(s_cum, 1)
            exponent(l, t, 0, 0)
            exponent(l, t, 0, 1)
            factor(l, t, 0, 0)
            if behind:
                hg_norm(l, t - 1, 1)
            st.end()

        SINKT = SMALL[:, 24:26]

        def head_round(l, t, fresh, behind):
            if fresh:
                st = Steps(dve, d_sink, 4 * l + t, 1)
                st(ts_(SINKT, PAR[:, ds(t + PSINK, 2, step=PAIRS)], 1.0, None, ALU.mult))
            for u in range(16):
                if not behind and u == 1:
                    qk_variance(l, 4)
                    qk_rope(l, 3)
                if not behind and u == 6:
                    qk_rope(l, 4)
                if fresh:
                    if u % 2 == 0:
                        att = att_shift(l, t, u // 2)
                    else:
                        att_probs(l, t, u // 2, att)
                if not behind and u == 2:
                    qk_norm(l, 4)
                if behind:
                    if u == 8:
                        hg_variance(l, t - 1, 0)
                    if u == 9:
                        hg_norm(l, t - 1, 0)
                    hg_step(l, t - 1, u)
                if fresh and u % 2 == 1:
                    att_split(l, t, u // 2)
            if behind:
                hg_variance(l, t - 1, 1)
            if fresh:
                prepare(l, t, behind)
            else:
                hg_norm(l, t - 1, 1)

        with dve.Fori(0, DEPTH) as l:
            st = Steps(dve, d_par, l, 1)
            st(ts_(PAR[:, :], PARA[:, ds(l, 1), :].rearrange("p o n -> p (o n)"), 1.0, None, ALU.mult))
            norm(l, 0, B_NORM1, PG1)
            dve.wait_ge(s_sp, 32 * l + 32)
            dve.memset(PR[:, :, 0:CHUNK], 0.0)
            dve.memset(KF[:, 0:P], 0.0)
            dve.memset(VT[:, 0, :], 0.0)
            for half in range(2):
                written(l, B_QK + half)
                ins = copy(VT[:, 1 + 4 * half:5 + 4 * half, :],
                           SM[half][:, :].rearrange("p (n c) -> p n c", n=4))
                ins.then_inc(s_sr, 1)
            dve.wait_ge(s_rl, 16 * l + 16)
            qk_variance(l, 0)
            qk_norm(l, 0)
            for i in range(3):
                qk_variance(l, i + 1)
                qk_rope(l, i)
                qk_norm(l, i + 1)
            head_round(l, 0, True, False)
            with dve.Fori(1, NH) as t:
                head_round(l, t, True, True)
            head_round(l, NH, False, True)

            def merge(j, w, o, o_gates, gates):
                for i in range(2):
                    dve.wait_ge(s_taken[i], taken(l, o_gates + i, i, 1))
                    for half in range(2):
                        dve.wait_ge(s_gemm, used(l, w, 4 * i + 2 * (half + 1)))
                        g = gates[i][:, 0, cols(half)]
                        tt(g, g, G[2 * i + half][:, :], ALU.mult).then_inc(s_taken[i], 1)
                dve.wait_ge(s_taken[0], taken(l, o, 0, 1))
                dve.wait_ge(s_taken[1], taken(l, o + 1, 1, 1))
                tt(MG[:, ds(j, 1), :], gates[0][:, :, :], gates[1][:, :, :], ALU.add).then_inc(s_mg, 1)

            def merged_low(n):
                j, half = MERGED[n]
                dve.wait_ge(s_mh, l * 2 * KT + n + 1)
                tt(HL[:, j, cols(half)], MG[:, j, cols(half)], HH[:, j, cols(half)].bitcast(F32),
                   ALU.subtract).then_inc(s_ml, 1)

            for j in range(2):
                merge(j, W_MERGE + 4 + j, O_MERGE + 4 + 2 * j, O_MERGE + 2 * j, GA[2 * j:2 * j + 2])
            gates = [SA[:, 0:1, :], SA[:, 1:2, :]]
            with dve.Fori(1, KT // 2 - 1) as jj:
                for h in range(2):
                    w, o = 6 * jj + (W_MERGE + 3 * h), 8 * jj + (O_MERGE + 4 * h)
                    merge(2 * jj + h, w + 2, o + 2, o, gates)
            for j in (KT - 2, KT - 1):
                if j == KT - 1:
                    for n in range(2 * KT - 2):
                        merged_low(n)
                w, o = W_MERGE + 3 * j, O_MERGE + 4 * j
                merge(j, w + 2, o + 2, o, gates)
            for n in (2 * KT - 2, 2 * KT - 1):
                merged_low(n)
            with dve.Fori(0, KT // 2) as jj:
                for h in range(2):
                    w, o = 2 * jj + (W_OUT + h), 2 * jj + (O_OUT + h)
                    dve.wait_ge(s_xb, 32 * l + 32)
                    for half in range(2):
                        dve.wait_ge(s_gemm, used(l, w, 4 * (half + 1)))
                        x = XT[:, ds(2 * jj + h, 1), cols(half)]
                        tt(x, x, G[2 * h + half][:, :].rearrange("p (o c) -> p o c", o=1),
                           ALU.add).then_inc(s_taken[h], 1)
            norm(l, 1, B_NORM2, PG2)
            st = Steps(dve, d_z, l, 1)
            st(dve.memset(CB[:, :, 0:2], 0.0))

            def up(g, w, o, buf, first=False):
                n = (l * HIDDEN_GROUPS + g) * 2
                st = Steps(dve, d_ffn, l * HIDDEN_GROUPS + g, 4)
                for i in range(2):
                    tap = lambda j: PAR[:, ds(2 * g + (PCW + j * FT + i), 1)]
                    dve.wait_ge(s_taken[0], taken(l, o + 2 * i, 0, 1))
                    co, cb = CO[:, i, :], CB[:, i, :]
                    st(ts_(co, cb[:, 0:SEQ], tap(0), tap(3), ALU.mult, ALU.add))
                    st(stt(co, cb[:, 1:SEQ + 1], tap(1), co, ALU.mult, ALU.add))
                    stt(co, cb[:, 2:SEQ + 2], tap(2), co, ALU.mult, ALU.add).then_inc(s_co, 1)
                    dve.wait_ge(s_si, n + i + 1)
                    for half in range(2):
                        n_gemm = PAIRED[1][half] if first and i == 0 else 4 * (half + 1)
                        dve.wait_ge(s_gemm, used(l, w + 2 * i + 1, n_gemm))
                        tt(UF[:, i, cols(half)], co[:, cols(half)], G[2 + half][:, :],
                           ALU.mult).then_inc(s_taken[1], 1)
                    dve.wait_ge(s_uhi, n + i + 1)
                    tt(UL[:, buf, i, :], UF[:, i, :], UH[:, buf, i, :].bitcast(F32),
                       ALU.subtract).then_inc(s_ulo, 1)
                st.end()

            def down(w, o, done=False):
                for j in range(KT):
                    par = j % 2
                    for half in range(2):
                        dve.wait_ge(s_gemm, used(l, w + j // 4, 2 * (j % 4) + half + 1))
                        x = XT[:, j, cols(half)]
                        tt(x, x, G[2 * par + half][:, :], ALU.add).then_inc(s_taken[par], 1)
                    if done:
                        dve.wait_ge(s_taken[par], taken(l, o + j, par, 1))
                        dve.memset(SMALL[:, 31:32], 0.0).then_inc(s_x, 1)

            up(0, W_FFN, O_FFN, 0, True)
            with dve.Fori(0, HIDDEN_GROUPS // 2) as p:
                w, o = 12 * p + (W_FFN + 4), 24 * p + (O_FFN + 4)
                up(2 * p + 1, w, o, 1)
                down(w + 4, o + 4)
                up(2 * p + 2, w + 6, o + 12, 0)
                down(w + 10, o + 16)
            down(W_LAYER - 2, O_LAYER - 8, True)
        for b in range(2 * NB):
            written(DEPTH, b)
            if b % 2 == 0 and b >= 4:
                dve.wait_ge(s_out[b // 2 % 2], 16 * (b // 4))
            copy(OUTB[:, (b // 2) % 2, cols(b % 2)], SM[b % 2][:, :]).then_inc(s_sr, 1)

    block.__exit__(None, None, None)


SIZES = {"init": 33, "att": 6, "hgn": 3, "prep": 5}

_INS = ["x", "positions", "norm1_g", "w_in", "q_norm_g", "k_norm_g", "sinks", "lb_logits", "hg_norm_g",
        "w_branch_a", "w_branch_b", "w_out", "norm2_g", "w_up", "conv_w", "conv_b", "w_down"]


def kernel(**inputs):
    import concourse.bacc as _bacc
    from concourse.bass_utils import run_bass_kernel_spmd as _run

    nc = _bacc.Bacc("TRN2", target_bir_lowering=False, num_devices=1)
    arrays, args = {}, {}
    for name in _INS + ["consts"]:
        a = constants() if name == "consts" else np.ascontiguousarray(inputs[name])
        arrays[f"in_{name}"] = a
        args[name] = nc.dram_tensor(f"in_{name}", a.shape, mybir.dt.from_np(a.dtype), kind="ExternalInput").ap()
    out = nc.dram_tensor("out_x", (1, SEQ, D), F32, kind="ExternalOutput").ap()
    build(nc, args, out)
    r = _run(nc, [arrays], core_ids=[0])
    return r.results[0]["out_x"]
```

```python
import concourse.bass as bass
import concourse.mybir as mybir
import numpy as np

F32 = mybir.dt.float32
F32R = mybir.dt.float32r
I32 = mybir.dt.int32
U8 = mybir.dt.uint8
ALU = mybir.AluOpType
ACT = mybir.ActivationFunctionType
AX = mybir.AxisListType
ds = bass.ds

P = 128
SEQ, D, DEPTH = 1024, 1024, 2
CHUNK, HD, NQ, NKV = 64, 64, 8, 2
ROT = HD // 4
NH = 4
DFF = 2816
EPS = 1e-6
THETA = 500000.0
NEG = -1e30
HALF = SEQ // 2
NB = SEQ // P
KT = D // P
FT = DFF // P
PAIRS = NQ // 2
COL_K, COL_V = 512, 640
COL_HQ, COL_HF, COL_HI, COL_HG, COL_GA, COL_GB = 768, 1280, 1792, 2304, 2816, 3840

PG1, PG2, PHG, PLB, PQG, PKG, PCW, PCB = 0, 8, 16, 17, 21, 22, 23, 89
NROW = 111
POML, PSINK, NPAR = 111, 115, 123

C_ID, C_ONES, C_BLK, C_ROT, C_MASK, C_FREQ, C_LEV = 0, 128, 256, 384, 512, 896, 897
NCONST = C_LEV + 7 * P
LEVELS = (0, 32, 16, 8, 4, 2, 1)

W_VKQ, W_HEAD, W_MERGE, W_OUT, W_FFN, W_LAYER = 0, 6, 22, 46, 54, 120
O_HEAD, O_MERGE, O_OUT, O_FFN, O_LAYER = 6, 22, 54, 62, 194
B_PRO, B_NORM1, B_QK, B_HEAD, B_NORM2, B_LAYER = 18, 0, 2, 24, 128, 130
HG_USES = 12
HEAD_USES = 2 * HG_USES + 2
CONST_LOADS, PARAM_LOADS = 16 * 3, 16 * 11 * DEPTH
PAIRED = ((2, 8), (-4, 8))
STEP_QUARTERS = [3, 1, 1, 1, 1, 1, 1, 1, 0, 1, 1, 1, 1, 1, 0, 1]
QUARTERS = [range(sum(STEP_QUARTERS[:u]), sum(STEP_QUARTERS[:u + 1])) for u in range(16)]
HIDDEN_GROUPS = FT // 2
MERGED = [(j, half) for half in range(2) for j in range(KT - 1)] + [(KT - 1, half) for half in range(2)]
TINY = 2.0 ** -63


def constants():
    c = np.zeros((P, NCONST), np.float32)
    c[:, C_ID:C_ID + P] = np.eye(P)
    c[:, C_ONES:C_ONES + P] = 1.0
    for h in range(2):
        s = slice(h * HD, (h + 1) * HD)
        c[s, C_BLK + h * HD:C_BLK + (h + 1) * HD] = 1.0
        for i in range(ROT // 2):
            c[h * HD + ROT // 2 + i, C_ROT + h * HD + i] = -1.0
            c[h * HD + i, C_ROT + h * HD + ROT // 2 + i] = 1.0
    for first in range(2):
        m = np.zeros((P, 192), np.float32)
        m[:CHUNK, 2 * CHUNK:] = NEG
        m[CHUNK:, :CHUNK] = NEG
        if first:
            m[:, :CHUNK] = NEG
        c[:, C_MASK + 192 * first:C_MASK + 192 * (first + 1)] = m
    s, t = np.arange(P)[:, None], np.arange(P)[None, :]
    for n, w in enumerate(LEVELS):
        if w == 0:
            m = s == t
        else:
            m = (s // (2 * w) == t // (2 * w)) & (s % (2 * w) < w) & (t % (2 * w) >= w)
        c[:, C_LEV + P * n:C_LEV + P * (n + 1)] = m
    freq = np.float32(THETA) ** (-np.arange(0, ROT, 2, dtype=np.float32) / np.float32(ROT))
    for h in range(2):
        c[h * HD:h * HD + ROT, C_FREQ] = np.concatenate([freq, freq])
    return c



class Steps:

    def __init__(self, eng, sem, rnd, size):
        self.eng, self.sem, self.base, self.size, self.n = eng, sem, rnd * size, size, 0

    def __call__(self, ins):
        self.n += 1
        ins.then_inc(self.sem, 1)
        self.eng.wait_ge(self.sem, self.base + self.n)

    def end(self):
        assert self.n == self.size, (self.sem, self.n, self.size)


def apart(eng, sem):
    eng.wait_ge(sem, 1)


def taken_before(l, o, par):
    return 1 + l * O_LAYER + o - par


def taken(l, o, par, half):
    return taken_before(l, o, par) + half + 1


def used(l, w, n):
    return 8 * (l * W_LAYER + w) + n


def use(l, b):
    return B_PRO + l * B_LAYER + b


def qk_sum_use(i):
    return B_QK + 2 + 2 * max(2 * i - 1, 0)


def qk_rotate_use(i):
    return B_QK + 2 + 2 * min(2 * i + 2, 9)


def head_use(t):
    return B_HEAD + 2 + HEAD_USES * t


def token_major_use(t):
    return B_HEAD + HEAD_USES * t


def summed(r, n):
    return r * (2 * KT + 1) + n + 1


def halves(t, c):
    return t.rearrange("p (b two c) -> p b two c", two=2, c=c)


def build(nc, A, out):
    R1 = 16512
    R2 = R1 + 32768
    R3 = R2 + 65536
    R4 = R3 + 65536

    def at(name, off, shape, dt=F32):
        return nc.alloc_sbuf_tensor_at(name, [P] + list(shape), dt, offset=off)

    XT = at("x_t", R1, [KT, SEQ])
    MG = at("merged", R1, [KT, SEQ])
    KF = at("k_feat", R1, [P + SEQ])
    VT = at("v_tok", R1 + 4608, [NB + 1, P])
    CUM = at("cum", R1 + 9216, [SEQ])
    QS = at("hg_q", R1 + 13312, [SEQ])
    KK = at("hg_k", R1 + 17408, [SEQ])
    IT = at("hg_i_tok", R1 + 21504, [NB, P])
    TMP = at("evac", R1 + 25600, [SEQ])
    STATE = at("state", R1 + 29696, [5, P])
    EL = at("exp_last", R1 + 32256, [SEQ // CHUNK])
    HH = at("h_hi", R2, [KT, SEQ], F32R)
    HL = at("h_lo", R2 + 32768, [KT, SEQ], F32R)
    XIN = at("x_in", R2, [NB, D])
    AH = at("a_hi", R3, [4, SEQ], F32R)
    AL = at("a_lo", R3 + 16384, [4, SEQ], F32R)
    GH = at("g_hi", R3 + 32768, [4, SEQ], F32R)
    GL = at("g_lo", R3 + 49152, [4, SEQ], F32R)
    QF = at("q_feat", R3, [4, SEQ])
    OF = at("o_feat", R3 + 32768, [4, SEQ])
    GATE = at("gate", R3 + 49152, [4, SEQ])
    QR = [at(f"qk_raw{i}", R3 + x, [SEQ]) for i, x in enumerate((32768, 45056))]
    SQ = [at(f"qk_sq{i}", R3 + x, [SEQ]) for i, x in enumerate((36864, 61440))]
    T2 = at("qk_rotated", R3 + 40960, [SEQ])
    QKR = at("qk_rs", R3 + 28672, [SEQ])
    ROPE = at("rope", R3 + 53248, [2, SEQ])
    NSQ = at("norm_sq", R3 + 32768, [4, HALF])
    NACC = at("norm_sum", R3 + 40960, [SEQ])
    NRS = at("norm_rs", R3 + 45056, [SEQ])
    NHF = at("norm_h", R3 + 49152, [2, HALF])
    ANG = [at(f"ang{i}", R3 + 4096 * i, [SEQ]) for i in range(5)]
    POSI = at("pos_i", R3 + 20480, [SEQ], I32)
    PROW = at("par_rows", R3 + 24576, [2, P])
    LEVF = at("level_f", R3 + 28672, [896])
    OUTB = at("out_rows", R3, [NB, D])
    UH = at("u_hi", R3, [2, 2, SEQ], F32R)
    UL = at("u_lo", R3 + 16384, [2, 2, SEQ], F32R)
    CB = at("conv_in", R3 + 32768, [2, SEQ + 2])
    CO = at("conv_out", R3 + 41088, [2, SEQ])
    UF = at("u_f", R3 + 49280, [2, SEQ])
    r = R4

    def more(name, shape, size, dt=F32):
        nonlocal r
        r += size
        return at(name, r - size, shape, dt)

    RAW = more("w_raw", [2, SEQ], 8192)
    WH = more("w_hi", [2, SEQ], 8192, F32R)
    WL = more("w_lo", [2, SEQ], 8192, F32R)
    CONST = more("consts", [C_LEV], 3616)
    LEVM = more("level_masks", [7, P], 896, U8)
    PARA = more("par_all", [DEPTH, NPAR], 992)
    PAR = more("par", [NPAR], 512)
    SA = at("sig", r, [2, SEQ])
    E = more("decay", [3, HALF], 6144)
    ST = more("s_t", [4, P], 2048)
    QE = more("q_decayed", [HALF], 2048)
    KE = more("k_decayed", [HALF], 2048)
    QB = more("q_block", [2, P], 1024)
    PR = more("probs", [2, 2 * P], 2048)
    PT = more("probs_t", [4, P], 2048)
    GA = [at(f"gates_{i}", x, [1, SEQ]) for i, x in enumerate((R1, R1 + 4096, R1 + 25600, r - 4096))]
    STAT = more("stats", [16], 64)
    SMALL = more("small", [32], 128)
    assert r <= 229344, r

    IDENT, ONES = CONST[:, C_ID:C_ID + P], CONST[:, C_ONES:C_ONES + P]
    FREQ = CONST[:, C_FREQ:C_FREQ + 1]
    BLK, ROTM = CONST[:, C_BLK:C_BLK + P], CONST[:, C_ROT:C_ROT + P]

    G = [nc.alloc_psum_tensor(f"gemm{i}", [P, 512], F32) for i in range(4)]
    SC = nc.alloc_psum_tensor("scores", [P, 512], F32)
    PX = nc.alloc_psum_tensor("probs_x", [P, 512], F32)
    SM = [nc.alloc_psum_tensor(f"small_ps{i}", [P, 512], F32) for i in range(2)]

    XS = nc.dram_tensor("x_spill", [P, KT, SEQ], F32, kind="Internal")
    RS = nc.dram_tensor("rope_spill", [P, 2, SEQ], F32, kind="Internal")

    sem = nc.alloc_semaphore
    s_const = sem("constants_loaded")
    s_params = sem("params_loaded")
    s_xin = [sem(f"x_loaded{i}") for i in range(2)]
    s_raw = [sem(f"weights_loaded{i}") for i in range(2)]
    s_rawfree = sem("raw_slot_free")
    s_whi = sem("weights_hi")
    s_split = sem("weights_split")
    s_gemm = sem("gemm_progress")
    s_taken = [sem(f"gemm_taken{i}") for i in range(2)]
    s_sw = sem("small_written")
    s_sr = sem("small_read")
    s_rope = sem("rope_saved")
    s_rl = sem("rope_loaded")
    s_sp = sem("x_spilled")
    s_xb = [sem(f"x_back{i}") for i in range(2)]
    s_sq = sem("norm_squares")
    s_acc = sem("norm_sum")
    s_sd = sem("norm_rs")
    s_h = sem("norm_h")
    s_hhi = sem("norm_h_hi")
    s_hlo = sem("norm_h_lo")
    s_qkq = sem("qk_squares")
    s_qks = sem("qk_rs")
    s_qkn = sem("qk_normed")
    s_qkd = sem("qk_done")
    s_ang = sem("angles")
    s_sin = sem("sines")
    s_lbx = sem("lb_exp")
    s_qb = sem("q_block_ready")
    s_as = sem("att_scores")
    s_am = sem("att_shift")
    s_ae = sem("att_exp")
    s_ap = sem("att_probs")
    s_at = sem("att_probs_t")
    s_ac = sem("att_probs_t_copied")
    s_ao = sem("att_out")
    s_ad = sem("att_done")
    s_rows = sem("hg_upper_rows")
    s_fs = sem("hg_f_sigmoid")
    s_clamp = sem("hg_f_clamped")
    s_ln = sem("hg_ln")
    s_cum = sem("hg_cum")
    s_el = sem("hg_exp_last")
    s_sub = sem("hg_exponent")
    s_exp = sem("hg_exp")
    s_fac = sem("hg_factor")
    s_qe = sem("hg_q_decayed")
    s_ket = sem("hg_k_tok")
    s_state = sem("hg_state")
    s_stu = sem("hg_state_used")
    s_osq = sem("hg_o_sq")
    s_osd = sem("hg_o_rs")
    s_hgd = sem("hg_done")
    s_mg = sem("merged_ready")
    s_mh = sem("merged_hi")
    s_ml = sem("merged_lo")
    s_co = sem("conv_ready")
    s_si = sem("silu_ready")
    s_uhi = sem("u_hi_ready")
    s_ulo = sem("u_lo_ready")
    s_x = sem("x_ready")
    s_out = sem("stored")
    d_init, d_qk, d_rope, d_att, d_split, d_hgn, d_prep, d_ffn, d_sink, d_par, d_z = (
        sem(f"dve_{n}") for n in ("init", "qk_newton", "rope", "att", "att_split", "hg_norm", "prep",
                                  "ffn", "sink", "par", "zero"))

    block = nc.Block()
    block.__enter__()

    @block.sync
    def _(sp):
        sp.dma_start(CONST[:, :], A["consts"][:, 0:C_LEV]).then_inc(s_const, 16)
        sp.dma_start(LEVF[:, :], A["consts"][:, C_LEV:C_LEV + 896]).then_inc(s_const, 16)
        sp.dma_start(POSI[:, :], A["positions"].to_broadcast([P, SEQ])).then_inc(s_const, 16)
        for l in range(DEPTH):
            for name, row, k in (("norm1_g", PG1, KT), ("norm2_g", PG2, KT), ("hg_norm_g", PHG, 1),
                                 ("lb_logits", PLB, NH), ("conv_b", PCB, FT)):
                sp.dma_start(PROW[row:row + k, l, :],
                             A[name][l].rearrange("(k c) -> k c", c=P)).then_inc(s_params, 16)
            for name, row in (("q_norm_g", PQG), ("k_norm_g", PKG)):
                for h in range(2):
                    sp.dma_start(PROW[row:row + 1, l, h * HD:(h + 1) * HD],
                                 A[name][l:l + 1, :]).then_inc(s_params, 16)
            sp.dma_start(PROW[PCW:PCW + 3 * FT, l, :],
                         A["conv_w"][l].rearrange("j (k c) -> (j k) c", c=P)).then_inc(s_params, 16)
            sp.dma_start(PARA[:, l, PSINK:PSINK + NQ],
                         A["sinks"][l:l + 1, :].to_broadcast([P, NQ])).then_inc(s_params, 16)
        x_rows = A["x"][0].rearrange("(b p) d -> p b d", p=P)
        for b in range(2):
            sp.dma_start(XIN[:, 4 * b:4 * b + 4, :], x_rows[:, 4 * b:4 * b + 4, :]).then_inc(s_xin[b], 16)

        def load(l, w, slot, parts, waited=False):
            assert len(parts) == 3
            if not waited:
                apart(sp, s_mg)
                sp.wait_ge(s_rawfree, l * W_LAYER + w + 1)
            for dst, src in parts:
                sp.dma_start(dst, src).then_inc(s_raw[slot], 16)

        def columns(l, w, slot, name, col):
            dst = RAW[:, slot, :].rearrange("p (k c) -> p k c", k=KT)
            src = A[name][l].rearrange("(k p) n -> p k n", p=P)
            load(l, w, slot, [(dst[:, a:b, :], src[:, a:b, ds(col, P)]) for a, b in ((0, 3), (3, 6), (6, 8))])

        with sp.Fori(0, DEPTH) as l:
            columns(l, 0, 0, "w_in", COL_V)
            columns(l, 1, 1, "w_in", COL_K)
            sp.wait_ge(s_x, (l + 1) * KT)
            for k in (slice(0, 4), slice(4, 8)):
                sp.dma_start(XS[:, k, :], XT[:, k, :]).then_inc(s_sp, 16)
            sp.wait_ge(s_rope, 16)
            sp.wait_ge(s_rawfree, l * W_LAYER + 3)
            sp.dma_start(ROPE[:, :, :], RS[:, :, :]).then_inc(s_rl, 16)
            for t in range(PAIRS):
                w = 2 + t
                dst = RAW[:, w % 2, :].rearrange("p (k c) -> p k c", k=KT)
                src = A["w_in"][l].rearrange("(k p) n -> p k n", p=P)
                c0, c1 = t * HD, (t + PAIRS) * HD
                load(l, w, w % 2, [(dst[:, :, 0:HD], src[:, :, c0:c0 + HD]),
                            (dst[:, 0:4, HD:P], src[:, 0:4, c1:c1 + HD]),
                            (dst[:, 4:8, HD:P], src[:, 4:8, c1:c1 + HD])], waited=(t == 0))
            with sp.Fori(0, NH) as t:
                for i, col in enumerate((COL_HG, COL_HI, COL_HF, COL_HQ)):
                    columns(l, W_HEAD + 4 * t + i, i % 2, "w_in", t * P + col)

            def branches(w, slot, j):
                dst = RAW[:, slot, :].rearrange("p (k c) -> p k c", k=KT)
                wa = A["w_branch_a"][l].rearrange("(g t p) n -> g p t n", g=2, t=PAIRS)
                wb = A["w_branch_b"][l].rearrange("(k p) n -> p k n", p=P)
                load(l, w, slot, [(dst[0:HD, 0:4, :], wa[0][:, :, ds(j * P, P)]),
                                  (dst[HD:P, 0:4, :], wa[1][:, :, ds(j * P, P)]),
                                  (dst[:, 4:8, :], wb[:, :, ds(j * P, P)])])

            for j in range(2):
                columns(l, W_MERGE + 2 * j, 0, "w_in", j * P + COL_GA)
                columns(l, W_MERGE + 2 * j + 1, 1, "w_in", j * P + COL_GB)
            for j in range(2):
                branches(W_MERGE + 4 + j, j, j)
            with sp.Fori(1, KT // 2) as jj:
                for h in range(2):
                    w = 6 * jj + (W_MERGE + 3 * h)
                    j = 2 * jj + h
                    columns(l, w, (3 * h) % 2, "w_in", j * P + COL_GA)
                    columns(l, w + 1, (3 * h + 1) % 2, "w_in", j * P + COL_GB)
                    branches(w + 2, (3 * h + 2) % 2, j)
            for h in range(2):
                columns(l, W_OUT + h, h, "w_out", h * P)
            for i, n in enumerate((2 * KT - 2, 2 * KT)):
                sp.wait_ge(s_ml, l * 2 * KT + n)
                k = slice(4 * i, 4 * i + 4)
                sp.dma_start(XT[:, k, :], XS[:, k, :]).then_inc(s_xb[i], 16)
            with sp.Fori(1, KT // 2) as jj:
                for h in range(2):
                    columns(l, 2 * jj + (W_OUT + h), h, "w_out", (2 * jj + h) * P)

            def up(g, w):
                for i in range(2):
                    columns(l, w + 2 * i, 0, "w_up", (2 * g + i) * P)
                    columns(l, w + 2 * i + 1, 1, "w_up", (2 * g + i) * P + DFF)

            def down(g, w):
                for h in range(2):
                    dst = RAW[:, h, :].rearrange("p (k n) -> p k n", k=2)
                    src = A["w_down"][l].rearrange("(k p) n -> p k n", p=P)
                    c = h * HALF
                    load(l, w + h, h, [(dst[:, 0:1, :], src[:, ds(2 * g, 1), c:c + HALF]),
                                    (dst[:, 1:2, 0:256], src[:, ds(2 * g + 1, 1), c:c + 256]),
                                    (dst[:, 1:2, 256:HALF], src[:, ds(2 * g + 1, 1), c + 256:c + HALF])])

            up(0, W_FFN)
            with sp.Fori(0, HIDDEN_GROUPS // 2) as p:
                w = 12 * p + (W_FFN + 4)
                up(2 * p + 1, w)
                down(2 * p, w + 4)
                up(2 * p + 2, w + 6)
                down(2 * p + 1, w + 10)
            down(HIDDEN_GROUPS - 1, W_LAYER - 2)
        out_rows = out[0].rearrange("(b p) d -> b p d", p=P)
        for b in range(NB):
            sp.wait_ge(s_sr, use(DEPTH, 2 * b + 1) + 1)
            sp.dma_start(out_rows[b], OUTB[:, b, :]).then_inc(s_out, 16)
        sp.wait_ge(s_out, 16 * NB)
        sp.wait_ge(s_sp, 32 * DEPTH)
        sp.wait_ge(s_rope, 16)

    @block.gpsimd
    def _(pool):
        pool.memset(SMALL[:, 0:1], 0.0).then_inc(s_rawfree, 1)
        pool.memset(SMALL[:, 1:2], 0.0).then_inc(s_rawfree, 1)

        def split(w, slot):
            pool.wait_ge(s_raw[slot], 24 * (w - slot) + 48)
            pool.tensor_tensor(WH[:, slot, :], RAW[:, slot, :], ONES[:, 0:1].to_broadcast([P, SEQ]),
                               ALU.mult).then_inc(s_whi, 1)
            pool.wait_ge(s_whi, w + 1)
            pool.tensor_tensor(WL[:, slot, :], RAW[:, slot, :], WH[:, slot, :].bitcast(F32),
                               ALU.subtract).then_inc(s_split, 1)
            pool.wait_ge(s_split, w + 1)
            pool.tensor_tensor(SMALL[:, 2:3], SMALL[:, 0:1], SMALL[:, 1:2], ALU.add).then_inc(s_rawfree, 1)

        pool.wait_ge(s_const, CONST_LOADS)
        split(0, 0)
        split(1, 1)
        with pool.Fori(1, DEPTH * W_LAYER // 2) as u:
            for s in range(2):
                pool.wait_ge(s_gemm, 16 * u + 8 * (s - 1))
                split(2 * u + s, s)

    @block.tensor
    def _(pe):
        pe.wait_ge(s_const, CONST_LOADS)
        pe.wait_ge(s_params, PARAM_LOADS)
        for b in range(B_PRO):
            if b >= 2:
                pe.wait_ge(s_sr, max(b - 1, 2))
            bank = SM[b % 2]
            if b < 2:
                mm = pe.transpose(bank[:, 0:NROW], PROW[0:NROW, b, :], IDENT[0:NROW, 0:NROW])
            else:
                j, half = (b - 2) % KT, (b - 2) // KT
                if j == 0:
                    pe.wait_ge(s_xin[half], 16)
                for i in range(4):
                    mm = pe.transpose(bank[:, i * P:(i + 1) * P],
                                      XIN[:, 4 * half + i, j * P:(j + 1) * P], IDENT)
            mm.then_inc(s_sw, 1)

        def small(l, b, par):
            pe.wait_ge(s_sr, use(l, b) - 1)
            return SM[par]

        def passes(slot, xh, xl, half, weights, dst, marks, part=None, ready=None):
            steps = [(a, x, k) for k in range(len(weights))
                     for a, x in ((WH, xh), (WH, xl), (WL, xh))]
            total = len(steps)
            lo, hi = (0, total) if part is None else (part * total // 2, (part + 1) * total // 2)
            for n in range(lo, hi):
                a, x, k = steps[n]
                if ready is not None and n % 3 == 0:
                    pe.wait_ge(ready[0], ready[1][k])
                mm = pe.matmul(dst, a[:, slot, weights[k]], x(k, half), start=(n == 0),
                               stop=(n == total - 1))
                if (n + 1) * marks % total == 0:
                    mm.then_inc(s_gemm, 1)

        def moving(t):
            return lambda k, half: t[:, k, half * HALF:(half + 1) * HALF]

        whole = [slice(k * P, (k + 1) * P) for k in range(KT)]

        def tile(l, w, slot, o, par, half, part=None, marks=4, ready=None):
            if part in (None, 0) and half == 0:
                pe.wait_ge(s_split, l * W_LAYER + w + 1)
                pe.wait_ge(s_taken[par], taken_before(l, o, par))
            passes(slot, moving(HH), moving(HL), half, whole, G[2 * par + half][:, :],
                   marks, part, ready)

        def first_tiles(l, norm, w, o):
            for half in range(2):
                h_ready = (s_hlo, [(2 * l + norm) * 2 * KT + KT * half + (k + 1) for k in range(KT)])
                for i in range(2):
                    marks = (2, 2) if half == 0 else (4, 8)
                    tile(l, w + i, i, o + i, i, half, marks=marks[i], ready=h_ready if i == 0 else None)

        def norm_sum(l, n, b):
            for half in range(2):
                pe.wait_ge(s_acc, summed(2 * l + n, 2 * KT - 1 + half))
                bank = small(l, b + half, half)
                pe.matmul(bank[:, :], ONES, NACC[:, half * HALF:(half + 1) * HALF],
                          start=True, stop=True).then_inc(s_sw, 1)

        def qk_sum(l, i):
            for half in range(2):
                bank = small(l, qk_sum_use(i) + half, half)
                pe.wait_ge(s_qkq, l * 10 + 2 * i + half + 1)
                pe.matmul(bank[:, :], BLK, SQ[i % 2][:, half * HALF:(half + 1) * HALF],
                          start=True, stop=True).then_inc(s_sw, 1)

        def qk_rotate(l, i):
            pe.wait_ge(s_qkn, l * 5 + i + 1)
            for half in range(2):
                bank = small(l, qk_rotate_use(i) + half, half)
                pe.matmul(bank[:, :], ROTM, QR[i % 2][:, half * HALF:(half + 1) * HALF],
                          start=True, stop=True).then_inc(s_sw, 1)

        def to_token_major(l, b, src):
            for half in range(2):
                bank = small(l, b + half, half)
                for i in range(4):
                    c = (4 * half + i) * P
                    mm = pe.transpose(bank[:, i * P:(i + 1) * P], src[:, c:c + P], IDENT)
                mm.then_inc(s_sw, 1)

        def att_scores(l, t, m):
            pe.wait_ge(s_qb, (4 * l + t) * 8 + m + 1)
            for h in range(2):
                mm = pe.matmul(SC[:, h * 192:(h + 1) * 192], QB[:, h, :],
                               KF[:, m * P + CHUNK:(m + 2) * P], start=True, stop=True)
            mm.then_inc(s_as, 1)

        def att_transpose(l, t, m):
            pe.wait_ge(s_ap, (4 * l + t) * 8 + m + 1)
            for n in range(4):
                mm = pe.transpose(PX[:, n * P:(n + 1) * P], PR[:, n // 2, (n % 2) * P:(n % 2 + 1) * P],
                                  IDENT)
            mm.then_inc(s_at, 1)

        def att_values(l, t, m):
            pe.wait_ge(s_ac, (4 * l + t) * 8 + m + 1)
            for h in range(2):
                rows = slice(h * HD, (h + 1) * HD)
                for kb in range(2):
                    mm = pe.matmul(PX[rows, 0:P], VT[:, m + kb, rows], PT[:, 2 * h + kb, :],
                                   start=(kb == 0), stop=(kb == 1))
            mm.then_inc(s_ao, 1)

        def hg_step(l, t, step):
            half, s = step // 8, step % 8
            b = head_use(t) + HG_USES * half
            rnd = 4 * l + t
            tok = half * HALF

            def product(n, lhs, rhs):
                bank = small(l, b + n, n % 2)
                for i in range(4):
                    c = slice(i * P, (i + 1) * P)
                    mm = pe.matmul(bank[:, c], lhs[:, c], rhs[:, c], start=True, stop=True)
                mm.then_inc(s_sw, 1)

            if s == 0:
                pe.wait_ge(s_cum, rnd + 1)
                pe.wait_ge(s_taken[1], taken(l, 4 * t + (O_HEAD + 3), 1, 1))
                product(0, KK[:, tok:tok + HALF], QS[:, tok:tok + HALF])
            if s < 6:
                pe.wait_ge(s_fac, rnd * 12 + 6 * half + s + 1)
                product(s + 1, E[:, s % 3, :], E[:, s % 3, :])
            if s == 5:
                pe.wait_ge(s_ket, rnd * 2 + half + 1)
                bank = small(l, b + 7, 1)
                for i in range(4):
                    mm = pe.transpose(bank[:, i * P:(i + 1) * P], KE[:, i * P:(i + 1) * P], IDENT)
                mm.then_inc(s_sw, 1)
            if s == 6:
                pe.wait_ge(s_sr, use(l, token_major_use(t) + 1) + 1)
                pe.wait_ge(s_sr, use(l, b + 7) + 1)
                for upper in range(2):
                    for q in range(2):
                        if upper == 0:
                            small(l, b + 8 + q, q)
                        else:
                            pe.wait_ge(s_rows, rnd * 4 + 2 * half + q + 1)
                        for i in (upper, upper + 2):
                            c = 4 * q + i
                            rows = slice(upper * CHUNK, (upper + 1) * CHUNK)
                            mm = pe.matmul(SM[q][:, i * P:(i + 1) * P],
                                           KE[rows, (c // 2) * P:(c // 2 + 1) * P],
                                           IT[rows, 4 * half + c // 2, :], start=True, stop=True)
                        mm.then_inc(s_rows if upper == 0 else s_sw, 1)
            if s == 7:
                pe.wait_ge(s_sr, use(l, b + 6) + 1)
                pe.wait_ge(s_qe, rnd * 2 + half + 1)
                bank = small(l, b + 10, 0)
                for c in range(8):
                    cols = slice(c * CHUNK, (c + 1) * CHUNK)
                    if c % 2 == 0:
                        pe.matmul(bank[:, c * CHUNK:(c + 2) * CHUNK], IT[:, 4 * half + c // 2, :],
                                  ST[:, c // 2, :], start=True, stop=False)
                    n = 8 * half + c
                    pe.wait_ge(s_state, rnd * 16 + n + 1)
                    mm = pe.matmul(bank[:, cols], STATE[:, n % 5, :], QE[:, cols], start=False,
                                   stop=(c % 2 == 1))
                    if c < 7:
                        mm.then_inc(s_stu, 1)
                mm.then_inc(s_sw, 1)

        def hg_norm_sum(l, t, half):
            pe.wait_ge(s_osq, (4 * l + t) * 2 + half + 1)
            bank = small(l, head_use(t) + HG_USES * half + 11, 1)
            pe.matmul(bank[:, :], ONES, QE[:, :], start=True, stop=True).then_inc(s_sw, 1)

        def head_round(l, t, fresh, behind):
            for u in range(16):
                if fresh and u % 2 == 0:
                    att_scores(l, t, u // 2)
                for quarter in QUARTERS[u]:
                    i, half, part = quarter // 4, quarter // 2 % 2, quarter % 2
                    tile(l, 4 * t + (W_HEAD + i), i % 2, 4 * t + (O_HEAD + i), i % 2, half, part)
                if fresh:
                    if not behind and u == 1:
                        qk_sum(l, 4)
                    if not behind and u == 8:
                        qk_rotate(l, 4)
                    if not behind and u % 2 == 0 and u > 0:
                        att_values(l, t, u // 2 - 1)
                    if u % 2 == 1:
                        att_transpose(l, t, u // 2)
                if behind:
                    if u == 8:
                        hg_norm_sum(l, t - 1, 0)
                    hg_step(l, t - 1, u)
                if behind and fresh and u % 2 == 1:
                    att_values(l, t, u // 2)
                if not behind and u == 1:
                    qk_rotate(l, 3)
            if not behind:
                att_values(l, t, NB - 1)
            if behind:
                hg_norm_sum(l, t - 1, 1)
            if fresh:
                o = 4 * t + (O_HEAD + 1)
                pe.wait_ge(s_taken[1], taken(l, o, 1, 1))
                to_token_major(l, token_major_use(t), TMP)

        with pe.Fori(0, DEPTH) as l:
            norm_sum(l, 0, B_NORM1)
            first_tiles(l, 0, 0, 0)
            for w in range(2, 6):
                for half in range(2):
                    tile(l, w, w % 2, w, w % 2, half)
                    if w == 2 and half == 0:
                        pe.wait_ge(s_taken[0], taken(l, 0, 0, 1))
                        to_token_major(l, B_QK, TMP)
                    if w >= 2 and half == 0:
                        qk_sum(l, w - 2)
                    if w >= 3 and half == 0:
                        qk_rotate(l, w - 3)
            head_round(l, 0, True, False)
            with pe.Fori(1, NH) as t:
                head_round(l, t, True, True)
            head_round(l, NH, False, True)

            def branches(w, slot, o, first=False):
                pe.wait_ge(s_split, l * W_LAYER + w + 1)
                for i, (xh, xl) in enumerate(((AH, AL), (GH, GL))):
                    if first and i == 0:
                        pe.wait_ge(s_ad, 32 * l + 32)
                    if first and i == 1:
                        pe.wait_ge(s_hgd, 4 * l + 4)
                    pe.wait_ge(s_taken[i], taken_before(l, o + i, i))
                    for half in range(2):
                        passes(slot, moving(xh), moving(xl), half, whole[4 * i:4 * i + 4],
                               G[2 * i + half][:, :], 2)

            for j in range(2):
                branches(W_MERGE + 4 + j, j, O_MERGE + 4 + 2 * j, j == 0)
            with pe.Fori(1, KT // 2) as jj:
                for h in range(2):
                    w, o = 6 * jj + (W_MERGE + 3 * h), 8 * jj + (O_MERGE + 4 * h)
                    for i in range(2):
                        for half in range(2):
                            tile(l, w + i, (3 * h + i) % 2, o + i, i, half)
                    branches(w + 2, (3 * h + 2) % 2, o + 2)
            with pe.Fori(0, KT // 2) as jj:
                for h in range(2):
                    for half in range(2):
                        counts = [MERGED.index((k, half)) + 1 for k in range(KT)]
                        m_ready = (s_ml, [l * 2 * KT + n for n in counts])
                        tile(l, 2 * jj + (W_OUT + h), h, 2 * jj + (O_OUT + h), h, half,
                             ready=m_ready if h == 0 else None)
            norm_sum(l, 1, B_NORM2)

            def up(w, o, first=False):
                if first:
                    first_tiles(l, 1, w, o)
                for i in range(2 if first else 0, 4):
                    for half in range(2):
                        tile(l, w + i, i % 2, o + i, i % 2, half)

            def down(g, w, o, buf):
                pe.wait_ge(s_ulo, (l * HIDDEN_GROUPS + g + 1) * 2)
                for j in range(KT):
                    slot, par = j // 4, j % 2
                    if j % 4 == 0:
                        pe.wait_ge(s_split, l * W_LAYER + w + slot + 1)
                    pe.wait_ge(s_taken[par], taken_before(l, o + j, par))
                    cols = [slice(k * HALF + (j % 4) * P, k * HALF + (j % 4 + 1) * P) for k in range(2)]
                    for half in range(2):
                        passes(slot, moving(UH[:, buf]), moving(UL[:, buf]), half, cols,
                               G[2 * par + half][:, :], 1)

            up(W_FFN, O_FFN, True)
            with pe.Fori(0, HIDDEN_GROUPS // 2) as p:
                w, o = 12 * p + (W_FFN + 4), 24 * p + (O_FFN + 4)
                up(w, o)
                down(2 * p, w + 4, o + 4, 0)
                up(w + 6, o + 12)
                down(2 * p + 1, w + 10, o + 16, 1)
            down(HIDDEN_GROUPS - 1, W_LAYER - 2, O_LAYER - 8, 0)
        for b in range(2 * NB):
            if b == 0:
                pe.wait_ge(s_x, (DEPTH + 1) * KT)
            bank = small(DEPTH, b, b % 2)
            for i in range(4):
                mm = pe.transpose(bank[:, i * P:(i + 1) * P],
                                  XT[:, 4 * (b % 2) + i, (b // 2) * P:(b // 2 + 1) * P], IDENT)
            mm.then_inc(s_sw, 1)

    @block.scalar
    def _(act):
        f = nc.scalar.activation
        act.wait_ge(s_lbx, 1)
        f(SMALL[:, 8:16], SMALL[:, 8:16], ACT.Exp).then_inc(s_lbx, 1)

        def cols(half):
            return slice(half * HALF, (half + 1) * HALF)

        def take_x(half, j):
            b = 2 + half * KT + j
            act.wait_ge(s_sw, b + 1)
            f(XT[:, j, cols(half)], SM[b % 2][:, :], ACT.Copy).then_inc(s_sr, 1)

        for j in range(KT):
            take_x(0, j)
        act.wait_ge(s_ang, 2)
        for i in range(2):
            f(ROPE[:, i, :], ANG[3 + i][:, :], ACT.Sin).then_inc(s_sin, 1)
        act.wait_ge(s_sin, 2)
        act.dma_start(RS[:, :, :], ROPE[:, :, :]).then_inc(s_rope, 16)

        def evac(l, w, o, par, half, dst, func=ACT.Copy, n=None, **kw):
            act.wait_ge(s_gemm, used(l, w, 4 * (half + 1) if n is None else n))
            f(dst, G[2 * par + half][:, :], func, **kw).then_inc(s_taken[par], 1)

        def squares(r, j, parity, first=False):
            for half in range(2):
                if not first:
                    act.wait_ge(s_acc, summed(r, 2 * j + (half - 3)))
                f(NSQ[:, 2 * parity + half:2 * parity + half + 1, :], XT[:, ds(j, 1), cols(half)],
                  ACT.Square).then_inc(s_sq, 1)

        def norm(l, n):
            r0 = 2 * l + n
            for half in range(2):
                act.wait_ge(s_sr, use(l, (B_NORM1, B_NORM2)[n] + half) + 1)
                f(NRS[:, cols(half)], NRS[:, cols(half)], ACT.Ln).then_inc(s_sd, 1)
            for half in range(2):
                act.wait_ge(s_sd, 4 * r0 + 1 + half)
                f(NRS[:, cols(half)], NRS[:, cols(half)], ACT.Exp, scale=-0.5).then_inc(s_sd, 1)
            for i in range(2 * KT):
                act.wait_ge(s_h, r0 * 16 + i + 1)
                f(HH[:, i % KT, cols(i // KT)], NHF[:, i % 2, :], ACT.Copy).then_inc(s_hhi, 1)

        def qk_rsqrt(l, i):
            for half in range(2):
                act.wait_ge(s_sr, use(l, qk_sum_use(i) + half) + 1)
                f(QKR[:, cols(half)], SQ[i % 2][:, cols(half)], ACT.Ln).then_inc(s_qks, 1)
            for half in range(2):
                act.wait_ge(s_qks, 4 * (5 * l + i) + 1 + half)
                f(QKR[:, cols(half)], QKR[:, cols(half)], ACT.Exp, scale=-0.5).then_inc(s_qks, 1)

        def q_block(l, t, m):
            for h in range(2):
                rows = slice(h * HD, (h + 1) * HD)
                ins = f(QB[rows, h:h + 1, :], QF[rows, ds(t, 1), m * P:(m + 1) * P], ACT.Copy)
            ins.then_inc(s_qb, 1)

        def att_exp(l, t, m):
            act.wait_ge(s_am, (4 * l + t) * 8 + m + 1)
            for h in range(2):
                f(PR[:, h, CHUNK:], PR[:, h, CHUNK:], ACT.Exp, bias=STAT[:, 4 + h:5 + h],
                  scale=HD ** -0.5, accum_out=STAT[:, 8 + h:9 + h])
            f(STAT[:, 10:12], STAT[:, 6:8], ACT.Exp).then_inc(s_ae, 1)

        def att_copy(l, t, m):
            act.wait_ge(s_at, (4 * l + t) * 8 + m + 1)
            f(PT[:, :, :], PX[:, :].rearrange("p (n c) -> p n c", n=4), ACT.Copy).then_inc(s_ac, 1)

        def hg_exp(l, t, half, n):
            rnd = (4 * l + t) * 2 + half
            sub = (0, 1, 2, 3, 4, 5, 5, 6)[n]
            act.wait_ge(s_sub, rnd * 7 + sub + 1)
            if n == 6:
                f(QE[:, :], CUM[:, cols(half)], ACT.Exp).then_inc(s_exp, 1)
            else:
                x = KE[:, :] if n == 5 else E[:, (n if n < 5 else 5) % 3, :]
                f(x, x, ACT.Exp).then_inc(s_exp, 1)

        def hg_step(l, t, step):
            half, s = step // 8, step % 8
            for n in {0: (2,), 1: (3,), 2: (4, 5, 6), 3: (7,)}.get(s, ()):
                hg_exp(l, t, half, n)
            if half == 0 and s in (6, 7):
                hg_exp(l, t, 1, s - 6)
            if s == 7:
                act.wait_ge(s_sr, use(l, head_use(t) + HG_USES * half + 10) + 1)
                f(QE[:, :], (OF[:, ds(t, 1), cols(half)]), ACT.Square).then_inc(s_osq, 1)

        def hg_norm(l, t, half, part=None):
            n = (4 * l + t) * 2 + half
            if part in (None, 0):
                act.wait_ge(s_sr, use(l, head_use(t) + HG_USES * half + 11) + 1)
                f(KE[:, :], KE[:, :], ACT.Ln).then_inc(s_osd, 1)
            if part in (None, 1):
                act.wait_ge(s_osd, 2 * n + 1)
                f(KE[:, :], KE[:, :], ACT.Exp, scale=-0.5).then_inc(s_osd, 1)

        def head_round(l, t, fresh, behind, pair_follows=True):
            if fresh and not behind:
                q_block(l, t, 0)
            for u in range(16):
                if not fresh and u in (5, 9, 13):
                    i = u // 4 - 1
                    for half in range(2):
                        evac(l, W_MERGE + i, O_MERGE + i, i % 2, half, GA[i][:, 0, cols(half)], ACT.Sigmoid)
                if fresh and u in (5, 9):
                    i = u // 4 - 1
                    w, o = 4 * t + (W_HEAD + i), 4 * t + (O_HEAD + i)
                    for half in range(2):
                        if i == 0:
                            evac(l, w, o, 0, half, GATE[:, ds(t, 1), cols(half)], ACT.Silu)
                        else:
                            evac(l, w, o, 1, half, TMP[:, cols(half)])
                if fresh and u % 2 == 0:
                    att_exp(l, t, u // 2)
                    if u < 14:
                        q_block(l, t, u // 2 + 1)
                    elif pair_follows:
                        q_block(l, t + 1, 0)
                    if not behind and u == 2:
                        qk_rsqrt(l, 4)
                if fresh and u % 2 == 1:
                    att_copy(l, t, u // 2)
                if behind:
                    if u == 8:
                        hg_norm(l, t - 1, 0)
                    hg_step(l, t - 1, u)
            if behind and not fresh:
                for half in range(2):
                    evac(l, W_MERGE + 3, O_MERGE + 3, 1, half, GA[3][:, 0, cols(half)], ACT.Sigmoid)
                hg_norm(l, t - 1, 1)
            if fresh:
                w, o = 4 * t + (W_HEAD + 2), 4 * t + (O_HEAD + 2)
                for half in range(2):
                    act.wait_ge(s_gemm, used(l, w, 4 * (half + 1)))
                    f(CUM[:, cols(half)], G[half][:, :], ACT.Sigmoid).then_inc(s_fs, 1)
                for half in range(2):
                    evac(l, w, o, 0, half, KK[:, cols(half)], ACT.Sigmoid, scale=-1.0)
                act.wait_ge(s_clamp, 4 * l + t + 1)
                f(CUM[:, :], CUM[:, :], ACT.Ln, bias=LBCUR[:, 0:1], scale=LBCUR[:, 1:2]).then_inc(s_ln, 1)
                if behind:
                    hg_norm(l, t - 1, 1, 0)
                for half in range(2):
                    evac(l, w + 1, o + 1, 1, half, QS[:, cols(half)], ACT.Silu)
                act.wait_ge(s_cum, 4 * l + t + 1)
                f(EL[:, :], CUM[:, CHUNK - 1::CHUNK], ACT.Exp).then_inc(s_el, 1)
                for n in range(2):
                    hg_exp(l, t, 0, n)
                if behind:
                    hg_norm(l, t - 1, 1, 1)

        LBCUR = STAT[:, 14:16]

        for j in range(KT):
            take_x(1, j)
            act.wait_ge(s_sr, 3 + KT + j)
            squares(0, j, j % 2, j < 2)
        with act.Fori(0, DEPTH) as l:
            norm(l, 0)
            act.wait_ge(s_sp, 32 * l + 32)
            for half in range(2):
                evac(l, 0, 0, 0, half, TMP[:, cols(half)], n=PAIRED[0][half])
            for i in range(5):
                w = i + 1
                if i >= 2:
                    act.wait_ge(s_qkd, 5 * l + i - 1)
                for half in range(2):
                    act.wait_ge(s_gemm, used(l, w, PAIRED[1][half] if i == 0 else 4 * (half + 1)))
                    f(SQ[i % 2][:, cols(half)], G[2 * (w % 2) + half][:, :], ACT.Square).then_inc(s_qkq, 1)
                    f(QR[i % 2][:, cols(half)], G[2 * (w % 2) + half][:, :], ACT.Copy).then_inc(s_taken[w % 2], 1)
                if i < 4:
                    qk_rsqrt(l, i)
            act.wait_ge(s_qkd, 5 * l + 2)
            head_round(l, 0, True, False)
            with act.Fori(1, NH - 1) as t:
                head_round(l, t, True, True)
            head_round(l, NH - 1, True, True, False)
            head_round(l, NH, False, True)
            with act.Fori(1, KT // 2) as jj:
                for h in range(2):
                    w, o = 6 * jj + (W_MERGE + 3 * h), 8 * jj + (O_MERGE + 4 * h)
                    act.wait_ge(s_mg, 8 * l + 2 * jj + (h + 1))
                    for i in range(2):
                        for half in range(2):
                            evac(l, w + i, o + i, i, half, SA[:, i, cols(half)], ACT.Sigmoid)
            for j, half in MERGED:
                if half == 0:
                    act.wait_ge(s_mg, 8 * l + j + 2)
                f(HH[:, j, cols(half)], MG[:, j, cols(half)], ACT.Copy).then_inc(s_mh, 1)
            for j in range(KT):
                act.wait_ge(s_taken[j % 2], taken(l, O_OUT + j, j % 2, 1))
                squares(2 * l + 1, j, j % 2, j < 2)
            norm(l, 1)

            def up(g, w, o, buf, first=False):
                n = (l * HIDDEN_GROUPS + g) * 2
                for i in range(2):
                    for half in range(2):
                        n_gemm = PAIRED[0][half] if first and i == 0 else 4 * (half + 1)
                        evac(l, w + 2 * i, o + 2 * i, 0, half, CB[:, i, 2 + half * HALF:2 + (half + 1) * HALF],
                             n=n_gemm)
                    act.wait_ge(s_co, n + i + 1)
                    f(CO[:, i, :], CO[:, i, :], ACT.Silu).then_inc(s_si, 1)
                    act.wait_ge(s_taken[1], taken(l, o + 2 * i + 1, 1, 1))
                    f(UH[:, buf, i, :], UF[:, i, :], ACT.Copy).then_inc(s_uhi, 1)

            up(0, W_FFN, O_FFN, 0, True)
            with act.Fori(0, HIDDEN_GROUPS // 2) as p:
                w, o = 12 * p + (W_FFN + 4), 24 * p + (O_FFN + 4)
                up(2 * p + 1, w, o, 1)
                up(2 * p + 2, w + 6, o + 12, 0)
            for j in range(KT):
                act.wait_ge(s_x, (l + 1) * KT + j + 1)
                squares(2 * l + 2, j, j % 2, j < 2)

    @block.vector
    def _(dve):
        tt, ts_, stt, copy = dve.tensor_tensor, dve.tensor_scalar, dve.scalar_tensor_tensor, dve.tensor_copy

        def cols(half):
            return slice(half * HALF, (half + 1) * HALF)

        for par in range(2):
            dve.memset(SMALL[:, 28 + par:29 + par], 0.0).then_inc(s_taken[par], 1)
        dve.memset(SMALL[:, 30:31], 0.0).then_inc(s_mg, 1)
        init = Steps(dve, d_init, 0, 33)
        init(dve.memset(QB[:, :, :], 0.0))
        dve.wait_ge(s_const, CONST_LOADS)
        init(copy(LEVM[:, :, :], LEVF[:, :].rearrange("p (n c) -> p n c", n=7)))
        two_pi, parts = 2 * np.pi, []
        for _ in range(4):
            m, e = np.frexp(two_pi)
            parts.append(float(np.ldexp(np.floor(m * 2048) / 2048, e)))
            two_pi -= parts[-1]
        magic = 1.5 * 2 ** 23
        pos, ang, turns = ANG[0], ANG[1], ANG[2]
        init(copy(pos[:, :], POSI[:, :]))
        init(ts_(ang[:, :], pos[:, :], FREQ, None, ALU.mult))

        def reduce_angle(i):
            red, quarter = ANG[3 + i], (0.25, 0.0)[i]
            init(ts_(turns[:, :], ang[:, :], float(1 / (2 * np.pi)), quarter, ALU.mult, ALU.add))
            init(ts_(turns[:, :], turns[:, :], magic, None, ALU.add))
            init(ts_(turns[:, :], turns[:, :], -magic, None, ALU.add))
            src = ang
            for c in parts:
                init(stt(red[:, :], turns[:, :], -c, src[:, :], ALU.mult, ALU.add))
                src = red
            init(ts_(red[:, :], red[:, :], quarter * 2 * np.pi, 3.1415925, ALU.add, ALU.min))
            ts_(red[:, :], red[:, :], -3.1415925, None, ALU.max).then_inc(s_ang, 1)

        reduce_angle(0)
        for b in range(2):
            dve.wait_ge(s_sw, b + 1)
            copy(PARA[:, b, 0:NROW], SM[b][:, 0:NROW]).then_inc(s_sr, 1)
        assert DEPTH == 2
        lbs = [PARA[:, l, PLB:PLB + NH] for l in range(DEPTH)]
        dve.wait_ge(s_sr, 2)
        init(tt(SMALL[:, 4:8], lbs[0], lbs[1], ALU.max))
        for l in range(DEPTH):
            init(tt(SMALL[:, 8 + 4 * l:12 + 4 * l], lbs[l], SMALL[:, 4:8], ALU.subtract))
        init(tt(SMALL[:, 4:8], SMALL[:, 4:8], SMALL[:, 4:8], ALU.subtract))
        dve.memset(SMALL[:, 31:32], 0.0).then_inc(s_lbx, 1)
        reduce_angle(1)
        dve.wait_ge(s_lbx, 2)
        e0, e1 = SMALL[:, 8:12], SMALL[:, 12:16]
        init(tt(SMALL[:, 16:20], e0, e1, ALU.add))
        init(dve.reciprocal(SMALL[:, 20:24], SMALL[:, 16:20]))
        init(tt(e0, e0, SMALL[:, 20:24], ALU.mult))
        init(tt(e1, e1, SMALL[:, 20:24], ALU.mult))
        init(tt(lbs[0], e0, e0, ALU.subtract))
        init(tt(SMALL[:, 16:20], e0, e1, ALU.add))
        init(tt(lbs[1], SMALL[:, 16:20], e0, ALU.subtract))
        for l in range(DEPTH):
            init(ts_(PARA[:, l, POML:POML + NH], lbs[l], -1.0, 1.0, ALU.mult, ALU.add))

        def add_squares(r, j, parity):
            for half in range(2):
                dve.wait_ge(s_sq, r * 2 * KT + 2 * j + (half + 1))
                dve.wait_ge(s_acc, summed(r, 2 * j + half))
                acc = NACC[:, cols(half)]
                tt(acc, acc, NSQ[:, 2 * parity + half, :], ALU.add).then_inc(s_acc, 1)

        dve.memset(NACC[:, :], 0.0).then_inc(s_acc, 1)
        for j in range(KT):
            dve.wait_ge(s_sr, 3 + KT + j)
            if j > 0:
                dve.wait_ge(s_x, j)
            dve.memset(SMALL[:, 31:32], 0.0).then_inc(s_x, 1)
            if j > 0:
                add_squares(0, j - 1, (j - 1) % 2)
        add_squares(0, KT - 1, 1)
        init.end()

        def written(l, b):
            dve.wait_ge(s_sw, use(l, b) + 1)

        def norm(l, n, b, gain):
            r0 = 2 * l + n
            for half in range(2):
                written(l, b + half)
                rs = NRS[:, cols(half)]
                ts_(rs, SM[half][:, :], 1.0 / D, EPS, ALU.mult, ALU.add).then_inc(s_sr, 1)
            for half in range(2):
                rs = NRS[:, cols(half)]
                dve.wait_ge(s_sd, 4 * r0 + 3 + half)
                for j in range(KT + 1):
                    i = half * KT + j
                    if j < KT:
                        if i >= 2:
                            dve.wait_ge(s_hlo, r0 * 16 + i - 1)
                        stt(NHF[:, i % 2, :], XT[:, j, cols(half)], PAR[:, gain + j:gain + j + 1], rs,
                            ALU.mult, ALU.mult).then_inc(s_h, 1)
                    if j > 0:
                        dve.wait_ge(s_hhi, r0 * 16 + i)
                        tt(HL[:, j - 1, cols(half)], NHF[:, (i - 1) % 2, :],
                           HH[:, j - 1, cols(half)].bitcast(F32), ALU.subtract).then_inc(s_hlo, 1)

        def qk_variance(l, i):
            var = SQ[i % 2]
            for half in range(2):
                written(l, qk_sum_use(i) + half)
                ts_(var[:, cols(half)], SM[half][:, :], 1.0 / HD, EPS, ALU.mult, ALU.add).then_inc(s_sr, 1)

        def qk_newton(l, i):
            st = Steps(dve, d_qk, 5 * l + i, 3)
            var = SQ[i % 2]
            dve.wait_ge(s_qks, 2 * (10 * l + 2 * i + 2))
            rs = QKR[:, :]
            st(stt(var[:, :], var[:, :], -0.5, rs, ALU.mult, ALU.mult))
            st(tt(var[:, :], var[:, :], rs, ALU.mult))
            st(stt(var[:, :], var[:, :], 1.5, rs, ALU.add, ALU.mult))

        def qk_norm(l, i):
            gain = PAR[:, PKG:PKG + 1] if i == 0 else PAR[:, PQG:PQG + 1]
            raw, var = QR[i % 2], SQ[i % 2]
            dve.wait_ge(s_taken[(i + 1) % 2], taken(l, i + 1, (i + 1) % 2, 1))
            stt(raw[:, :], raw[:, :], gain, var[:, :], ALU.mult, ALU.mult).then_inc(s_qkn, 1)

        def qk_rope(l, i):
            st = Steps(dve, d_rope, 5 * l + i, 1)
            raw = QR[i % 2]
            b = qk_rotate_use(i)
            for half in range(2):
                written(l, b + half)
                tt(T2[:, cols(half)], SM[half][:, :], ROPE[:, 1, cols(half)], ALU.mult).then_inc(s_sr, 1)
            dve.wait_ge(s_sr, use(l, b + 2))
            st(tt(raw[:, :], raw[:, :], ROPE[:, 0, :], ALU.mult))
            dst = KF[:, P:] if i == 0 else QF[:, i - 1, :]
            tt(dst, raw[:, :], T2[:, :], ALU.add).then_inc(s_qkd, 1)

        def att_shift(l, t, m):
            a = (4 * l + t) * 8 + m
            st = Steps(dve, d_att, a, 6)
            dve.wait_ge(s_as, a + 1)
            mask = CONST[:, C_MASK + 192 * (m == 0):C_MASK + 192 * (m == 0) + 192]
            scores = PR[:, :, CHUNK:]
            st(tt(scores, SC[:, 0:384].rearrange("p (h k) -> p h k", h=2),
                  mask.rearrange("p (o k) -> p o k", o=1).to_broadcast([P, 2, 192]), ALU.add))
            st(dve.tensor_reduce(STAT[:, 0:2], scores, AX.X, ALU.max))
            sink = SINKT[:, 0:2]
            st(stt(STAT[:, 2:4], STAT[:, 0:2], HD ** -0.5, sink, ALU.mult, ALU.max))
            st(tt(STAT[:, 6:8], sink, STAT[:, 2:4], ALU.subtract))
            ts_(STAT[:, 4:6], STAT[:, 2:4], -1.0, None, ALU.mult).then_inc(s_am, 1)
            return st

        def att_probs(l, t, m, st):
            a = (4 * l + t) * 8 + m
            dve.wait_ge(s_ae, a + 1)
            st(tt(STAT[:, 8:10], STAT[:, 8:10], STAT[:, 10:12], ALU.add))
            st(dve.reciprocal(STAT[:, 12:14], STAT[:, 8:10]))
            tt(PR[:, :, CHUNK:], PR[:, :, CHUNK:],
               STAT[:, 12:14].rearrange("p (h o) -> p h o", o=1).to_broadcast([P, 2, 192]),
               ALU.mult).then_inc(s_ap, 1)
            st.end()

        def att_split(l, t, m):
            a = (4 * l + t) * 8 + m
            dve.wait_ge(s_ao, a + 1)
            blk = slice(m * P, (m + 1) * P)
            st = Steps(dve, d_split, a, 1)
            st(ts_(AH[:, ds(t, 1), blk], PX[:, 0:P].rearrange("p (o c) -> p o c", o=1), 1.0, None, ALU.mult))
            tt(AL[:, ds(t, 1), blk], PX[:, 0:P].rearrange("p (o c) -> p o c", o=1),
               AH[:, ds(t, 1), blk].bitcast(F32), ALU.subtract).then_inc(s_ad, 1)

        def exponent(l, t, half, n):
            c = LEVELS[n + 1]
            cum, e = halves(CUM[:, cols(half)], c), halves(E[:, n % 3, :], c)
            meet = cum[:, :, 0, c - 1:c].to_broadcast([P, HALF // (2 * c), c])
            tt(e[:, :, 0, :], meet, cum[:, :, 0, :], ALU.subtract)
            tt(e[:, :, 1, :], cum[:, :, 1, :], meet, ALU.subtract).then_inc(s_sub, 1)

        def factor(l, t, half, n):
            rnd = (4 * l + t) * 2 + half
            c = LEVELS[n + 1]
            dve.wait_ge(s_exp, rnd * 8 + (n if n < 5 else 7) + 1)
            e = halves(E[:, n % 3, :], c)
            for two, x in enumerate((KK, QS)):
                ins = tt(e[:, :, two, :], e[:, :, two, :], halves(x[:, cols(half)], c)[:, :, two, :], ALU.mult)
            ins.then_inc(s_fac, 1)

        def states(l, t, half, lo, hi):
            rnd = 4 * l + t
            for m in range(lo, hi + 1):
                n = 8 * half + m
                bank, col = SM[(m - 1) // 4], ((m - 1) % 4) * P
                if m >= 5:
                    dve.wait_ge(s_stu, rnd * 14 + 7 * half + m - 4)
                last = m % 4 == 0
                if n < 16:
                    dve.wait_ge(s_state, rnd * 16 + n)
                    ins = stt(STATE[:, n % 5, :], STATE[:, (n - 1) % 5, :], EL[:, n - 1:n],
                              bank[:, col:col + P], ALU.mult, ALU.add)
                    ins.then_inc(s_state, 1)
                if last:
                    if n < 16:
                        dve.wait_ge(s_state, rnd * 16 + n + 1)
                    else:
                        dve.wait_ge(s_state, rnd * 16 + n)
                    dve.memset(SMALL[:, 31:32], 0.0).then_inc(s_sr, 1)

        def hg_step(l, t, step):
            half, s = step // 8, step % 8
            rnd = 4 * l + t
            b = head_use(t) + HG_USES * half
            bank3 = lambda i: SM[i][:, :].rearrange("p (n c) -> p n c", n=4)
            mask = lambda n: LEVM[:, n:n + 1, :].to_broadcast([P, 4, P])
            if s < 5:
                factor(l, t, half, s + 1)
            if s < 4:
                exponent(l, t, half, s + 2) if s != 3 else None
            if s == 2:
                c3 = lambda x: x.rearrange("p (n c) -> p n c", c=CHUNK)
                cum = c3(CUM[:, cols(half)])
                tt(c3(KE[:, :]), cum[:, :, CHUNK - 1:CHUNK].to_broadcast([P, 8, CHUNK]), cum,
                   ALU.subtract).then_inc(s_sub, 1)
            if s == 3:
                exponent(l, t, half, 5)
                dve.wait_ge(s_exp, (rnd * 2 + half) * 8 + 7)
                tt(KE[:, :], KE[:, :], KK[:, cols(half)], ALU.mult).then_inc(s_ket, 1)
                tt(QE[:, :], QE[:, :], QS[:, cols(half)], ALU.mult).then_inc(s_qe, 1)
            if s == 6 and half == 0:
                exponent(l, t, 1, 0)
            if s == 7 and half == 0:
                exponent(l, t, 1, 1)
                factor(l, t, 1, 0)
            if s == 0:
                written(l, b)
                tt(ST[:, :, :], bank3(0), mask(0), ALU.mult).then_inc(s_sr, 1)
            if s < 6:
                written(l, b + s + 1)
                dve.wait_ge(s_sr, use(l, b + s) + 1)
                dve.memset(SMALL[:, 31:32], 0.0)
                dve.copy_predicated(ST[:, :, :], mask(s + 1), bank3((s + 1) % 2)).then_inc(s_sr, 1)
            if s == 5:
                written(l, b + 7)
                copy(KE[:, :], SM[1][:, :]).then_inc(s_sr, 1)
            if s == 6:
                written(l, b + 8)
                if half == 0:
                    dve.wait_ge(s_el, rnd + 1)
                states(l, t, half, 1, 4)
            if s == 7:
                written(l, b + 9)
                states(l, t, half, 5, 8)
                written(l, b + 10)
                ts_(OF[:, ds(t, 1), cols(half)], SM[0][:, :].rearrange("p (o c) -> p o c", o=1),
                    1.0, None, ALU.mult).then_inc(s_sr, 1)

        def hg_variance(l, t, half):
            written(l, head_use(t) + HG_USES * half + 11)
            ts_(KE[:, :], SM[1][:, :], 1.0 / P, EPS, ALU.mult, ALU.add).then_inc(s_sr, 1)

        def hg_norm(l, t, half):
            rnd = (4 * l + t) * 2 + half
            st = Steps(dve, d_hgn, rnd, 3)
            dve.wait_ge(s_osd, 2 * rnd + 2)
            r3 = lambda x: x.rearrange("p (o c) -> p o c", o=1)
            ke = r3(KE[:, :])
            st(stt(ke, ke, PAR[:, PHG:PHG + 1], OF[:, ds(t, 1), cols(half)], ALU.mult, ALU.mult))
            st(tt(ke, ke, GATE[:, ds(t, 1), cols(half)], ALU.mult))
            st(ts_(GH[:, ds(t, 1), cols(half)], ke, 1.0, None, ALU.mult))
            ins = tt(GL[:, ds(t, 1), cols(half)], ke, GH[:, ds(t, 1), cols(half)].bitcast(F32), ALU.subtract)
            if half == 1:
                ins.then_inc(s_hgd, 1)
            st.end()

        def prepare(l, t, behind):
            rnd = 4 * l + t
            o = 4 * t + (O_HEAD + 2)
            st = Steps(dve, d_prep, rnd, 5)
            st(ts_(STAT[:, 14:15], PAR[:, ds(t + PLB, 1)], 1.0, None, ALU.mult))
            st(ts_(STAT[:, 15:16], PAR[:, ds(t + POML, 1)], 1.0, None, ALU.mult))
            st(dve.memset(STATE[:, 0, :], 0.0))
            dve.memset(SMALL[:, 31:32], 0.0).then_inc(s_state, 1)
            dve.wait_ge(s_fs, 2 * (rnd + 1))
            ts_(CUM[:, :], CUM[:, :], TINY, None, ALU.max).then_inc(s_clamp, 1)
            dve.wait_ge(s_taken[0], taken(l, o, 0, 1))
            st(ts_(KK[:, :], KK[:, :], STAT[:, 15:16], None, ALU.mult))
            b = token_major_use(t)
            for half in range(2):
                written(l, b + half)
                copy(IT[:, 4 * half:4 * half + 4, :],
                     SM[half][:, :].rearrange("p (n c) -> p n c", n=4)).then_inc(s_sr, 1)
            dve.wait_ge(s_ln, rnd + 1)
            for n in range(SEQ // CHUNK):
                c = CUM[:, n * CHUNK:(n + 1) * CHUNK]
                ins = dve.tensor_tensor_scan(c, ONES[:, 0:CHUNK], c, 0.0, ALU.mult, ALU.add)
            st(ins)
            dve.memset(SMALL[:, 31:32], 0.0).then_inc(s_cum, 1)
            exponent(l, t, 0, 0)
            exponent(l, t, 0, 1)
            factor(l, t, 0, 0)
            if behind:
                hg_norm(l, t - 1, 1)
            st.end()

        SINKT = SMALL[:, 24:26]

        def head_round(l, t, fresh, behind):
            if fresh:
                st = Steps(dve, d_sink, 4 * l + t, 1)
                st(ts_(SINKT, PAR[:, ds(t + PSINK, 2, step=PAIRS)], 1.0, None, ALU.mult))
            for u in range(16):
                if not behind and u == 1:
                    qk_variance(l, 4)
                if fresh:
                    if u % 2 == 0:
                        att = att_shift(l, t, u // 2)
                        if not behind and u > 0:
                            att_split(l, t, u // 2 - 1)
                    else:
                        att_probs(l, t, u // 2, att)
                if behind:
                    if u == 8:
                        hg_variance(l, t - 1, 0)
                    if u == 9:
                        hg_norm(l, t - 1, 0)
                    hg_step(l, t - 1, u)
                if behind and fresh and u % 2 == 1:
                    att_split(l, t, u // 2)
                if not behind and u == 1:
                    qk_rope(l, 3)
                if not behind and u == 4:
                    qk_newton(l, 4)
                if not behind and u == 5:
                    qk_norm(l, 4)
                if not behind and u == 9:
                    qk_rope(l, 4)
            if not behind:
                att_split(l, t, NB - 1)
            if behind:
                hg_variance(l, t - 1, 1)
            if fresh:
                prepare(l, t, behind)
            else:
                hg_norm(l, t - 1, 1)

        with dve.Fori(0, DEPTH) as l:
            st = Steps(dve, d_par, l, 1)
            st(ts_(PAR[:, :], PARA[:, ds(l, 1), :].rearrange("p o n -> p (o n)"), 1.0, None, ALU.mult))
            norm(l, 0, B_NORM1, PG1)
            dve.wait_ge(s_sp, 32 * l + 32)
            dve.memset(PR[:, :, 0:CHUNK], 0.0)
            dve.memset(KF[:, 0:P], 0.0)
            dve.memset(VT[:, 0, :], 0.0)
            for half in range(2):
                written(l, B_QK + half)
                ins = copy(VT[:, 1 + 4 * half:5 + 4 * half, :],
                           SM[half][:, :].rearrange("p (n c) -> p n c", n=4))
                ins.then_inc(s_sr, 1)
            dve.wait_ge(s_rl, 16 * l + 16)
            qk_variance(l, 0)
            qk_newton(l, 0)
            qk_norm(l, 0)
            for i in range(3):
                qk_variance(l, i + 1)
                qk_rope(l, i)
                qk_newton(l, i + 1)
                qk_norm(l, i + 1)
            head_round(l, 0, True, False)
            with dve.Fori(1, NH) as t:
                head_round(l, t, True, True)
            head_round(l, NH, False, True)

            def merge(j, w, o, o_gates, gates):
                for i in range(2):
                    dve.wait_ge(s_taken[i], taken(l, o_gates + i, i, 1))
                    for half in range(2):
                        dve.wait_ge(s_gemm, used(l, w, 4 * i + 2 * (half + 1)))
                        g = gates[i][:, 0, cols(half)]
                        tt(g, g, G[2 * i + half][:, :], ALU.mult).then_inc(s_taken[i], 1)
                dve.wait_ge(s_taken[0], taken(l, o, 0, 1))
                dve.wait_ge(s_taken[1], taken(l, o + 1, 1, 1))
                tt(MG[:, ds(j, 1), :], gates[0][:, :, :], gates[1][:, :, :], ALU.add).then_inc(s_mg, 1)

            def merged_low(n):
                j, half = MERGED[n]
                dve.wait_ge(s_mh, l * 2 * KT + n + 1)
                tt(HL[:, j, cols(half)], MG[:, j, cols(half)], HH[:, j, cols(half)].bitcast(F32),
                   ALU.subtract).then_inc(s_ml, 1)

            for j in range(2):
                merge(j, W_MERGE + 4 + j, O_MERGE + 4 + 2 * j, O_MERGE + 2 * j, GA[2 * j:2 * j + 2])
            gates = [SA[:, 0:1, :], SA[:, 1:2, :]]
            with dve.Fori(1, KT // 2 - 1) as jj:
                for h in range(2):
                    w, o = 6 * jj + (W_MERGE + 3 * h), 8 * jj + (O_MERGE + 4 * h)
                    merge(2 * jj + h, w + 2, o + 2, o, gates)
            for j in (KT - 2, KT - 1):
                if j == KT - 1:
                    for n in range(2 * KT - 2):
                        merged_low(n)
                w, o = W_MERGE + 3 * j, O_MERGE + 4 * j
                merge(j, w + 2, o + 2, o, gates)
            for n in (2 * KT - 2, 2 * KT - 1):
                merged_low(n)
            for half in range(2):
                dve.wait_ge(s_gemm, used(l, W_OUT, 4 * (half + 1)))
            dve.memset(NACC[:, :], 0.0).then_inc(s_acc, 1)
            for quad in range(2):
                with dve.Fori(2 * quad, 2 * quad + 2) as jj:
                    for h in range(2):
                        w, o = 2 * jj + (W_OUT + h), 2 * jj + (O_OUT + h)
                        dve.wait_ge(s_xb[quad], 16 * l + 16)
                        for half in range(2):
                            dve.wait_ge(s_gemm, used(l, w, 4 * (half + 1)))
                            x = XT[:, ds(2 * jj + h, 1), cols(half)]
                            tt(x, x, G[2 * h + half][:, :].rearrange("p (o c) -> p o c", o=1),
                               ALU.add).then_inc(s_taken[h], 1)
                        add_squares(2 * l + 1, 2 * jj + h, h)
            norm(l, 1, B_NORM2, PG2)
            st = Steps(dve, d_z, l, 1)
            st(dve.memset(CB[:, :, 0:2], 0.0))

            def up(g, w, o, buf, first=False):
                n = (l * HIDDEN_GROUPS + g) * 2
                st = Steps(dve, d_ffn, l * HIDDEN_GROUPS + g, 4)
                for i in range(2):
                    tap = lambda j: PAR[:, ds(2 * g + (PCW + j * FT + i), 1)]
                    dve.wait_ge(s_taken[0], taken(l, o + 2 * i, 0, 1))
                    co, cb = CO[:, i, :], CB[:, i, :]
                    st(ts_(co, cb[:, 0:SEQ], tap(0), tap(3), ALU.mult, ALU.add))
                    st(stt(co, cb[:, 1:SEQ + 1], tap(1), co, ALU.mult, ALU.add))
                    stt(co, cb[:, 2:SEQ + 2], tap(2), co, ALU.mult, ALU.add).then_inc(s_co, 1)
                    dve.wait_ge(s_si, n + i + 1)
                    for half in range(2):
                        n_gemm = PAIRED[1][half] if first and i == 0 else 4 * (half + 1)
                        dve.wait_ge(s_gemm, used(l, w + 2 * i + 1, n_gemm))
                        tt(UF[:, i, cols(half)], co[:, cols(half)], G[2 + half][:, :],
                           ALU.mult).then_inc(s_taken[1], 1)
                    dve.wait_ge(s_uhi, n + i + 1)
                    tt(UL[:, buf, i, :], UF[:, i, :], UH[:, buf, i, :].bitcast(F32),
                       ALU.subtract).then_inc(s_ulo, 1)
                st.end()

            def down(w, o, done=False):
                if done:
                    dve.memset(NACC[:, :], 0.0).then_inc(s_acc, 1)
                for j in range(KT):
                    par = j % 2
                    for half in range(2):
                        dve.wait_ge(s_gemm, used(l, w + j // 4, 2 * (j % 4) + half + 1))
                        x = XT[:, j, cols(half)]
                        tt(x, x, G[2 * par + half][:, :], ALU.add).then_inc(s_taken[par], 1)
                    if done:
                        dve.wait_ge(s_taken[par], taken(l, o + j, par, 1))
                        dve.memset(SMALL[:, 31:32], 0.0).then_inc(s_x, 1)
                        if j > 0:
                            add_squares(2 * l + 2, j - 1, (j - 1) % 2)
                if done:
                    add_squares(2 * l + 2, KT - 1, 1)

            up(0, W_FFN, O_FFN, 0, True)
            with dve.Fori(0, HIDDEN_GROUPS // 2) as p:
                w, o = 12 * p + (W_FFN + 4), 24 * p + (O_FFN + 4)
                up(2 * p + 1, w, o, 1)
                down(w + 4, o + 4)
                up(2 * p + 2, w + 6, o + 12, 0)
                down(w + 10, o + 16)
            down(W_LAYER - 2, O_LAYER - 8, True)
        for b in range(2 * NB):
            written(DEPTH, b)
            copy(OUTB[:, b // 2, cols(b % 2)], SM[b % 2][:, :]).then_inc(s_sr, 1)

    block.__exit__(None, None, None)



_INS = ["x", "positions", "norm1_g", "w_in", "q_norm_g", "k_norm_g", "sinks", "lb_logits", "hg_norm_g",
        "w_branch_a", "w_branch_b", "w_out", "norm2_g", "w_up", "conv_w", "conv_b", "w_down"]


def kernel(**inputs):
    import concourse.bacc as _bacc
    from concourse.bass_utils import run_bass_kernel_spmd as _run

    nc = _bacc.Bacc("TRN2", target_bir_lowering=False, num_devices=1)
    arrays, args = {}, {}
    for name in _INS + ["consts"]:
        a = constants() if name == "consts" else np.ascontiguousarray(inputs[name])
        arrays[f"in_{name}"] = a
        args[name] = nc.dram_tensor(f"in_{name}", a.shape, mybir.dt.from_np(a.dtype), kind="ExternalInput").ap()
    out = nc.dram_tensor("out_x", (1, SEQ, D), F32, kind="ExternalOutput").ap()
    build(nc, args, out)
    r = _run(nc, [arrays], core_ids=[0])
    return r.results[0]["out_x"]
```
